# Optimizing a Trainium2 kernel written in Bass

```python
import math
import jax, jax.numpy as jnp
from jax import lax
import numpy as np
import jax
import jax.numpy as jnp

D_MODEL = 1024
BATCH = 1
SEQ = 256
DEPTH = 1

N_META = 16
GDN_HEADS = 8
GDN_DK = 128
GDN_DV = 128
CONV_WIDTH = 4
CHUNK = 64
ATT_HEADS = 8
ATT_KV_HEADS = 2
ATT_HD = 128
ATT_GROUP = ATT_HEADS // ATT_KV_HEADS
IDX_HEADS = 8
IDX_HD = 64
TOPK_MAX = 256
Q_BLOCK = 128
ROPE_THETA = 10000.0
D_FF = 4 * D_MODEL
EPS = 1e-6

GDN_QK_W = GDN_HEADS * GDN_DK
GDN_V_W = GDN_HEADS * GDN_DV
ATT_Q_W = ATT_HEADS * ATT_HD
ATT_KV_W = ATT_KV_HEADS * ATT_HD
SPLITS = (GDN_QK_W, GDN_QK_W, GDN_V_W, GDN_V_W, GDN_HEADS, GDN_HEADS,
          ATT_Q_W, ATT_KV_W, ATT_KV_W, IDX_HEADS * IDX_HD, IDX_HD, IDX_HEADS,
          D_MODEL, D_MODEL)
N_IN = sum(SPLITS)


def _rmsnorm(x, g):
    xf = x.astype(jnp.float32)
    y = xf * lax.rsqrt(jnp.mean(xf * xf, axis=-1, keepdims=True) + EPS)
    return (y * g.astype(jnp.float32)).astype(x.dtype)

def _l2norm(x):
    return x * lax.rsqrt(jnp.sum(x * x, axis=-1, keepdims=True) + EPS)

def _rope_tables(pos, dim):
    inv = ROPE_THETA ** (-jnp.arange(0, dim, 2, dtype=jnp.float32) / dim)
    ang = pos.astype(jnp.float32)[:, None] * inv[None, :]
    return jnp.cos(ang), jnp.sin(ang)

def _apply_rope(x, cos, sin):
    half = x.shape[-1] // 2
    xf = x.astype(jnp.float32)
    x1, x2 = xf[..., :half], xf[..., half:]
    c = cos[None, :, None, :]
    s = sin[None, :, None, :]
    return jnp.concatenate([x1 * c - x2 * s, x2 * c + x1 * s], axis=-1).astype(x.dtype)

def _causal_conv(x, w):
    K = w.shape[0]
    T = x.shape[1]
    xp = jnp.pad(x, ((0, 0), (K - 1, 0), (0, 0)))
    y = xp[:, 0:T] * w[0]
    for j in range(1, K):
        y = y + xp[:, j:j + T] * w[j]
    return y

def _gated_delta_rule(q, k, v, beta, g):
    B_, T_, H, dk = q.shape
    dv = v.shape[-1]
    C = CHUNK
    pad = (-N_META) % C
    tail = (-(T_ + pad)) % C

    def padf(a):
        return jnp.pad(a, [(0, 0), (pad, tail)] + [(0, 0)] * (a.ndim - 2))

    q, k, v, beta, g = padf(q), padf(k), padf(v), padf(beta), padf(g)
    N = (T_ + pad + tail) // C

    def vec_chunks(a):
        return a.reshape(B_, N, C, H, a.shape[-1]).transpose(0, 3, 1, 2, 4)

    def sc_chunks(a):
        return a.reshape(B_, N, C, H).transpose(0, 3, 1, 2)

    q, k, v = vec_chunks(q), vec_chunks(k), vec_chunks(v)
    beta, g = sc_chunks(beta), sc_chunks(g)
    gc = jnp.cumsum(g, axis=-1)

    tri_incl = jnp.tril(jnp.ones((C, C), dtype=bool))
    tri_strict = jnp.tril(jnp.ones((C, C), dtype=bool), -1)
    decay = jnp.exp(jnp.where(tri_incl, gc[..., :, None] - gc[..., None, :], -jnp.inf))

    kb = k * beta[..., None]
    A = jnp.where(tri_strict, jnp.einsum('bhncd,bhnsd->bhncs', kb, k) * decay, 0.0)
    eye = jnp.eye(C, dtype=jnp.float32)
    Tm = lax.linalg.triangular_solve(A + eye, jnp.broadcast_to(eye, A.shape),
                                     left_side=True, lower=True, unit_diagonal=True)
    u = jnp.einsum('bhncs,bhnse->bhnce', Tm, v * beta[..., None])
    w = jnp.einsum('bhncs,bhnsd->bhncd', Tm, kb * jnp.exp(gc)[..., None])
    attn = jnp.einsum('bhncd,bhnsd->bhncs', q, k) * decay
    q_dec = q * jnp.exp(gc)[..., None]
    k_tail = k * jnp.exp(gc[..., -1:] - gc)[..., None]
    g_last = jnp.exp(gc[..., -1])

    def to_scan(a):
        return jnp.moveaxis(a, 2, 0)

    xs = (to_scan(q_dec), to_scan(attn), to_scan(u), to_scan(w), to_scan(k_tail), to_scan(g_last))

    def step(S, inp):
        qe, at, u_i, w_i, kt, gl = inp
        v_new = u_i - jnp.einsum('bhcd,bhde->bhce', w_i, S)
        o = jnp.einsum('bhcd,bhde->bhce', qe, S) + jnp.einsum('bhcs,bhse->bhce', at, v_new)
        S = S * gl[..., None, None] + jnp.einsum('bhcd,bhce->bhde', kt, v_new)
        return S, o

    S0 = jnp.zeros((B_, H, dk, dv), jnp.float32)
    _, o = lax.scan(step, S0, xs)
    o = o.transpose(1, 0, 3, 2, 4).reshape(B_, N * C, H, dv)
    return o[:, pad:pad + T_]

def _gdn_branch(q, k, v, z, b_raw, a_raw, conv_w, a_log, dt_bias, norm_w):
    B_, T_, _ = q.shape
    dt = q.dtype
    qkv = jax.nn.silu(_causal_conv(jnp.concatenate([q, k, v], axis=-1), conv_w))
    q, k, v = jnp.split(qkv, [GDN_QK_W, 2 * GDN_QK_W], axis=-1)
    q = q.reshape(B_, T_, GDN_HEADS, GDN_DK).astype(jnp.float32)
    k = k.reshape(B_, T_, GDN_HEADS, GDN_DK).astype(jnp.float32)
    v = v.reshape(B_, T_, GDN_HEADS, GDN_DV).astype(jnp.float32)
    q = _l2norm(q) * (GDN_DK ** -0.5)
    k = _l2norm(k)
    beta = jax.nn.sigmoid(b_raw.astype(jnp.float32))
    g = -jnp.exp(a_log.astype(jnp.float32)) * jax.nn.softplus(a_raw.astype(jnp.float32) + dt_bias.astype(jnp.float32))
    o = _gated_delta_rule(q, k, v, beta, g)
    zf = z.reshape(B_, T_, GDN_HEADS, GDN_DV).astype(jnp.float32)
    o = _rmsnorm(o, norm_w) * jax.nn.silu(zf)
    return o.reshape(B_, T_, GDN_V_W).astype(dt)

def _dsa_branch(q, k, v, qi, ki, wi, rope_att, rope_idx, n_visible):
    B_, T_, _ = q.shape
    cos_a, sin_a = rope_att
    cos_i, sin_i = rope_idx
    q = _apply_rope(q.reshape(B_, T_, ATT_HEADS, ATT_HD), cos_a, sin_a)
    k = _apply_rope(k.reshape(B_, T_, ATT_KV_HEADS, ATT_HD), cos_a, sin_a)
    v = v.reshape(B_, T_, ATT_KV_HEADS, ATT_HD)
    qi = _apply_rope(qi.reshape(B_, T_, IDX_HEADS, IDX_HD), cos_i, sin_i)
    ki = _apply_rope(ki.reshape(B_, T_, 1, IDX_HD), cos_i, sin_i)[:, :, 0]
    wi = wi * ((IDX_HEADS * IDX_HD) ** -0.5)
    kv = jnp.concatenate([k, v], axis=-1)
    topk = min(TOPK_MAX, n_visible // 4)
    nb = -(-T_ // Q_BLOCK)
    Tq = nb * Q_BLOCK

    def to_blocks(a):
        a = jnp.pad(a, [(0, 0), (0, Tq - T_)] + [(0, 0)] * (a.ndim - 2))
        return jnp.moveaxis(a.reshape((B_, nb, Q_BLOCK) + a.shape[2:]), 1, 0)

    key_pos = jnp.arange(T_, dtype=jnp.int32)

    def block(args):
        qb, qib, wib, posb = args
        s = jnp.einsum('bqhd,bsd->bqhs', qib, ki)
        s = jnp.einsum('bqhs,bqh->bqs', jax.nn.relu(s), wib).astype(jnp.float32)
        s = jnp.where(key_pos[None, None, :] <= posb[None, :, None], s, -jnp.inf)
        _, idx = lax.top_k(s, topk)
        kv_sel = jax.vmap(lambda a, i: a[i])(kv, idx)
        k_sel, v_sel = jnp.split(kv_sel, 2, axis=-1)
        qg = qb.reshape(B_, Q_BLOCK, ATT_KV_HEADS, ATT_GROUP, ATT_HD)
        logits = jnp.einsum('bqgrd,bqkgd->bqgrk', qg, k_sel).astype(jnp.float32) * (ATT_HD ** -0.5)
        valid = (idx <= posb[None, :, None])[:, :, None, None, :]
        p = jax.nn.softmax(jnp.where(valid, logits, -jnp.inf), axis=-1).astype(v.dtype)
        o = jnp.einsum('bqgrk,bqkgd->bqgrd', p, v_sel)
        return o.reshape(B_, Q_BLOCK, ATT_Q_W)

    pos_blocks = jnp.arange(Tq, dtype=jnp.int32).reshape(nb, Q_BLOCK)
    out = lax.map(block, (to_blocks(q), to_blocks(qi), to_blocks(wi), pos_blocks))
    return jnp.moveaxis(out, 0, 1).reshape(B_, Tq, ATT_Q_W)[:, :T_]

def first_inputs(seed: int = 0) -> dict:
    key = jax.random.key(seed)
    ks = jax.random.split(key, 20)
    f32 = jnp.float32

    def nrm(k, shape, scale):
        return jax.random.normal(k, shape, f32) * scale

    def gain(k, shape):
        return 1.0 + 0.02 * jax.random.normal(k, shape, f32)

    dt = jnp.exp(jax.random.uniform(ks[5], (DEPTH, GDN_HEADS), f32, math.log(1e-3), math.log(1e-1)))
    return {
        "x": jax.random.normal(ks[0], (BATCH, SEQ, D_MODEL), f32),
        "meta_tokens": nrm(ks[1], (N_META, D_MODEL), 1.0),
        "pre_mix_norm": gain(ks[2], (DEPTH, D_MODEL)),
        "w_in": nrm(ks[3], (DEPTH, D_MODEL, N_IN), D_MODEL ** -0.5),
        "conv_w": nrm(ks[4], (DEPTH, CONV_WIDTH, 2 * GDN_QK_W + GDN_V_W), CONV_WIDTH ** -0.5),
        "a_log": jnp.log(jax.random.uniform(ks[6], (DEPTH, GDN_HEADS), f32, 1.0, 16.0)),
        "dt_bias": jnp.log(jnp.expm1(dt)),
        "gdn_norm": gain(ks[7], (DEPTH, GDN_DV)),
        "w_branch_gdn": nrm(ks[8], (DEPTH, GDN_V_W, D_MODEL), GDN_V_W ** -0.5),
        "w_branch_dsa": nrm(ks[9], (DEPTH, ATT_Q_W, D_MODEL), ATT_Q_W ** -0.5),
        "w_out": nrm(ks[10], (DEPTH, D_MODEL, D_MODEL), D_MODEL ** -0.5),
        "post_mix_norm": gain(ks[11], (DEPTH, D_MODEL)),
        "pre_mlp_norm": gain(ks[12], (DEPTH, D_MODEL)),
        "w_up": nrm(ks[13], (DEPTH, D_MODEL, D_FF), D_MODEL ** -0.5),
        "w_down": nrm(ks[14], (DEPTH, D_FF, D_MODEL), D_FF ** -0.5),
        "post_mlp_norm": gain(ks[15], (DEPTH, D_MODEL)),
    }

def first_block(x, meta_tokens, pre_mix_norm, w_in, conv_w, a_log, dt_bias, gdn_norm,
              w_branch_gdn, w_branch_dsa, w_out, post_mix_norm, pre_mlp_norm, w_up, w_down,
              post_mlp_norm):
    B_, L, _ = x.shape
    meta = jnp.broadcast_to(meta_tokens.astype(x.dtype)[None], (B_, N_META, D_MODEL))
    h = jnp.concatenate([meta, x], axis=1)
    T_ = h.shape[1]
    pos = jnp.arange(T_, dtype=jnp.int32)
    rope_att = _rope_tables(pos, ATT_HD)
    rope_idx = _rope_tables(pos, IDX_HD)
    split_at = [int(i) for i in np.cumsum(SPLITS)[:-1]]

    for l in range(DEPTH):
        n = _rmsnorm(h, pre_mix_norm[l])
        proj = jnp.einsum('btd,dn->btn', n, w_in[l])
        (gq, gk, gv, gz, gb, ga, aq, ak, av, iq, ik, iw, gate_a, gate_b) = jnp.split(proj, split_at, axis=-1)
        y_gdn = _gdn_branch(gq, gk, gv, gz, gb, ga, conv_w[l], a_log[l], dt_bias[l], gdn_norm[l])
        y_dsa = _dsa_branch(aq, ak, av, iq, ik, iw, rope_att, rope_idx, L)
        merged = (jax.nn.sigmoid(gate_a) * jnp.einsum('btv,vd->btd', y_gdn, w_branch_gdn[l])
                  + jax.nn.sigmoid(gate_b) * jnp.einsum('btv,vd->btd', y_dsa, w_branch_dsa[l]))
        mix = jnp.einsum('btd,de->bte', merged, w_out[l])
        h = h + _rmsnorm(mix, post_mix_norm[l])
        n2 = _rmsnorm(h, pre_mlp_norm[l])
        u = jnp.square(jax.nn.relu(jnp.einsum('btd,df->btf', n2, w_up[l])))
        h = h + _rmsnorm(jnp.einsum('btf,fd->btd', u, w_down[l]), post_mlp_norm[l])

    return h[:, N_META:]


DEPTH_2 = 2

HEAD_DIM = 64
MIX_HEADS = 12
MIX_WIDTH = MIX_HEADS * HEAD_DIM
MEM_HEADS = 4
MEM_WIDTH = MEM_HEADS * HEAD_DIM
MEM_LEN = 256
CONV_WIDTH_2 = 3
ROPE_DIM = HEAD_DIM // 4
ROPE_THETA_2 = 500000.0
MOBA_BLOCK = 256
MOBA_TOPK = 3
MOBA_Q_CHUNK = 16
D_FF_2 = 2816
N_EXPERTS = 8
TOP_K = 2
LN_EPS = 1e-5
N_A_LAYERS = DEPTH_2 // 2
N_B_LAYERS = DEPTH_2 - N_A_LAYERS
N_DENSE = (DEPTH_2 + 1) // 2
N_MOE = DEPTH_2 // 2
DEEPNORM_ALPHA = float((2 * DEPTH_2) ** 0.25)
DEEPNORM_BETA = float((8 * DEPTH_2) ** -0.25)
ATTN_SCALE = HEAD_DIM ** -0.5


def layer_norm(x, g, b):
    xf = x.astype(jnp.float32)
    mu = jnp.mean(xf, axis=-1, keepdims=True)
    var = jnp.mean(jnp.square(xf - mu), axis=-1, keepdims=True)
    y = (xf - mu) * lax.rsqrt(var + LN_EPS)
    return (y * g + b).astype(x.dtype)

def rope_tables(positions):
    inv_freq = ROPE_THETA_2 ** (-jnp.arange(0, ROPE_DIM, 2, dtype=jnp.float32) / ROPE_DIM)
    angles = positions.astype(jnp.float32)[..., None] * inv_freq
    return jnp.cos(angles)[:, :, None, :], jnp.sin(angles)[:, :, None, :]

def apply_partial_rope(t, cos, sin):
    half = ROPE_DIM // 2
    t1 = t[..., :half].astype(jnp.float32)
    t2 = t[..., half:ROPE_DIM].astype(jnp.float32)
    rot = jnp.concatenate([t1 * cos - t2 * sin, t2 * cos + t1 * sin], axis=-1).astype(t.dtype)
    return jnp.concatenate([rot, t[..., ROPE_DIM:]], axis=-1)

def short_conv_mixer(u_b, u_c, u_h, conv_w):
    z = u_c * u_h
    z = lax.conv_general_dilated(
        z, conv_w[:, None, :], window_strides=(1,), padding=[(CONV_WIDTH_2 - 1, 0)],
        dimension_numbers=('NWC', 'WIO', 'NWC'), feature_group_count=MIX_WIDTH)
    return u_b * z

def memory_cross_attention(q, k, v):
    logits = jnp.einsum('bshd,bmhd->bhsm', q, k).astype(jnp.float32) * ATTN_SCALE
    probs = jax.nn.softmax(logits, axis=-1).astype(v.dtype)
    out = jnp.einsum('bhsm,bmhd->bshd', probs, v)
    return out.reshape(q.shape[0], q.shape[1], -1)

def shared_key_value(h, w_kv, cos, sin):
    bsz, seq, _ = h.shape
    kv = jnp.einsum('bsd,de->bse', h, w_kv)
    k = apply_partial_rope(kv[..., :MIX_WIDTH].reshape(bsz, seq, MIX_HEADS, HEAD_DIM), cos, sin)
    v = kv[..., MIX_WIDTH:].reshape(bsz, seq, MIX_HEADS, HEAD_DIM)
    pad = (-seq) % MOBA_BLOCK
    k = jnp.pad(k, ((0, 0), (0, pad), (0, 0), (0, 0)))
    v = jnp.pad(v, ((0, 0), (0, pad), (0, 0), (0, 0)))
    n_blocks = (seq + pad) // MOBA_BLOCK
    k_blocks = k.reshape(bsz, n_blocks, MOBA_BLOCK, MIX_HEADS, HEAD_DIM).transpose(0, 3, 1, 2, 4)
    v_blocks = v.reshape(bsz, n_blocks, MOBA_BLOCK, MIX_HEADS, HEAD_DIM).transpose(0, 3, 1, 2, 4)
    k_means = jnp.mean(k_blocks.astype(jnp.float32), axis=3).astype(k.dtype)
    return k_blocks, v_blocks, k_means

def moba_attention(q, k_blocks, v_blocks, k_means):
    bsz, seq, n_heads, head_dim = q.shape
    n_blocks = k_blocks.shape[2]
    topk = min(MOBA_TOPK, n_blocks)
    n_sel = topk * MOBA_BLOCK
    n_chunks = seq // MOBA_Q_CHUNK
    q_chunks = q.reshape(bsz, n_chunks, MOBA_Q_CHUNK, n_heads, head_dim).transpose(1, 0, 3, 2, 4)
    b_idx = jnp.arange(bsz)[:, None, None, None]
    h_idx = jnp.arange(n_heads)[None, :, None, None]
    block_ids = jnp.arange(n_blocks)

    def one_chunk(args):
        c, qc = args
        start = c * MOBA_Q_CHUNK
        own = start // MOBA_BLOCK
        q_pos = start + jnp.arange(MOBA_Q_CHUNK)
        gate = jnp.einsum('bhqd,bhnd->bhqn', qc, k_means).astype(jnp.float32)
        gate = jnp.where(block_ids < own, gate, -jnp.inf)
        _, sel = lax.top_k(gate, topk)
        sel_valid = sel < own
        k_sel = k_blocks[b_idx, h_idx, sel]
        v_sel = v_blocks[b_idx, h_idx, sel]
        k_own = lax.dynamic_index_in_dim(k_blocks, own, axis=2, keepdims=False)
        v_own = lax.dynamic_index_in_dim(v_blocks, own, axis=2, keepdims=False)
        s_sel = jnp.einsum('bhqd,bhqkjd->bhqkj', qc, k_sel).astype(jnp.float32) * ATTN_SCALE
        s_sel = jnp.where(sel_valid[..., None], s_sel, -jnp.inf)
        s_own = jnp.einsum('bhqd,bhjd->bhqj', qc, k_own).astype(jnp.float32) * ATTN_SCALE
        k_pos = own * MOBA_BLOCK + jnp.arange(MOBA_BLOCK)
        s_own = jnp.where(k_pos[None, :] <= q_pos[:, None], s_own, -jnp.inf)
        scores = jnp.concatenate([s_sel.reshape(bsz, n_heads, MOBA_Q_CHUNK, n_sel), s_own], axis=-1)
        probs = jax.nn.softmax(scores, axis=-1).astype(qc.dtype)
        p_sel = probs[..., :n_sel].reshape(bsz, n_heads, MOBA_Q_CHUNK, topk, MOBA_BLOCK)
        p_own = probs[..., n_sel:]
        return (jnp.einsum('bhqkj,bhqkjd->bhqd', p_sel, v_sel)
                + jnp.einsum('bhqj,bhjd->bhqd', p_own, v_own))

    out = lax.map(one_chunk, (jnp.arange(n_chunks), q_chunks))
    return out.transpose(1, 0, 3, 2, 4).reshape(bsz, seq, n_heads * head_dim)

def swiglu(x, w_gu, w_down):
    gu = jnp.einsum('bsd,df->bsf', x, w_gu)
    g, u = gu[..., :D_FF_2], gu[..., D_FF_2:]
    return jnp.einsum('bsf,fd->bsd', jax.nn.silu(g) * u, w_down)

def moe_swiglu(x, w_router, w_gu, w_down):
    logits = jnp.einsum('bsd,de->bse', x, w_router).astype(jnp.float32)
    top_logits, top_idx = lax.top_k(logits, TOP_K)
    top_gates = jax.nn.softmax(top_logits, axis=-1)
    gates = jnp.sum(jax.nn.one_hot(top_idx, N_EXPERTS, dtype=jnp.float32) * top_gates[..., None], axis=-2)
    gates = gates.astype(x.dtype)
    out = jnp.zeros_like(x)
    for e in range(N_EXPERTS):
        out = out + gates[..., e:e + 1] * swiglu(x, w_gu[e], w_down[e])
    return out

def second_inputs(seed: int = 0) -> dict:
    key = jax.random.key(seed)
    ks = jax.random.split(key, 20)
    f32 = jnp.float32

    def nrm(k, shape, scale):
        return jax.random.normal(k, shape, f32) * scale

    x = nrm(ks[0], (BATCH, SEQ, D_MODEL), 1.0)
    mem = nrm(ks[1], (BATCH, MEM_LEN, D_MODEL), 1.0)
    offset = jax.random.randint(ks[2], (BATCH, 1), 0, 1024, dtype=jnp.int32)
    positions = offset + jnp.arange(SEQ, dtype=jnp.int32)[None, :]
    w_in_a = nrm(ks[3], (N_A_LAYERS, D_MODEL, 3 * MIX_WIDTH + MEM_WIDTH), D_MODEL ** -0.5)
    conv_a = nrm(ks[4], (N_A_LAYERS, CONV_WIDTH_2, MIX_WIDTH), CONV_WIDTH_2 ** -0.5)
    w_q_b = nrm(ks[5], (N_B_LAYERS, D_MODEL, MIX_WIDTH + MEM_WIDTH), D_MODEL ** -0.5)
    w_kv_shared = nrm(ks[6], (D_MODEL, 2 * MIX_WIDTH), D_MODEL ** -0.5)
    w_mem_kv = nrm(ks[7], (DEPTH_2, D_MODEL, 2 * MEM_WIDTH), D_MODEL ** -0.5)
    w_o = nrm(ks[8], (DEPTH_2, MIX_WIDTH + MEM_WIDTH, D_MODEL), (MIX_WIDTH + MEM_WIDTH) ** -0.5 * DEEPNORM_BETA)
    ln1_g = 1.0 + nrm(ks[9], (DEPTH_2, D_MODEL), 0.02)
    ln1_b = nrm(ks[10], (DEPTH_2, D_MODEL), 0.02)
    ln2_g = 1.0 + nrm(ks[11], (DEPTH_2, D_MODEL), 0.02)
    ln2_b = nrm(ks[12], (DEPTH_2, D_MODEL), 0.02)
    w_gu_dense = nrm(ks[13], (N_DENSE, D_MODEL, 2 * D_FF_2), D_MODEL ** -0.5)
    w_down_dense = nrm(ks[14], (N_DENSE, D_FF_2, D_MODEL), D_FF_2 ** -0.5 * DEEPNORM_BETA)
    w_router = nrm(ks[15], (N_MOE, D_MODEL, N_EXPERTS), D_MODEL ** -0.5)
    w_gu_moe = nrm(ks[16], (N_MOE, N_EXPERTS, D_MODEL, 2 * D_FF_2), D_MODEL ** -0.5)
    w_down_moe = nrm(ks[17], (N_MOE, N_EXPERTS, D_FF_2, D_MODEL), D_FF_2 ** -0.5 * DEEPNORM_BETA)
    return {'x': x, 'mem': mem, 'positions': positions, 'w_in_a': w_in_a, 'conv_a': conv_a,
            'w_q_b': w_q_b, 'w_kv_shared': w_kv_shared, 'w_mem_kv': w_mem_kv, 'w_o': w_o,
            'ln1_g': ln1_g, 'ln1_b': ln1_b, 'ln2_g': ln2_g, 'ln2_b': ln2_b,
            'w_gu_dense': w_gu_dense, 'w_down_dense': w_down_dense, 'w_router': w_router,
            'w_gu_moe': w_gu_moe, 'w_down_moe': w_down_moe}

def second_block(x, mem, positions, w_in_a, conv_a, w_q_b, w_kv_shared, w_mem_kv, w_o,
              ln1_g, ln1_b, ln2_g, ln2_b, w_gu_dense, w_down_dense, w_router,
              w_gu_moe, w_down_moe):
    bsz, seq, _ = x.shape
    cos, sin = rope_tables(positions)
    shared = None
    for layer in range(DEPTH_2):
        mem_kv = jnp.einsum('bmd,de->bme', mem, w_mem_kv[layer])
        mem_k = mem_kv[..., :MEM_WIDTH].reshape(bsz, -1, MEM_HEADS, HEAD_DIM)
        mem_v = mem_kv[..., MEM_WIDTH:].reshape(bsz, -1, MEM_HEADS, HEAD_DIM)
        if layer < N_A_LAYERS:
            proj = jnp.einsum('bsd,de->bse', x, w_in_a[layer])
            u_b = proj[..., :MIX_WIDTH]
            u_c = proj[..., MIX_WIDTH:2 * MIX_WIDTH]
            u_h = proj[..., 2 * MIX_WIDTH:3 * MIX_WIDTH]
            q_mem = proj[..., 3 * MIX_WIDTH:]
            main = short_conv_mixer(u_b, u_c, u_h, conv_a[layer])
        else:
            proj = jnp.einsum('bsd,de->bse', x, w_q_b[layer - N_A_LAYERS])
            q = apply_partial_rope(proj[..., :MIX_WIDTH].reshape(bsz, seq, MIX_HEADS, HEAD_DIM), cos, sin)
            q_mem = proj[..., MIX_WIDTH:]
            k_blocks, v_blocks, k_means = shared
            main = moba_attention(q, k_blocks, v_blocks, k_means)
        mem_out = memory_cross_attention(q_mem.reshape(bsz, seq, MEM_HEADS, HEAD_DIM), mem_k, mem_v)
        mix = jnp.einsum('bse,ed->bsd', jnp.concatenate([main, mem_out], axis=-1), w_o[layer])
        x = layer_norm(DEEPNORM_ALPHA * x + mix, ln1_g[layer], ln1_b[layer])
        if layer % 2 == 0:
            ffn = swiglu(x, w_gu_dense[layer // 2], w_down_dense[layer // 2])
        else:
            ffn = moe_swiglu(x, w_router[layer // 2], w_gu_moe[layer // 2], w_down_moe[layer // 2])
        x = layer_norm(DEEPNORM_ALPHA * x + ffn, ln2_g[layer], ln2_b[layer])
        if layer == N_A_LAYERS - 1:
            shared = shared_key_value(x, w_kv_shared, cos, sin)
    return x


def setup_inputs(seed=0):
    out = dict(first_inputs(seed))
    for name, value in second_inputs(seed + 1).items():
        if name != "x":
            out[name + "_2"] = value
    return out


def reference(
    x, meta_tokens, pre_mix_norm, w_in, conv_w, a_log, dt_bias, gdn_norm, w_branch_gdn,
    w_branch_dsa, w_out, post_mix_norm, pre_mlp_norm, w_up, w_down, post_mlp_norm, mem_2,
    positions_2, w_in_a_2, conv_a_2, w_q_b_2, w_kv_shared_2, w_mem_kv_2, w_o_2, ln1_g_2,
    ln1_b_2, ln2_g_2, ln2_b_2, w_gu_dense_2, w_down_dense_2, w_router_2, w_gu_moe_2,
    w_down_moe_2,
):
    x = first_block(
        x, meta_tokens, pre_mix_norm, w_in, conv_w, a_log, dt_bias, gdn_norm, w_branch_gdn,
        w_branch_dsa, w_out, post_mix_norm, pre_mlp_norm, w_up, w_down, post_mlp_norm,
    )
    return second_block(
        x, mem_2, positions_2, w_in_a_2, conv_a_2, w_q_b_2, w_kv_shared_2, w_mem_kv_2, w_o_2,
        ln1_g_2, ln1_b_2, ln2_g_2, ln2_b_2, w_gu_dense_2, w_down_dense_2, w_router_2,
        w_gu_moe_2, w_down_moe_2,
    )


_drawn_inputs = setup_inputs


def setup_inputs(seed=0):
    import zlib

    import numpy as np

    out = dict(_drawn_inputs(seed))
    spreads = {}
    factors = {'post_mlp_norm': 2.806}
    for name, (base, spread) in spreads.items():
        noise = np.random.default_rng([zlib.crc32(name.encode()), seed]).standard_normal(out[name].shape)
        drawn = base * np.exp(spread * noise) if base else spread * noise
        out[name] = jnp.asarray(drawn.astype(out[name].dtype))
    for name, factor in factors.items():
        out[name] = (out[name] * factor).astype(out[name].dtype)
    return out
```

```python
from contextlib import ExitStack

import numpy as np

import concourse.bass as bass
from concourse import mybir

F32 = mybir.dt.float32
I32 = mybir.dt.int32
U32 = mybir.dt.uint32
ALU = mybir.AluOpType
ACT = mybir.ActivationFunctionType
AX = mybir.AxisListType.X

P = 128
NM = 16
SEQ = 256
T = NM + SEQ
NSLOT = 4
NEG = -1e30
TAKEN = -3e38

C_IN = dict(gq=0, gk=1024, gv=2048, gz=3072, gb=4096, ga=4104, aq=4112, ak=5136, av=5392,
            iq=5648, ik=6160, iw=6224, gate_a=6232, gate_b=7256)


def shape_constants():
    i = np.arange(P)
    s, c = i[:, None], i[None, :]
    f = np.float32
    out = {}
    out["ident"] = (s == c).astype(f)
    out["ones"] = np.ones((P, P), f)
    out["U"] = (s <= c).astype(f)
    out["Us"] = (s < c).astype(f)
    same = s // 16 == c // 16
    out["Ub"] = (same & (s <= c)).astype(f)
    out["Ubs"] = (same & (s < c)).astype(f)
    out["OB"] = same.astype(f)
    for b in (1, 2, 4, 8, 16, 32, 64):
        out[f"m{b}"] = ((s // (2 * b) == c // (2 * b)) & (c % (2 * b) >= b) & (s % (2 * b) < b)).astype(f)
    for name, hd, half in (("R128", 128, 64), ("R64", 64, 32), ("R16", 64, 8)):
        r = np.zeros((P, P), f)
        for m in range(P):
            if m % hd < half:
                r[m + half, m] = -1
            elif m % hd < 2 * half:
                r[m - half, m] = 1
        out[name] = r
    out["hmask"] = (s // 16 == np.arange(8)[None, :]).astype(f)
    out["Rep"] = ((s == c % 16) & (s < 16)).astype(f)
    out["CB"] = np.concatenate([np.zeros((P, P), f), np.where(c <= s, 0, NEG).astype(f)], 1)
    pos = np.arange(T, dtype=f)
    for name, dim in (("A", 128), ("I", 64)):
        inv = f(10000.0) ** (-np.arange(0, dim, 2, dtype=f) / f(dim))
        ang = pos[None, :] * inv.astype(f)[i % (dim // 2)][:, None]
        out["cos" + name] = np.cos(ang).astype(f)
        out["sin" + name] = np.sin(ang).astype(f)
    inv2 = f(500000.0) ** (-np.arange(0, 16, 2, dtype=f) / f(16))
    out["inv2"] = np.where(i % 64 < 16, inv2[i % 8], 0).astype(f)[:, None]
    out["iota"] = np.tile(np.arange(2 * P, dtype=f), (P, 1))
    out["iota8"] = np.tile(np.arange(8, dtype=f), (P, 1))
    return out


def layout():
    off, n = {}, 0
    for k, v in shape_constants().items():
        off[k] = (n, v.shape[1])
        n += v.shape[1]
    return off, n


class Queue:

    def __init__(self, name, sem):
        self.name, self.sem, self.ops, self.n, self.seen = name, sem, [], 0, {}

    def wait(self, *tokens):
        for t in tokens:
            if t is None:
                continue
            if isinstance(t, list):
                self.wait(*t)
                continue
            sem, val = t
            if self.seen.get(id(sem), 0) < val:
                self.seen[id(sem)] = val
                self.ops.append(lambda e, sem=sem, val=val: e.wait_ge(sem, val))

    def __call__(self, fn, *tokens):
        self.wait(*tokens)
        self.n += 1
        self.ops.append(lambda e, fn=fn, done=self.sem: fn(e).then_inc(done, 1))
        return (self.sem, self.n)

    def quiet(self, fn, *tokens):
        self.wait(*tokens)
        self.ops.append(fn)

    def last(self):
        return (self.sem, self.n) if self.n else None

    def play(self, e):
        for op in self.ops:
            op(e)

    def enter(self, sem):
        self.kept = (self.ops, self.n, self.sem, self.seen)
        self.ops, self.n, self.sem, self.seen = [], 0, sem, dict(self.seen)

    def leave(self, flag, *tokens):
        body = self.ops
        self.ops, self.n, self.sem, self.seen = self.kept
        self.wait(*tokens)

        def run(e):
            with e.If(e.value_load(flag, min_val=0, max_val=1) > 0):
                for op in body:
                    op(e)

        self.ops.append(run)


class Pool:

    def __init__(self, bufs):
        self.bufs, self.free, self.i = bufs, [[] for _ in bufs], 0

    def take(self):
        i = self.i
        self.i = (i + 1) % len(self.bufs)
        return i, self.bufs[i], self.free[i]

    def give(self, i, *tokens):
        self.free[i] = list(tokens)


def program(nc, A, cst, out, dbg=None):
    ctx = ExitStack()
    with ctx:
        def sb(name, shape, dt=F32):
            return ctx.enter_context(nc.sbuf_tensor(name, shape, dt))

        def sem(name):
            return ctx.enter_context(nc.semaphore(name))

        off, ncst = layout()
        ring = sb("ring", [P, NSLOT, 4096])
        C = sb("consts", [P, ncst])
        hT = sb("hT", [P, 8, T])
        nT = sb("nT", [P, 8, T])
        vec = sb("vec", [P, 224])
        sm = sb("sm", [P, 512])
        ARN = 27200
        arena = sb("arena", [P, ARN])
        bank = [ctx.enter_context(nc.psum_tensor(f"bank{i}", [P, 512], F32)) for i in range(8)]

        def cc(name, a=0, b=None):
            o, n = off[name]
            return C[:, o + a:o + (n if b is None else b)]

        PE = Queue("PE", sem("s_pe"))
        V = Queue("V", sem("s_dve"))
        S = Queue("S", sem("s_act"))
        G = Queue("G", sem("s_pool"))
        SP = Queue("SP", None)
        s_slot = [sem(f"s_slot{i}") for i in range(NSLOT)]
        n_slot = [0] * NSLOT
        s_in = [sem(f"s_in{i}") for i in range(8)]
        n_in = [0] * 8
        s_out = sem("s_out")
        PS = Pool([b[:, :] for b in bank])
        W = Pool([ring[:, i, :] for i in range(NSLOT)])

        top = [0]

        def carve(*dims):
            n = int(np.prod(dims))
            a = arena[:, top[0]:top[0] + n]
            top[0] += n
            assert top[0] <= ARN, top[0]
            if len(dims) == 2:
                a = a.rearrange("p (a b) -> p a b", a=dims[0])
            elif len(dims) == 3:
                a = a.rearrange("p (a b c) -> p a b c", a=dims[0], b=dims[1])
            return a

        smtop = [0]

        def small(n):
            a = sm[:, smtop[0]:smtop[0] + n]
            smtop[0] += n
            assert smtop[0] <= 512
            return a

        def everyone():
            return [q.last() for q in (PE, V, S, G)]

        def load_in(which, dst, src, *tokens):
            n_in[which] += 16
            SP.quiet(lambda e: e.dma_start(dst, src).then_inc(s_in[which], 16), *tokens)
            return (s_in[which], n_in[which])

        def stream(parts, shape):
            i, buf, free = W.take()
            k, n = shape
            view = buf[:, 0:k * n].rearrange("p (k n) -> p k n", k=k)
            for pick, src in parts:
                n_slot[i] += 16
                SP.quiet(lambda e, d=pick(view), s=src, done=s_slot[i]: e.dma_start(d, s).then_inc(done, 16), *free)
            return i, view, (s_slot[i], n_slot[i])

        def lin(w, K, c0, ncols, rhs, n, t_rhs, evac):
            KT = K // P
            for g0 in range(0, ncols, 512):
                gw = min(512, ncols - g0)
                banks = {}
                for kb in range(0, KT, 8):
                    nk = min(8, KT - kb)
                    src = w[kb * P:(kb + nk) * P, c0 + g0:c0 + g0 + gw].rearrange("(k p) n -> p k n", p=P)
                    slot, view, tw = stream([(lambda v: v, src)], (nk, gw))
                    for mi in range(gw // P):
                        if kb == 0:
                            banks[mi] = PS.take()
                        bi, ps, free = banks[mi]
                        PE.wait(tw, t_rhs, free)
                        for k in range(nk):
                            kk = kb + k
                            f = lambda e, ps=ps, view=view, k=k, mi=mi, kk=kk, r=rhs(kk): e.matmul(
                                ps[:, 0:n], view[:, k, mi * P:(mi + 1) * P], r,
                                start=(kk == 0), stop=(kk == KT - 1))
                            if k == nk - 1:
                                t = PE(f)
                            else:
                                PE.quiet(f)
                        if kb + nk == KT:
                            PS.give(bi, evac(g0 // P + mi, ps[:, 0:n], t))
                    W.give(slot, t)

        def lin_tok(view, ncols, lhs, nk, t_w, t_lhs, m):
            bi, ps, free = PS.take()
            PE.wait(t_w, t_lhs, free)
            for k in range(nk):
                f = lambda e, ps=ps, k=k, a=lhs(k), b=view(k): e.matmul(ps[0:m, 0:ncols], a, b, start=(k == 0), stop=(k == nk - 1))
                if k == nk - 1:
                    t = PE(f)
                else:
                    PE.quiet(f)
            return bi, ps[0:m, 0:ncols], t

        def mm1(ps, lhsT, rhs, *tokens, start=True, stop=True):
            return PE(lambda e, ps=ps: e.matmul(ps, lhsT, rhs, start=start, stop=stop), *tokens)

        ident = cc("ident")
        ones = cc("ones")

        wsm = carve(8, 24)
        top_g = top[0]
        xin = carve(2, 1024)
        min_ = carve(1024)[0:NM, :]
        rows = carve(2, P)
        t_c = load_in(0, C[:, :], cst)
        t_x = load_in(1, xin, A["x"][0].rearrange("(a p) d -> p a d", p=P))
        t_x = load_in(1, min_, A["meta_tokens"])
        vrows, nv = {}, 0
        for key in ("pre_mix_norm", "post_mix_norm", "pre_mlp_norm", "post_mlp_norm"):
            vrows[key] = nv
            t_v = load_in(2, rows[nv:nv + 8, 0, :], A[key].rearrange("l (a p) -> (l a) p", p=P))
            nv += 8
        for key in ("ln1_g_2", "ln1_b_2", "ln2_g_2", "ln2_b_2"):
            vrows[key] = nv
            t_v = load_in(2, rows[nv:nv + 16, 0, :], A[key].rearrange("l (a p) -> (l a) p", p=P))
            nv += 16
        vrows["conv_a_2"] = nv
        t_v = load_in(2, rows[nv:nv + 18, 0, :], A["conv_a_2"].rearrange("l j (a p) -> (l j a) p", p=P))
        nv += 18
        vrows["gdn_norm"] = nv
        t_v = load_in(2, rows[nv:nv + 1, 0, :], A["gdn_norm"])
        nv += 1
        t_v = load_in(2, rows[0:96, 1, :], A["conv_w"].rearrange("l j (a p) -> (l j a) p", p=P))
        vrows["conv_w"] = 128
        dtb = small(8)
        alog = small(8)
        t_g = load_in(3, dtb, A["dt_bias"].to_broadcast([P, 8]))
        t_g = load_in(3, alog, A["a_log"].to_broadcast([P, 8]))
        posi = sb("posi", [P, SEQ], I32)
        t_pos = load_in(4, posi[:, :], A["positions_2"].to_broadcast([P, SEQ]))
        win = A["w_in"][0]
        for dst0, src0, nn in ((0, C_IN["gb"], 16), (16, C_IN["iw"], 8)):
            t_wsm = load_in(5, wsm[:, :, dst0:dst0 + nn], win[:, src0:src0 + nn].rearrange("(k p) n -> p k n", p=P))
        eps6, eps5, one1 = small(1), small(1), small(1)
        zero1 = small(1)
        for ap, v in ((eps6, 1e-6), (eps5, 1e-5), (one1, 1.0), (zero1, 0.0)):
            t_eps = G(lambda e, ap=ap, v=v: e.memset(ap, v))

        for j, n in ((0, nv), (1, 96)):
            bi, ps, free = PS.take()
            t = PE(lambda e, ps=ps, j=j, n=n: e.transpose(ps[:, 0:n], rows[0:n, j, :], cc("ident")[0:n, 0:n]), t_v, t_c, free)
            t_vec = V(lambda e, ps=ps, j=j, n=n: e.tensor_copy(vec[:, 128 * j:128 * j + n], ps[:, 0:n]), t)
            PS.give(bi, t_vec)

        def vcol(name, i):
            return vec[:, vrows[name] + i:vrows[name] + i + 1]

        t_h = []
        for k in range(8):
            bi, ps, free = PS.take()
            PE.wait(t_x, t_c, free)
            PE.quiet(lambda e, ps=ps, k=k: e.transpose(ps[:, 0:NM], min_[:, k * P:(k + 1) * P], cc("ident")[0:NM, 0:NM]))
            PE.quiet(lambda e, ps=ps, k=k: e.transpose(ps[:, NM:NM + P], xin[:, 0, k * P:(k + 1) * P], ident))
            t = PE(lambda e, ps=ps, k=k: e.transpose(ps[:, NM + P:T], xin[:, 1, k * P:(k + 1) * P], ident))
            q = V if k % 2 else S
            if q is V:
                t = V(lambda e, ps=ps, k=k: e.tensor_copy(hT[:, k, :], ps[:, 0:T]), t)
            else:
                t = S(lambda e, ps=ps, k=k: e.copy(hT[:, k, :], ps[:, 0:T]), t)
            PS.give(bi, t)
            t_h.append(t)

        def inv_rms(sq, K, n, scale, eps, dst, t_sq):
            bi, ps, free = PS.take()
            PE.wait(t_sq, t_c, free)
            for k in range(K):
                f = lambda e, ps=ps, k=k, b=sq(k): e.matmul(ps[:, 0:n], ones, b, start=(k == 0), stop=(k == K - 1))
                if k == K - 1:
                    t = PE(f)
                else:
                    PE.quiet(f)
            t1 = S(lambda e, ps=ps: e.activation(dst, ps[:, 0:n], ACT.Sqrt, bias=eps, scale=scale), t, t_eps)
            PS.give(bi, t1)
            return V(lambda e: e.reciprocal(dst, dst), t1)

        def rms_scaled(src, n, gname, gi, dst, add, t_src):
            m = top[0]
            sq = carve(8, n)
            r = carve(n)
            tmp = carve(8, n) if add is not None else None
            top[0] = m
            guard = everyone()
            t = S(lambda e: e.activation(sq, src, ACT.Square), t_src, guard)
            t_r = inv_rms(lambda k: sq[:, k, :], 8, n, 1.0 / 1024, eps6, r, [t, guard])
            res = []
            for k in range(8):
                d = dst if add is None else tmp
                t = V(lambda e, d=d, k=k: e.scalar_tensor_tensor(out=d[:, k, :], in0=src[:, k, :], scalar=vcol(gname, gi + k), in1=r, op0=ALU.mult, op1=ALU.mult), t_r, t_vec, guard)
                if add is not None:
                    t = G(lambda e, k=k: e.tensor_tensor(dst[:, k, :], add[:, k, :], tmp[:, k, :], ALU.add), t)
                res.append(t)
            return res

        top_in = 2048
        t_n = rms_scaled(hT[:, :, :], T, "pre_mix_norm", 0, nT, None, t_h)
        t_in_done = everyone()

        top[0] = top_g
        gq = carve(8, T)
        gk = carve(8, T)
        gv = carve(8, T)
        mark_gdn = top[0]
        xpads = [carve(T + 3) for _ in range(4)]
        sqs = [carve(T) for _ in range(3)]
        rs_ = [carve(T) for _ in range(3)]
        XP, SQ, RR = Pool(xpads), Pool(sqs), Pool(rs_)
        t_z = None
        for x in xpads:
            t_z = G(lambda e, x=x: e.memset(x[:, 0:3], 0.0), t_in_done)

        toks = ((0, 16, P), (1, 16 + P, P), (2, 0, NM))
        at = small(24)
        g3 = small(24)
        b3 = small(24)
        iw = small(16)
        t_at0 = V(lambda e: e.memset(at, 0.0))
        t_b30 = V(lambda e: e.memset(b3, 0.0))
        t_g3 = []
        for c, t0, n in toks:
            bi, ps, t = lin_tok(lambda k: wsm[:, k, :], 24, lambda k, t0=t0, n=n: nT[:, k, t0:t0 + n], 8, t_wsm, t_n, n)
            t = S(lambda e, ps=ps, c=c, n=n: e.activation(b3[0:n, 8 * c:8 * c + 8], ps[:, 0:8], ACT.Sigmoid), t, t_b30)
            ts = [t, V(lambda e, ps=ps, c=c, n=n: e.tensor_tensor(at[0:n, 8 * c:8 * c + 8], ps[:, 8:16], dtb[0:n, :], ALU.add), t, t_g, t_at0)]
            if c < 2:
                ts.append(V(lambda e, ps=ps, c=c: e.tensor_scalar(iw[:, 8 * c:8 * c + 8], ps[:, 16:24], float(512 ** -0.5), None, ALU.mult), t))
            PS.give(bi, *ts)
            t_g3 += ts
        t_iw = t_g3
        na, ea = small(24), small(24)
        t = V(lambda e: e.tensor_scalar(na, at, -1.0, None, ALU.mult), t_g3)
        t = V(lambda e: e.tensor_tensor(na, na, at, ALU.min), t)
        t = S(lambda e: e.activation(ea, na, ACT.Exp), t)
        t = S(lambda e: e.activation(ea, ea, ACT.Ln, bias=one1), t, t_eps)
        t_al = S(lambda e: e.activation(alog, alog, ACT.Exp), t_g)
        t = V(lambda e: e.scalar_tensor_tensor(out=g3, in0=at, scalar=0.0, in1=ea, op0=ALU.max, op1=ALU.add), t)
        for c in range(3):
            t_g3 = V(lambda e, c=c: e.scalar_tensor_tensor(out=g3[:, 8 * c:8 * c + 8], in0=g3[:, 8 * c:8 * c + 8], scalar=-1.0, in1=alog, op0=ALU.mult, op1=ALU.mult), t, t_al)

        def conv_group(c0, w0, dst, norm):
            done = []

            def evac(j, ps, t):
                xi, xp, xfree = XP.take()
                t1 = S(lambda e, ps=ps: e.copy(xp[:, 3:3 + T], ps), t, xfree, t_z)
                d = dst[:, j, :]
                tv = V(lambda e: e.tensor_scalar(d, xp[:, 0:T], vcol("conv_w", w0 + j), None, ALU.mult), t1, t_vec, t_in_done)
                for u in range(1, 4):
                    tv = V(lambda e, u=u: e.scalar_tensor_tensor(out=d, in0=xp[:, u:u + T], scalar=vcol("conv_w", 24 * u + w0 + j), in1=d, op0=ALU.mult, op1=ALU.add), tv)
                XP.give(xi, tv)
                t2 = S(lambda e: e.activation(d, d, ACT.Silu), tv)
                done.append(t2)
                return t1

            lin(win, 1024, c0, 1024, lambda k: nT[:, k, :], T, t_n, evac)
            if norm is None:
                return done
            fin = []
            for j in range(8):
                d = dst[:, j, :]
                si, sq, sfree = SQ.take()
                ri, r, rfree = RR.take()
                t = G(lambda e, d=d, sq=sq: e.tensor_tensor(sq, d, d, ALU.mult), done[j], sfree)
                V.wait(rfree)
                S.wait(rfree)
                t = inv_rms(lambda k, sq=sq: sq, 1, T, 1.0, eps6, r, t)
                SQ.give(si, t)
                t = V(lambda e, d=d, r=r: e.scalar_tensor_tensor(out=d, in0=d, scalar=norm, in1=r, op0=ALU.mult, op1=ALU.mult), t)
                RR.give(ri, t)
                fin.append(t)
            return fin

        t_k = conv_group(C_IN["gk"], 8, gk, 1.0)
        t_v_ = conv_group(C_IN["gv"], 16, gv, None)
        t_q = conv_group(C_IN["gq"], 0, gq, float(128 ** -0.5))
        top[0] = mark_gdn
        g0 = everyone()
        dec = carve(17, P)
        AT = carve(17, P)
        D = carve(17, P)
        DT = carve(17, P)
        nkb = carve(17, P)
        kta = carve(17, P)
        vb = carve(17, P)
        S1 = carve(8, P)
        S2 = carve(8, P)
        MTs = Pool([carve(4, P) for _ in range(3)])
        Ys = Pool([carve(4, P) for _ in range(3)])
        EGs = Pool([b for b in MTs.bufs[:2]])
        kmeta, vmeta = S2[:, 0, :], S2[:, 1, :]
        for a, b, t in ((kmeta, gk, t_k), (vmeta, gv, t_v_)):
            t_meta = V(lambda e, a=a, b=b: e.tensor_copy(a.rearrange("p (h t) -> p h t", h=8), b[:, :, 0:NM]), t, g0)

        gG, gB, GC, GL = small(17), small(17), small(17), small(17)
        eg, ekt, egl, nbe = small(17), small(17), small(17), small(17)
        gmb = small(16)
        hm = small(16)
        t = V(lambda e: e.tensor_copy(gG[:, 0:16].rearrange("p (h c) -> p c h", c=2), g3[:, 0:16].rearrange("p (c h) -> p c h", c=2)), t_g3)
        t2 = V(lambda e: e.tensor_copy(gB[:, 0:16].rearrange("p (h c) -> p c h", c=2), b3[:, 0:16].rearrange("p (c h) -> p c h", c=2)), t_iw)
        t3 = V(lambda e: e.tensor_copy(gmb[:, 0:8], g3[:, 16:24]), t_g3)
        t4 = V(lambda e: e.tensor_copy(gmb[:, 8:16], b3[:, 16:24]), t_iw)
        bi, ps, free = PS.take()
        t = mm1(ps[:, 0:16], cc("Rep")[0:NM, :], gmb[0:NM, :], t, t2, t3, t4, free)
        t5 = V(lambda e, ps=ps: e.tensor_tensor(hm[:, 0:8], ps[:, 0:8], cc("hmask"), ALU.mult), t)
        t6 = V(lambda e, ps=ps: e.tensor_tensor(hm[:, 8:16], ps[:, 8:16], cc("hmask"), ALU.mult), t)
        PS.give(bi, t5, t6)
        t = V(lambda e: e.tensor_reduce(gG[:, 16:17], hm[:, 0:8], AX, ALU.add), t5)
        t_gb = V(lambda e: e.tensor_reduce(gB[:, 16:17], hm[:, 8:16], AX, ALU.add), t6)
        bi, ps, free = PS.take()
        mm1(ps[:, 0:16], cc("U"), gG[:, 0:16], t_gb, free)
        mm1(ps[:, 16:17], cc("Ub"), gG[:, 16:17])
        mm1(ps[:, 17:33], ones, gG[:, 0:16])
        t = mm1(ps[:, 33:34], cc("OB"), gG[:, 16:17])
        t1 = V(lambda e, ps=ps: e.tensor_copy(GC, ps[:, 0:17]), t)
        t2 = V(lambda e, ps=ps: e.tensor_copy(GL, ps[:, 17:34]), t)
        PS.give(bi, t1, t2)
        t3 = V(lambda e: e.tensor_tensor(ekt, GL, GC, ALU.subtract), t2)
        ta = S(lambda e: e.activation(ekt, ekt, ACT.Exp), t3)
        tb = S(lambda e: e.activation(eg, GC, ACT.Exp), t1)
        tc = S(lambda e: e.activation(egl, GL, ACT.Exp), t2)
        td = V(lambda e: e.scalar_tensor_tensor(out=nbe, in0=gB, scalar=-1.0, in1=eg, op0=ALU.mult, op1=ALU.mult), tb)
        t_gates = [ta, tb, tc, td]

        groups = [list(range(4 * i, 4 * i + 4)) for i in range(4)] + [[16]]

        def tok(x, m):
            if m == 16:
                return kmeta if x is gk else vmeta
            return x[:, m // 2, NM + P * (m % 2):NM + P * (m % 2) + P]

        def bc(ap, n):
            return ap.unsqueeze(1).to_broadcast([P, n, P])

        t_kv, t_dec, t_AT, t_att, t_qd = {}, {}, {}, {}, {}
        for g in groups:
            n = len(g) * P
            gl = slice(g[0], g[-1] + 1)
            msk = (cc("Ub"), cc("Ubs")) if g[0] == 16 else (cc("U"), cc("Us"))
            bi, ps, free = PS.take()
            PE.wait(t_k, free, g0, t_meta)
            for x, m in enumerate(g):
                t = PE(lambda e, ps=ps, x=x, m=m: e.transpose(ps[:, x * P:(x + 1) * P], tok(gk, m), ident))
            ts = []
            for x, m in enumerate(g):
                ts.append(S(lambda e, ps=ps, x=x, m=m: e.activation(nkb[:, m, :], ps[:, x * P:(x + 1) * P], ACT.Copy, scale=nbe[:, m:m + 1]), t, t_gates, g0))
            t = ts[-1]
            for x, m in enumerate(g):
                ts.append(V(lambda e, ps=ps, x=x, m=m: e.tensor_scalar(kta[:, m, :], ps[:, x * P:(x + 1) * P], ekt[:, m:m + 1], None, ALU.mult), t, t_gates, g0))
            PS.give(bi, *ts)
            bi, ps, free = PS.take()
            PE.wait(t_v_, free)
            for x, m in enumerate(g):
                t = PE(lambda e, ps=ps, x=x, m=m: e.transpose(ps[:, x * P:(x + 1) * P], tok(gv, m), ident))
            for x, m in enumerate(g):
                ts.append(S(lambda e, ps=ps, x=x, m=m: e.activation(vb[:, m, :], ps[:, x * P:(x + 1) * P], ACT.Copy, scale=gB[:, m:m + 1]), t, t_gb))
            PS.give(bi, *ts[-len(g):])
            t_kv[g[0]] = ts
            bi, ps, free = PS.take()
            PE.wait(free, t_gb)
            for x, m in enumerate(g):
                t = mm1(ps[:, x * P:(x + 1) * P], gG[:, m:m + 1].to_broadcast([P, P]), cc("Ub" if m == 16 else "U"))
            tr = []
            if g[0] != 16:
                ei, eb, efree = EGs.take()
                t = te = S(lambda e, ps=ps, eb=eb: e.activation(eb.rearrange("p a b -> p (a b)"), ps, ACT.Exp), t, efree, g0)
                h0 = g[0] // 2
                qv = gq[:, h0:h0 + 2, NM:T]
                t_qd[g[0]] = (ei, eb, te, qv)
            for x, m in enumerate(g):
                td = V(lambda e, ps=ps, x=x, m=m: e.tensor_scalar(dec[:, m, :], ps[:, x * P:(x + 1) * P], GC[:, m:m + 1], 0.0, ALU.subtract, ALU.min), t, t_gates, g0)
            tr.append(td)
            PS.give(bi, *tr)
            td = S(lambda e, gl=gl: e.activation(dec[:, gl, :], dec[:, gl, :], ACT.Exp), td)
            t_s = G(lambda e, gl=gl, k=len(g), mk=msk[1]: e.tensor_tensor(AT[:, gl, :], dec[:, gl, :], bc(mk, k), ALU.mult), td, g0)
            t_i = G(lambda e, gl=gl, k=len(g), mk=msk[0]: e.tensor_tensor(dec[:, gl, :], dec[:, gl, :], bc(mk, k), ALU.mult), t_s)
            bi, ps, free = PS.take()
            PE.wait(free, t_gb)
            for x, m in enumerate(g):
                t = mm1(ps[:, x * P:(x + 1) * P], gB[:, m:m + 1].to_broadcast([P, P]), ident)
            t = V(lambda e, ps=ps, gl=gl, n=n: e.tensor_tensor(AT[:, gl, :].rearrange("p a b -> p (a b)"), AT[:, gl, :].rearrange("p a b -> p (a b)"), ps[:, 0:n], ALU.mult), t, t_s)
            PS.give(bi, t)
            bi, ps, free = PS.take()
            PE.wait(free)
            for x, m in enumerate(g):
                t2 = mm1(ps[:, x * P:(x + 1) * P], tok(gk, m), tok(gk, m))
            t = V(lambda e, ps=ps, gl=gl, n=n: e.tensor_tensor(AT[:, gl, :].rearrange("p a b -> p (a b)"), AT[:, gl, :].rearrange("p a b -> p (a b)"), ps[:, 0:n], ALU.mult), t, t2)
            PS.give(bi, t)
            t_AT[g[0]] = t
            if g[0] != 16:
                bi, ps, free = PS.take()
                PE.wait(free, t_q)
                for x, m in enumerate(g):
                    t2 = mm1(ps[:, x * P:(x + 1) * P], tok(gk, m), tok(gq, m))
                t = V(lambda e, ps=ps, gl=gl, n=n: e.tensor_tensor(dec[:, gl, :].rearrange("p a b -> p (a b)"), dec[:, gl, :].rearrange("p a b -> p (a b)"), ps[:, 0:n], ALU.mult), t_i, t2)
                PS.give(bi, t)
                t_att[g[0]] = t
                ei, eb, te, qv = t_qd[g[0]]
                tq = G(lambda e, qv=qv, eb=eb: e.tensor_tensor(qv, qv, eb.rearrange("p (h c) b -> p h (c b)", c=2), ALU.mult), te, t2)
                EGs.give(ei, tq)
                t_qd[g[0]] = tq

        t_D = {g[0]: (V(lambda e, g=g: e.tensor_copy(D[:, g[0]:g[-1] + 1, :], bc(ident, len(g))), g0),
                      G(lambda e, g=g: e.tensor_copy(DT[:, g[0]:g[-1] + 1, :], bc(ident, len(g))), g0)) for g in groups}
        MTs.free = [list(EGs.free[0]), list(EGs.free[1]), []]
        steps = [(b, g) for b in (1, 2, 4, 8, 16, 32, 64) for g in groups if b < 16 or g[0] != 16]
        live = {}

        def inv_a(i):
            b, g = steps[i]
            gl, k, n = slice(g[0], g[-1] + 1), len(g), len(g) * P
            mi, mt, mfree = MTs.take()
            yi, y, yfree = Ys.take()
            t = G(lambda e: e.tensor_tensor(mt[:, 0:k, :], AT[:, gl, :], bc(cc(f"m{b}"), k), ALU.mult), t_AT[g[0]], mfree)
            bi, ps, free = PS.take()
            PE.wait(free, t, *t_D[g[0]])
            for x, m in enumerate(g):
                t = mm1(ps[:, x * P:(x + 1) * P], mt[:, x, :], D[:, m, :])
            MTs.give(mi, t)
            t = S(lambda e, ps=ps: e.copy(y[:, 0:k, :].rearrange("p a b -> p (a b)"), ps[:, 0:n]), t, yfree, g0)
            PS.give(bi, t)
            live[i] = (yi, y, t)

        def inv_b(i):
            b, g = steps[i]
            gl, n = slice(g[0], g[-1] + 1), len(g) * P
            yi, y, ty = live.pop(i)
            lastlevel = (b == 64) or (g[0] == 16 and b == 8)
            bi, ps, free = PS.take()
            PE.wait(free, ty)
            for x, m in enumerate(g):
                t = mm1(ps[:, x * P:(x + 1) * P], y[:, x, :], DT[:, m, :])
            if not lastlevel:
                bj, ps2, free2 = PS.take()
                PE.wait(free2)
                for x, m in enumerate(g):
                    t = mm1(ps2[:, x * P:(x + 1) * P], DT[:, m, :], y[:, x, :])
            Ys.give(yi, t)
            fl = lambda a: a[:, gl, :].rearrange("p a b -> p (a b)")
            t2 = V(lambda e, ps=ps: e.tensor_tensor(fl(DT), fl(DT), ps[:, 0:n], ALU.subtract), t)
            PS.give(bi, t2)
            t1 = t2
            if not lastlevel:
                t1 = V(lambda e: e.tensor_tensor(fl(D), fl(D), ps2[:, 0:n], ALU.subtract), t)
                PS.give(bj, t1)
            t_D[g[0]] = (t1, t2)

        for i in range(len(steps) + 1):
            if i < len(steps):
                inv_a(i)
            if i >= 1:
                inv_b(i - 1)
        TT = DT
        t_T = [t_D[g[0]][1] for g in groups]
        t_kvs = [t for v in t_kv.values() for t in v]

        bi, ps, free = PS.take()
        t = mm1(ps[:, 0:P], TT[:, 16, :], vb[:, 16, :], t_T, t_kvs, free)
        vn = D
        t_vn = V(lambda e, ps=ps: e.tensor_copy(vn[:, 16, :], ps[:, 0:P]), t)
        PS.give(bi, t_vn)
        ktm = S2
        for h in range(8):
            t = G(lambda e, h=h: e.tensor_scalar(ktm[:, h, :], kta[:, 16, :], cc("hmask", h, h + 1), None, ALU.mult), t_kvs, t_T)
        t_S = []
        for q in range(2):
            bi, ps, free = PS.take()
            PE.wait(t, t_vn, free)
            for x in range(4):
                t2 = mm1(ps[:, x * P:(x + 1) * P], ktm[:, 4 * q + x, :], vn[:, 16, :])
            t_S.append(V(lambda e, ps=ps, q=q: e.tensor_copy(S1[:, 4 * q:4 * q + 4, :].rearrange("p a b -> p (a b)"), ps), t2))
            PS.give(bi, t_S[-1])
        t_ktm = t2
        t_w = {}
        wT = AT
        for g in groups[:4]:
            bi, ps, free = PS.take()
            PE.wait(free)
            for x, m in enumerate(g):
                t = mm1(ps[:, x * P:(x + 1) * P], nkb[:, m, :], TT[:, m, :])
            t_w[g[0]] = S(lambda e, ps=ps, g=g: e.copy(wT[:, g[0]:g[-1] + 1, :].rearrange("p a b -> p (a b)"), ps), t, [PE.last()], [G.last()])
            PS.give(bi, t_w[g[0]])
        oT = gv
        t_o = {}
        cur, t_cur = S1, {h: t_S[h // 4] for h in range(8)}
        for c in range(2):
            nxt = {}
            for hp in range(0, 8, 4):
                bi, ps, free = PS.take()
                PE.wait(free)
                for x in range(4):
                    h = hp + x
                    m = 2 * h + c
                    mm1(ps[:, x * P:(x + 1) * P], TT[:, m, :], vb[:, m, :], stop=False)
                    t = mm1(ps[:, x * P:(x + 1) * P], wT[:, m, :], cur[:, h, :], t_w[m // 4 * 4], t_cur[h], start=False)
                ms = [2 * (hp + x) + c for x in range(4)]
                vview = vn[:, ms[0]:ms[-1] + 1:2, :]
                tv = S(lambda e, ps=ps, vview=vview: e.copy(vview, ps.rearrange("p (a b) -> p a b", b=P)), t)
                PS.give(bi, tv)
                if c == 0:
                    bi, ps, free = PS.take()
                    PE.wait(free, tv)
                    for x in range(4):
                        t = mm1(ps[:, x * P:(x + 1) * P], kta[:, ms[x], :], vn[:, ms[x], :])
                    for x in range(4):
                        h = hp + x
                        nxt[h] = V(lambda e, ps=ps, x=x, h=h, m=ms[x]: e.scalar_tensor_tensor(out=S2[:, h, :], in0=S1[:, h, :], scalar=egl[:, m:m + 1], in1=ps[:, x * P:(x + 1) * P], op0=ALU.mult, op1=ALU.add), t, t_ktm, t_cur[h])
                    PS.give(bi, *nxt.values())
                bi, ps, free = PS.take()
                PE.wait(free, tv)
                for x in range(4):
                    h, m = hp + x, ms[x]
                    mm1(ps[:, x * P:(x + 1) * P], cur[:, h, :], tok(gq, m), t_qd[m // 4 * 4], stop=False)
                    t = mm1(ps[:, x * P:(x + 1) * P], vn[:, m, :], dec[:, m, :], t_att[m // 4 * 4], start=False)
                to = S(lambda e, ps=ps, hp=hp, c=c: e.copy(oT[:, hp:hp + 4, P * c:P * c + P], ps.rearrange("p (a b) -> p a b", b=P)), t)
                PS.give(bi, to)
                t_o[(c, hp)] = to
            cur, t_cur = S2, nxt
        yg = gk
        t_y = []
        g1 = everyone()
        gz = nkb.rearrange("p a b -> p (a b)")[:, 0:8 * SEQ].rearrange("p (a b) -> p a b", a=8)
        t_zz = []

        def evac_z(j, ps, t):
            t = S(lambda e, ps=ps: e.activation(gz[:, j, :], ps, ACT.Silu), t, g1)
            t_zz.append(t)
            return t

        lin(win, 1024, C_IN["gz"], 1024, lambda k: nT[:, k, NM:T], SEQ, t_n, evac_z)
        rr2 = [dec[:, 2 * j:2 * j + 2, :].rearrange("p a b -> p (a b)") for j in range(8)]
        sq2 = [AT[:, 2 * j:2 * j + 2, :].rearrange("p a b -> p (a b)") for j in range(8)]
        for h in range(8):
            o = oT[:, h, 0:SEQ]
            t = G(lambda e, h=h, o=o: e.tensor_tensor(sq2[h], o, o, ALU.mult), g1)
            S.wait(g1)
            t = inv_rms(lambda k, h=h: sq2[h], 1, SEQ, 1.0 / 128, eps6, rr2[h], t)
            t = V(lambda e, h=h, o=o: e.scalar_tensor_tensor(out=o, in0=o, scalar=vcol("gdn_norm", 0), in1=rr2[h], op0=ALU.mult, op1=ALU.mult), t)
            t_y.append(G(lambda e, h=h, o=o: e.tensor_tensor(yg[:, h, 0:SEQ], o, gz[:, h, :], ALU.mult), t, t_zz))
        if dbg is not None and "yg" in dbg:
            SP.quiet(lambda e: e.dma_start(dbg["yg"], yg[:, :, 0:SEQ]).then_inc(s_out, 16), t_y)

        def rope(dst, src, rot, cosn, sinn, t_src, guard, tmp, scale=None):
            n = src.shape[-1]
            bi, ps, free = PS.take()
            t = mm1(ps[:, 0:n], rot, src, t_src, free)
            ti, tb, tfree = tmp.take()
            t1 = V(lambda e, ps=ps: e.tensor_tensor(tb[:, 0:n], ps[:, 0:n], sinn, ALU.mult), t, tfree, guard)
            PS.give(bi, t1)
            t2 = G(lambda e: e.tensor_tensor(src, src, cosn, ALU.mult), t, t_src)
            if scale is None:
                t3 = V(lambda e: e.tensor_tensor(dst, src, tb[:, 0:n], ALU.add), t1, t2)
            else:
                t2 = V(lambda e: e.tensor_tensor(src, src, tb[:, 0:n], ALU.add), t1, t2)
                t3 = V(lambda e: e.tensor_scalar(dst, src, scale, None, ALU.mult), t2)
            tmp.give(ti, t3)
            return t3

        top[0] = mark_gdn
        g2 = everyone()
        aq = carve(8, SEQ)
        ak = carve(2, T)
        iq = carve(4, SEQ)
        ik = carve(T)
        av = carve(3, 256)
        yd = carve(8, SEQ)
        rtmp = Pool([carve(T) for _ in range(3)])
        mb = carve(2, T)
        work = carve(2, T)
        m8 = carve(2, 8)
        rel = Pool([carve(T) for _ in range(3)])
        m_att = top[0]
        t_r = {}

        def roped(dst, names, rot, scale, n0):
            res = []
            t_r[id(dst)] = res

            def evac(j, ps, t):
                d = dst[:, j, :]
                t = S(lambda e, ps=ps: e.copy(d, ps), t, g2)
                res.append((d, t))
                return t
            return evac, res

        ev, raw_iq = roped(iq, None, None, None, None)
        lin(win, 1024, C_IN["iq"], 512, lambda k: nT[:, k, NM:T], SEQ, t_n, ev)
        slot, view, tw = stream([(lambda v: v[:, :, 0:64], win[:, C_IN["ik"]:C_IN["ik"] + 64].rearrange("(k p) n -> p k n", p=P)),
                                 (lambda v: v[:, :, 64:128], win[:, C_IN["ik"]:C_IN["ik"] + 64].rearrange("(k p) n -> p k n", p=P))], (8, P))
        bi, ps, t = lin_tok(lambda k: nT[:, k, :], T, lambda k: view[:, k, :], 8, tw, t_n, P)
        W.give(slot, t)
        t = S(lambda e, ps=ps: e.copy(ik, ps), t, g2)
        PS.give(bi, t)
        t_ik = rope(ik, ik, cc("R64"), cc("cosI"), cc("sinI"), t, g2, rtmp)
        t_iq = [rope(d, d, cc("R64"), cc("cosI", NM), cc("sinI", NM), t, g2, rtmp) for d, t in raw_iq]

        slot, view, tw = stream([(lambda v: v, win[:, C_IN["ak"]:C_IN["ak"] + 512].rearrange("(k p) n -> p k n", p=P))], (8, 512))
        raw_ak = []
        for j in range(2):
            bi, ps, t = lin_tok(lambda k: nT[:, k, :], T, lambda k, j=j: view[:, k, j * P:(j + 1) * P], 8, tw, t_n, P)
            t = S(lambda e, ps=ps, j=j: e.copy(ak[:, j, :], ps), t, g2)
            PS.give(bi, t)
            raw_ak.append(t)
        t_av = []
        for c, (k0, n) in enumerate(((0, NM), (NM, P), (NM + P, P))):
            bi, ps, t = lin_tok(lambda k: view[:, k, 256:512], 256, lambda k, k0=k0, n=n: nT[:, k, k0:k0 + n], 8, tw, t_n, n)
            t2 = S(lambda e, ps=ps, c=c, n=n: e.copy(av[0:n, c, :], ps), t, g2)
            PS.give(bi, t2)
            t_av.append(t2)
        W.give(slot, t)
        t_ak = [rope(ak[:, j, :], ak[:, j, :], cc("R128"), cc("cosA"), cc("sinA"), raw_ak[j], g2, rtmp) for j in range(2)]

        t_mb = []
        t_acc = []
        for qt in range(2):
            nk = NM + P * (qt + 1)
            acc = work[:, qt, :]
            t_a = None
            if nk < T:
                t_a = V(lambda e, acc=acc, nk=nk: e.memset(acc[:, nk:T], NEG), g2)
            for h in range(8):
                p0 = 64 * (h % 2)
                bi, ps, free = PS.take()
                t = mm1(ps[:, 0:nk], iq[p0:p0 + 64, h // 2, qt * P:(qt + 1) * P], ik[p0:p0 + 64, 0:nk], t_iq[h // 2], t_ik, free)
                ri, r, rfree = rel.take()
                t = S(lambda e, ps=ps, r=r, nk=nk: e.activation(r[:, 0:nk], ps[:, 0:nk], ACT.Relu), t, rfree, g2)
                PS.give(bi, t)
                w1 = iw[:, 8 * qt + h:8 * qt + h + 1]
                if h == 0:
                    t_a = V(lambda e, r=r, acc=acc, nk=nk, w1=w1: e.tensor_scalar(acc[:, 0:nk], r[:, 0:nk], w1, None, ALU.mult), t, t_a, t_iw)
                else:
                    t_a = V(lambda e, r=r, acc=acc, nk=nk, w1=w1: e.scalar_tensor_tensor(out=acc[:, 0:nk], in0=r[:, 0:nk], scalar=w1, in1=acc[:, 0:nk], op0=ALU.mult, op1=ALU.add), t, t_a)
                rel.give(ri, t_a)
            t_a = V(lambda e, acc=acc, nk=nk: e.tensor_tensor(acc[:, nk - P:nk], acc[:, nk - P:nk], cc("CB", P, 2 * P), ALU.add), t_a)
            t_acc.append(t_a)
        for it in range(8):
            for qt in range(2):
                w = work[:, qt, :]
                t = V(lambda e, w=w, qt=qt: e.max(m8[:, qt, :], w), t_acc[qt])
                t_acc[qt] = V(lambda e, w=w, qt=qt: e.match_replace(w, m8[:, qt, :], w, TAKEN), t)
        for qt in range(2):
            nk = NM + P * (qt + 1)
            t = V(lambda e, qt=qt: e.tensor_scalar(mb[:, qt, :], work[:, qt, :], -2e38, NEG, ALU.is_gt, ALU.mult), t_acc[qt])
            t_mb.append(V(lambda e, qt=qt, nk=nk: e.tensor_tensor(mb[:, qt, nk - P:nk], mb[:, qt, nk - P:nk], cc("CB", P, 2 * P), ALU.add), t))

        ev, raw_aq = roped(aq, None, None, None, None)
        lin(win, 1024, C_IN["aq"], 1024, lambda k: nT[:, k, NM:T], SEQ, t_n, ev)
        t_aq = [rope(d, d, cc("R128"), cc("cosA", NM), cc("sinA", NM), t, g2, rtmp, float(128 ** -0.5)) for d, t in raw_aq]

        def attention(units, segs, guard):
            m = top[0]
            ns = len(segs)
            mx = max(u["nk"](1) for u in units)
            Ls = Pool([carve(mx) for _ in range(3)])
            Pbs = Pool([carve(mx) for _ in range(4)])
            PTs = Pool([carve(ns, P) for _ in range(3)])
            sts = Pool([carve(4) for _ in range(4)])
            top[0] = m
            items = [(u, qt) for u in units for qt in range(2)]
            st = {}
            res = []

            def s1(i):
                u, qt = items[i]
                nk = u["nk"](qt)
                bi, ps, free = PS.take()
                t = mm1(ps[:, 0:nk], u["q"][:, qt * P:(qt + 1) * P], u["k"][:, 0:nk], u["t"], free)
                si, s, sfree = sts.take()
                pi, pb, pfree = Pbs.take()
                if u["bias"] is not None:
                    li, L, lfree = Ls.take()
                    t = V(lambda e, ps=ps: e.tensor_tensor(L[:, 0:nk], ps[:, 0:nk], u["bias"](qt), ALU.add), t, lfree, guard)
                    PS.give(bi, t)
                    src = L[:, 0:nk]
                else:
                    src = ps[:, 0:nk]
                t = V(lambda e: e.tensor_reduce(s[:, 0:1], src, AX, ALU.max, negate=True), t, sfree, guard)
                t = S(lambda e: e.activation(pb[:, 0:nk], src, ACT.Exp, bias=s[:, 0:1], accum_out=s[:, 1:2]), t, pfree, guard)
                if u["bias"] is not None:
                    Ls.give(li, t)
                else:
                    PS.give(bi, t)
                t = V(lambda e: e.reciprocal(s[:, 2:3], s[:, 1:2]), t)
                t = V(lambda e: e.tensor_scalar(pb[:, 0:nk], pb[:, 0:nk], s[:, 2:3], None, ALU.mult), t)
                sts.give(si, t)
                st[i] = (pi, pb, t)

            def s2(i):
                u, qt = items[i]
                nk = u["nk"](qt)
                pi, pb, tp = st[i]
                use = [(j, a, n) for j, (a, n) in enumerate(segs) if a < nk]
                bi, ps, free = PS.take()
                PE.wait(tp, free)
                for j, a, n in use:
                    t = PE(lambda e, ps=ps, j=j, a=a, n=n: e.transpose(ps[0:n, j * P:(j + 1) * P], pb[:, a:a + n], ident))
                Pbs.give(pi, t)
                ti, pt, tfree = PTs.take()
                ts = []
                full = [j for j, a, n in use if n == P]
                for j, a, n in use:
                    if n < P:
                        ts.append(S(lambda e, ps=ps, j=j, n=n: e.copy(pt[0:n, j, :], ps[0:n, j * P:(j + 1) * P]), t, tfree, guard))
                j0, j1 = full[0], full[-1] + 1
                ts.append(S(lambda e, ps=ps: e.copy(pt[:, j0:j1, :].rearrange("p a b -> p (a b)"), ps[:, j0 * P:j1 * P]), t, tfree, guard))
                PS.give(bi, *ts)
                st[i] = (ti, pt, ts, use)

            obank = {}

            def s3(i):
                u, qt = items[i]
                ti, pt, ts, use = st.pop(i)
                hd, p0 = u["hd"], u["p0"]
                if qt == 0:
                    obank["b"] = PS.take()
                bi, ps, free = obank["b"]
                PE.wait(free, ts)
                for x, (j, a, n) in enumerate(use):
                    t = mm1(ps[p0:p0 + hd, qt * P:(qt + 1) * P], u["v"](j)[0:n, :], pt[0:n, j, :], start=(x == 0), stop=(x == len(use) - 1))
                PTs.give(ti, t)
                if qt == 1:
                    t = V(lambda e, ps=ps: e.tensor_copy(u["out"], ps[p0:p0 + hd, 0:SEQ]), t, guard)
                    PS.give(bi, t)
                    res.append(t)

            N = len(items)
            for i in range(N + 4):
                if i < N:
                    s1(i)
                if 0 <= i - 2 < N:
                    s2(i - 2)
                if 0 <= i - 3 < N:
                    s3(i - 3)
            return res

        units = [dict(q=aq[:, h, :], k=ak[:, h // 4, :], v=lambda j, h=h: av[:, j, (h // 4) * P:(h // 4 + 1) * P],
                      bias=lambda qt: mb[:, qt, 0:NM + P * (qt + 1)], nk=lambda qt: NM + P * (qt + 1),
                      hd=P, p0=0, out=yd[:, h, :], t=[t_aq[h], t_ak[h // 4], t_mb, t_av]) for h in range(8)]
        t_yd = attention(units, [(0, NM), (NM, P), (NM + P, P)], g2)
        if dbg is not None and "yd" in dbg:
            SP.quiet(lambda e: e.dma_start(dbg["yd"], yd).then_inc(s_out, 16), t_yd)

        top[0] = m_att
        g3_ = everyone()
        gate = carve(16, SEQ)
        mg = aq
        t_gate = []

        def evac_gate(j0):
            def evac(j, ps, t):
                t = S(lambda e, ps=ps: e.activation(gate[:, j0 + j, :], ps, ACT.Sigmoid), t, g3_)
                t_gate.append(t)
                return t
            return evac

        lin(win, 1024, C_IN["gate_a"], 1024, lambda k: nT[:, k, NM:T], SEQ, t_n, evac_gate(0))
        lin(win, 1024, C_IN["gate_b"], 1024, lambda k: nT[:, k, NM:T], SEQ, t_n, evac_gate(8))
        t_mg = [None] * 8

        def evac_a(j, ps, t):
            t_mg[j] = V(lambda e, ps=ps: e.tensor_tensor(mg[:, j, :], ps, gate[:, j, :], ALU.mult), t, t_gate, g3_)
            return t_mg[j]

        def evac_b(j, ps, t):
            t1 = V(lambda e, ps=ps: e.tensor_tensor(gate[:, 8 + j, :], ps, gate[:, 8 + j, :], ALU.mult), t, t_gate)
            t_mg[j] = G(lambda e: e.tensor_tensor(mg[:, j, :], mg[:, j, :], gate[:, 8 + j, :], ALU.add), t1, t_mg[j])
            return t1

        lin(A["w_branch_gdn"][0], 1024, 0, 1024, lambda k: yg[:, k, 0:SEQ], SEQ, t_y, evac_a)
        lin(A["w_branch_dsa"][0], 1024, 0, 1024, lambda k: yd[:, k, :], SEQ, t_yd, evac_b)

        def keep(dst, ts, guard):
            def evac(j, ps, t):
                if j % 2:
                    t = V(lambda e, ps=ps: e.tensor_copy(dst[:, j, :], ps), t, guard)
                else:
                    t = S(lambda e, ps=ps: e.copy(dst[:, j, :], ps), t, guard)
                ts.append(t)
                return t
            return evac

        mix, t_mix = yg, []
        lin(A["w_out"][0], 1024, 0, 1024, lambda k: mg[:, k, :], SEQ, list(t_mg), keep(gv[:, :, 0:SEQ], t_mix, g3_))
        top[0] = 0
        x2 = carve(8, SEQ)
        n2 = nT[:, :, 0:SEQ]
        top[0] = m_att
        t_x2 = rms_scaled(gv[:, :, 0:SEQ], SEQ, "post_mix_norm", 0, x2, hT[:, :, NM:T], t_mix)
        top[0] = m_att
        t_n2 = rms_scaled(x2, SEQ, "pre_mlp_norm", 0, n2, None, t_x2)
        g4 = everyone()
        top[0] = top_in
        u_ = carve(32, SEQ)
        t_u = []

        def evac_u(j, ps, t):
            t1 = S(lambda e, ps=ps: e.activation(u_[:, j, :], ps, ACT.Relu), t, g4)
            t_u.append(G(lambda e: e.tensor_tensor(u_[:, j, :], u_[:, j, :], u_[:, j, :], ALU.mult), t1))
            return t1

        lin(A["w_up"][0], 1024, 0, 4096, lambda k: n2[:, k, :], SEQ, t_n2, evac_u)
        dn, t_dn = carve(8, SEQ), []
        lin(A["w_down"][0], 4096, 0, 1024, lambda k: u_[:, k, :], SEQ, t_u, keep(dn, t_dn, g4))
        t_x3 = rms_scaled(dn, SEQ, "post_mlp_norm", 0, x2, x2, t_dn)
        if dbg is not None and "x3" in dbg:
            SP.quiet(lambda e: e.dma_start(dbg["x3"], x2).then_inc(s_out, 16), t_x3)

        g5 = everyone()
        top[0] = top_in
        xm = carve(8, SEQ)
        mix2 = carve(8, SEQ)
        m_moe = top[0]
        memT = carve(8, SEQ)
        qm = carve(2, SEQ)
        km = carve(2, SEQ)
        vm = carve(2, 256)
        kx = carve(6, SEQ)
        vx = carve(2, 768)
        qx = carve(6, SEQ)
        cos2, sin2 = carve(SEQ), carve(SEQ)
        rtmp2 = Pool([carve(SEQ) for _ in range(3)])
        m_b2 = top[0]
        memin = carve(2, 1024)
        t_mem = load_in(6, memin, A["mem_2"][0].rearrange("(a p) d -> p a d", p=P), g5)
        t_memT = []
        for k in range(8):
            bi, ps, free = PS.take()
            PE.wait(t_mem, free)
            for a in range(2):
                t = PE(lambda e, ps=ps, a=a, k=k: e.transpose(ps[:, a * P:(a + 1) * P], memin[:, a, k * P:(k + 1) * P], ident))
            t = S(lambda e, ps=ps, k=k: e.copy(memT[:, k, :], ps[:, 0:SEQ]), t, g5)
            PS.give(bi, t)
            t_memT.append(t)
        ang, kf = carve(SEQ), carve(SEQ)
        ki = posi
        two_pi = 2 * np.pi
        t = V(lambda e: e.tensor_copy(ang, posi[:, :]), t_pos, g5)
        t = V(lambda e: e.tensor_scalar(ang, ang, cc("inv2"), None, ALU.mult), t)
        for big in (4096.0, 1.0):
            rest = two_pi * big
            parts = []
            for bits in (8, 8):
                sc = 2.0 ** (bits - 1 - np.floor(np.log2(rest)))
                p_ = float(np.floor(rest * sc) / sc)
                parts.append(p_)
                rest -= p_
            parts += [float(np.float32(rest))]
            t = V(lambda e, big=big: e.tensor_scalar(kf, ang, float(1.0 / (two_pi * big)), None, ALU.mult), t)
            t = V(lambda e: e.tensor_copy(ki[:, :], kf), t)
            t = V(lambda e: e.tensor_copy(kf, ki[:, :]), t)
            for p_ in parts:
                t = V(lambda e, p_=p_: e.scalar_tensor_tensor(out=ang, in0=kf, scalar=-p_, in1=ang, op0=ALU.mult, op1=ALU.add), t)
        for cmp_, sgn in ((ALU.is_gt, -two_pi), (ALU.is_lt, two_pi)):
            lim = float(np.pi) if sgn < 0 else -float(np.pi)
            t = V(lambda e, cmp_=cmp_, lim=lim, sgn=sgn: e.tensor_scalar(kf, ang, lim, float(sgn), cmp_, ALU.mult), t)
            t = V(lambda e: e.tensor_tensor(ang, ang, kf, ALU.add), t)
        t = V(lambda e: e.tensor_scalar(ang, ang, 3.1415925, -3.1415925, ALU.min, ALU.max), t)
        t_s2 = S(lambda e: e.activation(sin2, ang, ACT.Sin), t)
        t = S(lambda e: e.activation(kf, ang, ACT.Sin, scale=0.5), t)
        t = V(lambda e: e.tensor_tensor(kf, kf, kf, ALU.mult), t)
        t_rot = [t_s2, V(lambda e: e.tensor_scalar(cos2, kf, -2.0, 1.0, ALU.mult, ALU.add), t)]
        top[0] = m_b2
        alpha = float(4 ** 0.25)
        xcur, t_xc = x2, t_x3

        def mem_kv(layer):
            w = A["w_mem_kv_2"][layer]
            slot, view, tw = stream([(lambda v: v, w.rearrange("(k p) n -> p k n", p=P))], (8, 512))
            tk, tv = [], []
            for j in range(2):
                bi, ps, t = lin_tok(lambda k: memT[:, k, :], SEQ, lambda k, j=j: view[:, k, j * P:(j + 1) * P], 8, tw, t_memT, P)
                t = S(lambda e, ps=ps, j=j: e.copy(km[:, j, :], ps), t, g_l)
                PS.give(bi, t)
                tk.append(t)
            for c in range(2):
                bi, ps, t = lin_tok(lambda k: view[:, k, 256:512], 256, lambda k, c=c: memT[:, k, c * P:(c + 1) * P], 8, tw, t_memT, P)
                t2 = V(lambda e, ps=ps, c=c: e.tensor_copy(vm[:, c, :], ps), t, g_l)
                PS.give(bi, t2)
                tv.append(t2)
            W.give(slot, t)
            return tk + tv

        def layer_norm(src, gname, bname, li, dst, t_src):
            m = top[0]
            mu, r, sq = carve(SEQ), carve(SEQ), carve(8, SEQ)
            top[0] = m
            guard = everyone()
            bi, ps, free = PS.take()
            PE.wait(t_src, free)
            for k in range(8):
                t = PE(lambda e, k=k, ps=ps: e.matmul(ps[:, 0:SEQ], ones, src[:, k, :], start=(k == 0), stop=(k == 7)))
            t = S(lambda e, ps=ps: e.activation(mu, ps[:, 0:SEQ], ACT.Copy, scale=1.0 / 1024), t, guard)
            PS.give(bi, t)
            tsq = []
            for k in range(8):
                tc_ = V(lambda e, k=k: e.tensor_tensor(src[:, k, :], src[:, k, :], mu, ALU.subtract), t, t_src)
                tsq.append(S(lambda e, k=k: e.activation(sq[:, k, :], src[:, k, :], ACT.Square), tc_))
            t = inv_rms(lambda k: sq[:, k, :], 8, SEQ, 1.0 / 1024, eps5, r, tsq)
            res = []
            for k in range(8):
                t1 = V(lambda e, k=k: e.scalar_tensor_tensor(out=src[:, k, :], in0=src[:, k, :], scalar=vcol(gname, 8 * li + k), in1=r, op0=ALU.mult, op1=ALU.mult), t)
                res.append(S(lambda e, k=k: e.activation(dst[:, k, :], src[:, k, :], ACT.Identity, bias=vcol(bname, 8 * li + k)), t1, guard))
            return res

        def add_alpha(base, dst, ts, guard):
            def evac(j, ps, t):
                t = V(lambda e, ps=ps: e.scalar_tensor_tensor(out=dst[:, j, :], in0=base[:, j, :], scalar=alpha, in1=ps, op0=ALU.mult, op1=ALU.add), t, guard)
                ts.append(t)
                return t
            return evac

        def memory_units(t_q):
            return [dict(q=qm[64 * (h % 2):64 * (h % 2) + 64, h // 2, :], k=km[64 * (h % 2):64 * (h % 2) + 64, h // 2, :],
                         v=lambda j, h=h: vm[:, j, 64 * h:64 * h + 64], bias=None, nk=lambda qt: SEQ, hd=64, p0=64 * (h % 2),
                         out=mix2[64 * (h % 2):64 * (h % 2) + 64, 6 + h // 2, :], t=t_q) for h in range(4)]

        segs2 = [(0, P), (P, P)]

        def scaled(dst, ts, guard, j0=0):
            def evac(j, ps, t):
                t = S(lambda e, ps=ps: e.activation(dst[:, j - j0, :], ps, ACT.Copy, scale=0.125), t, guard)
                ts.append(t)
                return t
            return evac

        for layer in range(2):
            g_l = everyone()
            t_mkv = mem_kv(layer)
            if layer == 0:
                wa = A["w_in_a_2"][0]
                uc = carve(6, SEQ)
                zp = carve(6, SEQ + 2)
                t_zp = G(lambda e: e.memset(zp[:, :, 0:2], 0.0), g_l)
                tc_, tz_, tm_ = [], [], []
                lin(wa, 1024, 768, 768, lambda k: xcur[:, k, :], SEQ, t_xc, keep(uc, tc_, g_l))

                def evac_h(j, ps, t):
                    t = V(lambda e, ps=ps: e.tensor_tensor(zp[:, j, 2:2 + SEQ], ps, uc[:, j, :], ALU.mult), t, tc_[j], g_l)
                    tz = V(lambda e: e.tensor_scalar(uc[:, j, :], zp[:, j, 0:SEQ], vcol("conv_a_2", j), None, ALU.mult), t, t_zp)
                    for u in (1, 2):
                        tz = V(lambda e, u=u: e.scalar_tensor_tensor(out=uc[:, j, :], in0=zp[:, j, u:u + SEQ], scalar=vcol("conv_a_2", 6 * u + j), in1=uc[:, j, :], op0=ALU.mult, op1=ALU.add), tz)
                    tz_.append(tz)
                    return t

                lin(wa, 1024, 1536, 768, lambda k: xcur[:, k, :], SEQ, t_xc, evac_h)

                def evac_bb(j, ps, t):
                    t = V(lambda e, ps=ps: e.tensor_tensor(mix2[:, j, :], ps, uc[:, j, :], ALU.mult), t, tz_[j], g_l)
                    tm_.append(t)
                    return t

                t_qm = []
                lin(wa, 1024, 2304, 256, lambda k: xcur[:, k, :], SEQ, t_xc, scaled(qm, t_qm, g_l))
                lin(wa, 1024, 0, 768, lambda k: xcur[:, k, :], SEQ, t_xc, evac_bb)
                t_mix2 = tm_ + attention(memory_units(t_qm + t_mkv), segs2, g_l)
            else:
                raw = []
                t_qm = []
                wq = A["w_q_b_2"][0]
                lin(wq, 1024, 0, 768, lambda k: xcur[:, k, :], SEQ, t_xc, keep(qx, raw, g_l))
                lin(wq, 1024, 768, 256, lambda k: xcur[:, k, :], SEQ, t_xc, scaled(qm, t_qm, g_l))
                t_qx = [rope(qx[:, j, :], qx[:, j, :], cc("R16"), cos2, sin2, [raw[j], t_rot], g_l, rtmp2, 0.125) for j in range(6)]
                units = [dict(q=qx[64 * (h % 2):64 * (h % 2) + 64, h // 2, :], k=kx[64 * (h % 2):64 * (h % 2) + 64, h // 2, :],
                              v=lambda j, h=h: vx[:, j, 64 * h:64 * h + 64], bias=lambda qt: cc("CB", P, 2 * P) if qt == 0 else cc("CB"),
                              nk=lambda qt: P * (qt + 1), hd=64, p0=64 * (h % 2),
                              out=mix2[64 * (h % 2):64 * (h % 2) + 64, h // 2, :], t=[t_qx[h // 2], t_kx, t_vx]) for h in range(12)]
                t_mix2 = attention(memory_units(t_qm + t_mkv) + units, segs2, g_l)
            t_s = []
            lin(A["w_o_2"][layer], 1024, 0, 1024, lambda k: mix2[:, k, :], SEQ, t_mix2, add_alpha(xcur, xm, t_s, g_l))
            top[0] = m_b2
            t_xc = layer_norm(xm, "ln1_g_2", "ln1_b_2", layer, xcur, t_s)
            if dbg is not None and f"l{layer}a" in dbg:
                SP.quiet(lambda e, layer=layer: e.dma_start(dbg[f"l{layer}a"], xcur).then_inc(s_out, 16), t_xc)
            g_f = everyone()
            if layer == 0:
                gg = carve(22, SEQ)
                t_gg = [None] * 22

                def swiglu_up(wgu, gg, t_gg, guard, base=0):
                    def evac_g(j, ps, t):
                        t_gg[j] = S(lambda e, ps=ps: e.activation(gg[:, j, :], ps, ACT.Silu), t, guard)
                        return t_gg[j]

                    def evac_u2(j, ps, t):
                        t_gg[j] = V(lambda e, ps=ps: e.tensor_tensor(gg[:, j, :], gg[:, j, :], ps, ALU.mult), t, t_gg[j])
                        return t_gg[j]

                    lin(wgu, 1024, 0, 2816, lambda k: xcur[:, k, :], SEQ, t_xc, evac_g)
                    lin(wgu, 1024, 2816, 2816, lambda k: xcur[:, k, :], SEQ, t_xc, evac_u2)

                swiglu_up(A["w_gu_dense_2"][0], gg, t_gg, g_f)
                t_s = []
                lin(A["w_down_dense_2"][0], 2816, 0, 1024, lambda k: gg[:, k, :], SEQ, list(t_gg), add_alpha(xcur, xm, t_s, g_f))
                top[0] = m_b2
                t_xc = layer_norm(xm, "ln2_g_2", "ln2_b_2", layer, xcur, t_s)
                if dbg is not None and "l0" in dbg:
                    SP.quiet(lambda e: e.dma_start(dbg["l0"], xcur).then_inc(s_out, 16), t_xc)
                g_k = everyone()
                raw, t_vx = [], []
                wkv = A["w_kv_shared_2"]
                lin(wkv, 1024, 0, 768, lambda k: xcur[:, k, :], SEQ, t_xc, keep(kx, raw, g_k))
                t_kx = [rope(kx[:, j, :], kx[:, j, :], cc("R16"), cos2, sin2, [raw[j], t_rot], g_k, rtmp2) for j in range(6)]
                for c0, nn in ((0, 512), (512, 256)):
                    slot, view, tw = stream([(lambda v: v, wkv[:, 768 + c0:768 + c0 + nn].rearrange("(k p) n -> p k n", p=P))], (8, nn))
                    for c in range(2):
                        bi, ps, t = lin_tok(lambda k: view[:, k, :], nn, lambda k, c=c: xcur[:, k, c * P:(c + 1) * P], 8, tw, t_xc, P)
                        t2 = V(lambda e, ps=ps, c=c, c0=c0, nn=nn: e.tensor_copy(vx[:, c, c0:c0 + nn], ps), t, g_k)
                        PS.give(bi, t2)
                        t_vx.append(t2)
                    W.give(slot, t)

        g_m = everyone()
        top[0] = m_moe
        acc = carve(8, SEQ)
        xt = carve(2, 1024)
        wr = carve(8, 8)
        t_wr = load_in(7, wr, A["w_router_2"][0].rearrange("(k p) n -> p k n", p=P), g_m)
        lg, m8b, gt2, oh = carve(2, 8), carve(2, 8), carve(2, 8), carve(2, 2, 8)
        ix = sb("ix", [P, 2, 8], U32)
        flag = sb("flag", [P, 1], I32)
        ixf, sel, ge, posm, cnt = carve(2, 8), carve(2, 8), carve(2, 8), carve(2, 8), carve(8)
        t_sel, t_ge = [], []
        for c in range(2):
            bi, ps, t = lin_tok(lambda k: wr[:, k, :], 8, lambda k, c=c: xcur[:, k, c * P:(c + 1) * P], 8, t_wr, t_xc, P)
            t = V(lambda e, ps=ps, c=c: e.tensor_copy(lg[:, c, :], ps), t, g_m)
            PS.give(bi, t)
            t = V(lambda e, c=c: e.max(m8b[:, c, :], lg[:, c, :]), t)
            t2 = V(lambda e, c=c: e.max_index(ix[:, c, :], m8b[:, c, :], lg[:, c, :]), t)
            t2 = V(lambda e, c=c: e.tensor_copy(ixf[:, c, :], ix[:, c, :]), t2)
            g_ = gt2[:, c, :]
            t = V(lambda e, c=c, g_=g_: e.tensor_tensor(g_[:, 2:3], m8b[:, c, 1:2], m8b[:, c, 0:1], ALU.subtract), t)
            t = S(lambda e, g_=g_: e.activation(g_[:, 3:4], g_[:, 2:3], ACT.Exp), t)
            t = V(lambda e, g_=g_: e.tensor_scalar(g_[:, 4:5], g_[:, 3:4], 1.0, None, ALU.add), t)
            t = V(lambda e, g_=g_: e.reciprocal(g_[:, 0:1], g_[:, 4:5]), t)
            t = V(lambda e, g_=g_: e.tensor_tensor(g_[:, 1:2], g_[:, 3:4], g_[:, 0:1], ALU.mult), t)
            for r in range(2):
                t3 = V(lambda e, c=c, r=r: e.tensor_scalar(oh[:, c, r, :], cc("iota8"), ixf[:, c, r:r + 1], None, ALU.is_equal), t2)
            t_sel.append(V(lambda e, c=c: e.tensor_tensor(sel[:, c, :], oh[:, c, 0, :], oh[:, c, 1, :], ALU.add), t3))
            t = V(lambda e, c=c, g_=g_: e.tensor_scalar(ge[:, c, :], oh[:, c, 0, :], g_[:, 0:1], None, ALU.mult), t, t3)
            t_ge.append(V(lambda e, c=c, g_=g_: e.scalar_tensor_tensor(out=ge[:, c, :], in0=oh[:, c, 1, :], scalar=g_[:, 1:2], in1=ge[:, c, :], op0=ALU.mult, op1=ALU.add), t))
        t_xt = []
        for c in range(2):
            for hf in range(2):
                bi, ps, free = PS.take()
                PE.wait(free, t_xc)
                for k in range(4):
                    t = PE(lambda e, ps=ps, k=k, hf=hf, c=c: e.transpose(ps[:, k * P:(k + 1) * P], xcur[:, 4 * hf + k, c * P:(c + 1) * P], ident))
                t = S(lambda e, ps=ps, c=c, hf=hf: e.copy(xt[:, c, 512 * hf:512 * hf + 512], ps), t, g_m)
                PS.give(bi, t)
                t_xt.append(t)
        t_pos = []
        for c in range(2):
            bi, ps, free = PS.take()
            t = mm1(ps[:, 0:8], cc("U"), sel[:, c, :], t_sel, free, stop=(c == 0))
            if c == 1:
                t = mm1(ps[:, 0:8], ones, sel[:, 0, :], start=False)
            t = V(lambda e, ps=ps, c=c: e.tensor_tensor(posm[:, c, :], ps[:, 0:8], sel[:, c, :], ALU.mult), t)
            PS.give(bi, t)
            t_pos.append(V(lambda e, c=c: e.tensor_scalar(posm[:, c, :], posm[:, c, :], -1.0, None, ALU.add), t))
        bi, ps, free = PS.take()
        mm1(ps[:, 0:8], ones, sel[:, 0, :], free, stop=False)
        t = mm1(ps[:, 0:8], ones, sel[:, 1, :], start=False)
        t = V(lambda e, ps=ps: e.tensor_reduce(cnt[:, 0:1], ps[:, 0:8], AX, ALU.max), t)
        PS.give(bi, t)
        t = V(lambda e: e.tensor_scalar(cnt[:, 1:2], cnt[:, 0:1], float(P), None, ALU.is_gt), t)
        t_flag = V(lambda e: e.tensor_copy(flag[:, :], cnt[:, 1:2]), t)

        Pm = Pool([carve(2, P) for _ in range(2)])
        GP = Pool([carve(2, P) for _ in range(2)])
        GPT = Pool([carve(SEQ) for _ in range(2)])
        XS = Pool([carve(8, P) for _ in range(2)])
        YE = Pool([carve(1024) for _ in range(2)])
        gg = carve(22, P)

        def pick(q, base, t_start):
            pi, pm, pfree = Pm.take()
            gi, gp, gfree = GP.take()
            for c in range(2):
                t1 = V(lambda e, c=c: e.tensor_scalar(pm[:, c, :], cc("iota", base, base + P), posm[:, c, q:q + 1], None, ALU.is_equal), t_pos, pfree, g_m, t_start)
                t2 = V(lambda e, c=c: e.tensor_scalar(gp[:, c, :], cc("iota", base, base + P), posm[:, c, q:q + 1], ge[:, c, q:q + 1], ALU.is_equal, ALU.mult), t_pos, t_ge, gfree, g_m)
            xi, xs, xfree = XS.take()
            ts = []
            for hf in range(2):
                bi, ps, free = PS.take()
                PE.wait(free, t1, t_xt)
                for k in range(4):
                    kk = 4 * hf + k
                    for c in range(2):
                        t = mm1(ps[:, k * P:(k + 1) * P], xt[:, c, kk * P:(kk + 1) * P], pm[:, c, :], start=(c == 0), stop=(c == 1))
                tx = S(lambda e, ps=ps, hf=hf: e.copy(xs[:, 4 * hf:4 * hf + 4, :].rearrange("p a b -> p (a b)"), ps), t, xfree, g_m)
                PS.give(bi, tx)
                ts.append(tx)
            Pm.give(pi, t)
            ti, gt, tfree = GPT.take()
            bi, ps, free = PS.take()
            PE.wait(free, t2)
            for c in range(2):
                t = PE(lambda e, ps=ps, c=c: e.transpose(ps[:, c * P:(c + 1) * P], gp[:, c, :], ident))
            GP.give(gi, t)
            tg = S(lambda e, ps=ps: e.copy(gt, ps[:, 0:SEQ]), t, tfree, g_m)
            PS.give(bi, tg)
            return (xi, xs, ts, ti, gt, tg)

        def expert_up(q, picked):
            xi, xs, ts, ti, gt, tg = picked
            t_gg = [None] * 22
            guard = [PE.last()]

            def evac_g(j, ps, t):
                t_gg[j] = S(lambda e: e.activation(gg[:, j, :], ps, ACT.Silu), t, guard, g_m)
                return t_gg[j]

            def evac_u2(j, ps, t):
                t_gg[j] = V(lambda e: e.tensor_tensor(gg[:, j, :], gg[:, j, :], ps, ALU.mult), t, t_gg[j])
                return t_gg[j]

            w = A["w_gu_moe_2"][0, q]
            lin(w, 1024, 0, 2816, lambda k: xs[:, k, :], P, ts, evac_g)
            lin(w, 1024, 2816, 2816, lambda k: xs[:, k, :], P, ts, evac_u2)
            XS.give(xi, PE.last())
            return t_gg

        def expert_down(q, t_gg):
            w = A["w_down_moe_2"][0, q]
            b = [PS.take() for _ in range(2)]
            for f0 in range(0, 22, 4):
                nk = min(4, 22 - f0)
                slot, view, tw = stream([(lambda v: v, w[f0 * P:(f0 + nk) * P, :].rearrange("(k p) n -> p k n", p=P))], (nk, 1024))
                for hf in range(2):
                    bi, ps, free = b[hf]
                    PE.wait(tw, free, t_gg)
                    for k in range(nk):
                        t = PE(lambda e, ps=ps, view=view, k=k, hf=hf, f=f0 + k: e.matmul(ps, gg[:, f, :], view[:, k, 512 * hf:512 * hf + 512], start=(f == 0), stop=(f == 21)))
                W.give(slot, t)
            yi, ye, yfree = YE.take()
            ts = []
            for hf in range(2):
                bi, ps, free = b[hf]
                if hf:
                    ts.append(V(lambda e, ps=ps: e.tensor_copy(ye[:, 512:1024], ps), t, yfree, g_m))
                else:
                    ts.append(S(lambda e, ps=ps: e.copy(ye[:, 0:512], ps), t, yfree, g_m))
                PS.give(bi, ts[-1])
            return yi, ye, ts

        t_acc = [None] * 4

        def spread(q, first, picked, made):
            xi, xs, _, ti, gt, tg = picked
            yi, ye, ts = made
            for h2 in range(4):
                bi, ps, free = PS.take()
                PE.wait(free, ts, tg)
                for k in range(2):
                    kk = 2 * h2 + k
                    t = mm1(ps[:, k * SEQ:(k + 1) * SEQ], ye[:, kk * P:(kk + 1) * P], gt)
                av_ = acc[:, 2 * h2:2 * h2 + 2, :].rearrange("p a b -> p (a b)")
                if first:
                    t_acc[h2] = V(lambda e, ps=ps, av_=av_: e.tensor_copy(av_, ps), t, g_m)
                else:
                    t_acc[h2] = V(lambda e, ps=ps, av_=av_: e.tensor_tensor(av_, av_, ps, ALU.add), t, t_acc[h2])
                PS.give(bi, t_acc[h2])
            YE.give(yi, t)
            GPT.give(ti, t)

        def all_experts(base, first, t_start):
            nxt = pick(0, base, t_start)
            prev = None
            for q in range(8):
                cur_ = nxt
                t_gg = expert_up(q, cur_)
                if prev is not None:
                    spread(q - 1, first and q == 1, *prev)
                if q < 7:
                    nxt = pick(q + 1, base, None)
                made = expert_down(q, t_gg)
                prev = (cur_, made)
            spread(7, False, *prev)

        all_experts(0, True, None)

        main_slots = (list(s_slot), list(n_slot))
        queues = (PE, V, S, G, SP)
        before = everyone()
        for q_, s_ in zip(queues, (sem("x_pe"), sem("x_dve"), sem("x_act"), sem("x_pool"), None)):
            q_.enter(s_)
            q_.wait(before)
        s_slot[:] = [sem(f"x_slot{i}") for i in range(NSLOT)]
        n_slot[:] = [0] * NSLOT
        pools = (PS, W, Pm, GP, GPT, XS, YE)
        for p_ in pools:
            p_.free = [[] for _ in p_.bufs]
        t_acc_main = list(t_acc)
        all_experts(P, False, None)
        done = everyone()
        for q_ in queues:
            q_.wait(done)
        for q_ in queues:
            q_.leave(flag[0:1, 0:1], t_flag, before)
        s_slot[:], n_slot[:] = main_slots
        for p_ in pools:
            p_.free = [[] for _ in p_.bufs]
        t_acc = [t_acc_main[j // 2] for j in range(8)]
        t_s = []
        for j in range(8):
            t_s.append(V(lambda e, j=j: e.scalar_tensor_tensor(out=xm[:, j, :], in0=xcur[:, j, :], scalar=alpha, in1=acc[:, j, :], op0=ALU.mult, op1=ALU.add), t_acc[j]))
        top[0] = m_b2
        t_xc = layer_norm(xm, "ln2_g_2", "ln2_b_2", 1, xcur, t_s)

        g_o = everyone()
        fin = carve(2, 1024)
        for c in range(2):
            tf = []
            for hf in range(2):
                bi, ps, free = PS.take()
                PE.wait(free, t_xc)
                for k in range(4):
                    t = PE(lambda e, ps=ps, k=k, hf=hf, c=c: e.transpose(ps[:, k * P:(k + 1) * P], xcur[:, 4 * hf + k, c * P:(c + 1) * P], ident))
                if hf:
                    t = V(lambda e, ps=ps, c=c: e.tensor_copy(fin[:, c, 512:1024], ps), t, g_o)
                else:
                    t = S(lambda e, ps=ps, c=c: e.copy(fin[:, c, 0:512], ps), t, g_o)
                PS.give(bi, t)
                tf.append(t)
            SP.quiet(lambda e, c=c: e.dma_start(out[0, c * P:(c + 1) * P, :], fin[:, c, :]).then_inc(s_out, 16), tf)
        n_out = 16 * (2 + (len(dbg) if dbg is not None else 0))
        SP.quiet(lambda e: e.wait_ge(s_out, n_out))

        block = ctx.enter_context(nc.Block())

        @block.sync
        def _(e):
            SP.play(e)

        @block.tensor
        def _(e):
            PE.play(e)

        @block.vector
        def _(e):
            V.play(e)

        @block.scalar
        def _(e):
            S.play(e)

        @block.gpsimd
        def _(e):
            G.play(e)


INS = ["x", "meta_tokens", "pre_mix_norm", "w_in", "conv_w", "a_log", "dt_bias", "gdn_norm", "w_branch_gdn",
       "w_branch_dsa", "w_out", "post_mix_norm", "pre_mlp_norm", "w_up", "w_down", "post_mlp_norm", "mem_2",
       "positions_2", "w_in_a_2", "conv_a_2", "w_q_b_2", "w_kv_shared_2", "w_mem_kv_2", "w_o_2", "ln1_g_2",
       "ln1_b_2", "ln2_g_2", "ln2_b_2", "w_gu_dense_2", "w_down_dense_2", "w_router_2", "w_gu_moe_2",
       "w_down_moe_2"]


def kernel(**inputs):
    from concourse import bacc
    from concourse.bass_utils import run_bass_kernel_spmd

    nc = bacc.Bacc("TRN2", target_bir_lowering=False, num_devices=1)
    arrays, aps = {}, {}
    for name in INS:
        a = np.ascontiguousarray(inputs[name])
        arrays[f"in_{name}"] = a
        aps[name] = nc.dram_tensor(f"in_{name}", a.shape, mybir.dt.from_np(a.dtype), kind="ExternalInput").ap()
    table = np.ascontiguousarray(np.concatenate(list(shape_constants().values()), axis=1))
    arrays["in_table"] = table
    cst = nc.dram_tensor("in_table", table.shape, F32, kind="ExternalInput").ap()
    out = nc.dram_tensor("out_0", (1, SEQ, 1024), F32, kind="ExternalOutput").ap()
    program(nc, aps, cst, out)
    r = run_bass_kernel_spmd(nc, [arrays], core_ids=[0])
    return r.results[0]["out_0"]
```

```python
from contextlib import ExitStack

import numpy as np

import concourse.bass as bass
from concourse import mybir

F32 = mybir.dt.float32
F32R = mybir.dt.float32r
I32 = mybir.dt.int32
U32 = mybir.dt.uint32
ALU = mybir.AluOpType
ACT = mybir.ActivationFunctionType
AX = mybir.AxisListType.X

P = 128
NM = 16
SEQ = 256
T = NM + SEQ
NRAW, NHI = 6, 4
BLK = 2048
ARN = 22976
NEG = -1e30
TAKEN = -3e38

C_IN = dict(gq=0, gk=1024, gv=2048, gz=3072, gb=4096, ga=4104, aq=4112, ak=5136, av=5392,
            iq=5648, ik=6160, iw=6224, gate_a=6232, gate_b=7256)


def shape_constants():
    i = np.arange(P)
    s, c = i[:, None], i[None, :]
    f = np.float32
    out = {}
    out["ident"] = (s == c).astype(f)
    out["ones"] = np.ones((P, P), f)
    out["U"] = (s <= c).astype(f)
    out["Us"] = (s < c).astype(f)
    same = s // 16 == c // 16
    out["Ub"] = (same & (s <= c)).astype(f)
    out["Ubs"] = (same & (s < c)).astype(f)
    out["OB"] = same.astype(f)
    for b in (1, 2, 4, 8, 16, 32, 64):
        out[f"m{b}"] = ((s // (2 * b) == c // (2 * b)) & (c % (2 * b) >= b) & (s % (2 * b) < b)).astype(f)
    for name, hd, half in (("R128", 128, 64), ("R64", 64, 32), ("R16", 64, 8)):
        r = np.zeros((P, P), f)
        for m in range(P):
            if m % hd < half:
                r[m + half, m] = -1
            elif m % hd < 2 * half:
                r[m - half, m] = 1
        out[name] = r
    out["hmask"] = (s // 16 == np.arange(8)[None, :]).astype(f)
    out["Rep"] = ((s == c % 16) & (s < 16)).astype(f)
    out["CB"] = np.concatenate([np.zeros((P, P), f), np.where(c <= s, 0, NEG).astype(f)], 1)
    pos = np.arange(T, dtype=f)
    for name, dim in (("A", 128), ("I", 64)):
        inv = f(10000.0) ** (-np.arange(0, dim, 2, dtype=f) / f(dim))
        ang = pos[None, :] * inv.astype(f)[i % (dim // 2)][:, None]
        out["cos" + name] = np.cos(ang).astype(f)
        out["sin" + name] = np.sin(ang).astype(f)
    inv2 = f(500000.0) ** (-np.arange(0, 16, 2, dtype=f) / f(16))
    out["inv2"] = np.where(i % 64 < 16, inv2[i % 8], 0).astype(f)[:, None]
    out["iota"] = np.tile(np.arange(2 * P, dtype=f), (P, 1))
    out["iota8"] = np.tile(np.arange(8, dtype=f), (P, 1))
    return out


def layout():
    off, n = {}, 0
    for k, v in shape_constants().items():
        off[k] = (n, v.shape[1])
        n += v.shape[1]
    return off, n


class Queue:

    def __init__(self, name, sem):
        self.name, self.sem, self.ops, self.n, self.seen = name, sem, [], 0, {}

    def wait(self, *tokens):
        for t in tokens:
            if t is None:
                continue
            if isinstance(t, list):
                self.wait(*t)
                continue
            sem, val = t
            if self.seen.get(id(sem), 0) < val:
                self.seen[id(sem)] = val
                self.ops.append(lambda e, sem=sem, val=val: e.wait_ge(sem, val))

    def __call__(self, fn, *tokens):
        self.wait(*tokens)
        self.n += 1
        self.ops.append(lambda e, fn=fn, done=self.sem: fn(e).then_inc(done, 1))
        return (self.sem, self.n)

    def quiet(self, fn, *tokens):
        self.wait(*tokens)
        self.ops.append(fn)

    def tick(self):
        fn = self.ops.pop()
        return self(fn)

    def last(self):
        return (self.sem, self.n) if self.n else None

    def play(self, e):
        for op in self.ops:
            op(e)

    def enter(self, sem):
        self.kept = (self.ops, self.n, self.sem, self.seen)
        self.ops, self.n, self.sem, self.seen = [], 0, sem, dict(self.seen)

    def leave(self, flag, *tokens):
        body = self.ops
        self.ops, self.n, self.sem, self.seen = self.kept
        self.wait(*tokens)

        def run(e):
            with e.If(e.value_load(flag, min_val=0, max_val=1) > 0):
                for op in body:
                    op(e)

        self.ops.append(run)


class Pool:

    def __init__(self, bufs):
        self.bufs, self.free, self.i = bufs, [[] for _ in bufs], 0

    def take(self):
        i = self.i
        self.i = (i + 1) % len(self.bufs)
        return i, self.bufs[i], self.free[i]

    def give(self, i, *tokens):
        self.free[i] = list(tokens)


class Pair:

    def __init__(self, hi, lo):
        self.hi, self.lo = hi, lo


def program(nc, A, cst, out, dbg=None):
    off, ncst = layout()
    ctx = ExitStack()
    with ctx:
        made = {}

        def sb(name, shape, dt=F32):
            if name not in made:
                made[name] = ctx.enter_context(nc.sbuf_tensor(name, shape, dt))
            return made[name]

        def sem(name):
            if name not in made:
                made[name] = ctx.enter_context(nc.semaphore(name))
            return made[name]

        arena = sb("arena", [P, ARN])
        ring = sb("ring", [P, NRAW * BLK])
        ring_r = nc.alloc_sbuf_tensor_at("ring_r", [P, NRAW * BLK], F32R, offset=nc.lookup_mloc("ring").addr)
        arena_r = nc.alloc_sbuf_tensor_at("arena_r", [P, ARN], F32R, offset=nc.lookup_mloc("arena").addr)
        C = sb("consts", [P, ncst])
        vec = sb("vec", [P, 224])
        sm = sb("sm", [P, 512])
        bank = [ctx.enter_context(nc.psum_tensor(f"bank{i}", [P, 512], F32)) for i in range(8)]
        _, plan = emit(nc, A, cst, out, dbg, sb, sem, arena, arena_r, ring, ring_r, C, vec, sm, bank, off, None)
        (PE, V, S, G, SP), _ = emit(nc, A, cst, out, dbg, sb, sem, arena, arena_r, ring, ring_r, C, vec, sm, bank, off, plan)

        block = ctx.enter_context(nc.Block())

        @block.sync
        def _(e):
            SP.play(e)

        @block.tensor
        def _(e):
            PE.play(e)

        @block.vector
        def _(e):
            V.play(e)

        @block.scalar
        def _(e):
            S.play(e)

        @block.gpsimd
        def _(e):
            G.play(e)


def emit(nc, A, cst, out, dbg, sb, sem, arena, arena_r, ring, ring_r, C, vec, sm, bank, off, plan):
    if True:
        def cc(name, a=0, b=None):
            o, n = off[name]
            return C[:, o + a:o + (n if b is None else b)]

        PE = Queue("PE", sem("s_pe"))
        V = Queue("V", sem("s_dve"))
        S = Queue("S", sem("s_act"))
        G = Queue("G", sem("s_pool"))
        SP = Queue("SP", None)
        s_slot = [sem(f"s_slot{i}") for i in range(NRAW)]
        n_slot = [0] * NRAW
        s_in = [sem(f"s_in{i}") for i in range(9)]
        n_in = [0] * 9
        s_out = sem("s_out")
        PS = Pool([b[:, :] for b in bank])
        RAW = Pool(list(range(NRAW)))
        HI = Pool(list(range(NHI)))

        top = [0]

        def shaped(a, dims):
            if len(dims) == 2:
                return a.rearrange("p (a b) -> p a b", a=dims[0])
            if len(dims) == 3:
                return a.rearrange("p (a b c) -> p a b c", a=dims[0], b=dims[1])
            return a

        def carve(*dims, of=arena):
            n = int(np.prod(dims))
            a = of[:, top[0]:top[0] + n]
            top[0] += n
            assert top[0] <= ARN, top[0]
            return shaped(a, dims)

        def carve_pair(*dims):
            return Pair(carve(*dims, of=arena_r), carve(*dims, of=arena_r))

        hi_ring = sb("hi_ring", [P, NHI * BLK], F32R)
        XH = sb("XH", [P, 8, T], F32R)
        XL = sb("XL", [P, 8, T], F32R)
        nX = Pair(XH[:, :, :], XL[:, :, :])
        X = Pair(XH[:, :, 0:SEQ], XL[:, :, 0:SEQ])

        smtop = [0]

        def small(n):
            a = sm[:, smtop[0]:smtop[0] + n]
            smtop[0] += n
            assert smtop[0] <= 512
            return a

        def everyone():
            return [q.last() for q in (PE, V, S, G)]

        def load_in(which, dst, src, *tokens):
            n_in[which] += 16
            SP.quiet(lambda e: e.dma_start(dst, src).then_inc(s_in[which], 16), *tokens)
            return (s_in[which], n_in[which])

        W = dict(rec=[[]], seg=0, at=0, dma=[], cut=[])

        def block_load(i):
            parts, (k, n) = W["list"][i]
            ri, _, free = RAW.take()
            a = ri * BLK
            block = shaped(ring[:, a:a + k * n], (k, n))
            for pick, src in parts:
                n_slot[ri] += 16
                SP.quiet(lambda e, d=pick(block), s=src, done=s_slot[ri]: e.dma_start(d, s).then_inc(done, 16), *free)
            W["dma"].append((ri, (s_slot[ri], n_slot[ri])))

        def block_split(i):
            _, (k, n) = W["list"][i]
            ri, t = W["dma"][i]
            hi_, _, free = HI.take()
            a, b = ri * BLK, hi_ * BLK
            m = k * n
            t1 = S(lambda e: e.copy(hi_ring[:, b:b + m], ring[:, a:a + m]), t, *free)
            t2 = V(lambda e: e.tensor_tensor(ring_r[:, a:a + m], ring[:, a:a + m], hi_ring[:, b:b + m].bitcast(F32), ALU.subtract), t1)
            W["cut"].append((ri, hi_, Pair(shaped(hi_ring[:, b:b + m], (k, n)), shaped(ring_r[:, a:a + m], (k, n))), [t1, t2]))

        def stream(parts, shape):
            i = W["at"]
            W["at"] += 1
            rec = W["rec"][W["seg"]]
            rec.append((parts, shape))
            W["list"] = plan[W["seg"]] if plan is not None else rec
            while len(W["dma"]) < min(len(W["list"]), i + (NRAW if plan is not None else 1)):
                block_load(len(W["dma"]))
            while len(W["cut"]) < min(len(W["list"]), i + 3):
                block_split(len(W["cut"]))
            ri, hi_, pair, ts = W["cut"][i]
            return (ri, hi_), pair, ts

        def release(slots, t):
            RAW.give(slots[0], t)
            HI.give(slots[1], t)

        def new_segment():
            W["rec"].append([])
            W.update(seg=W["seg"] + 1, at=0, dma=[], cut=[])

        def mm3(ps, a, b, first, last):
            PE.quiet(lambda e: e.matmul(ps, a[0], b[0], start=first, stop=False))
            PE.quiet(lambda e: e.matmul(ps, a[0], b[1], start=False, stop=False))
            f = lambda e: e.matmul(ps, a[1], b[0], start=False, stop=last)
            if last:
                return PE(f)
            PE.quiet(f)

        def source(w, k0, nk, c0, gw):
            return w[k0 * P:(k0 + nk) * P, c0:c0 + gw].rearrange("(k p) n -> p k n", p=P)

        def whole(v):
            return v

        def lin_block(parts, gw, x, x0, n, t_x, evac, j0=0):
            slots, w, tw = stream(parts, (8, gw))
            for mi in range(gw // P):
                bi, ps, free = PS.take()
                PE.wait(tw, t_x, free)
                for k in range(8):
                    t = mm3(ps[:, 0:n], (w.hi[:, k, mi * P:(mi + 1) * P], w.lo[:, k, mi * P:(mi + 1) * P]),
                            (x.hi[:, k, x0:x0 + n], x.lo[:, k, x0:x0 + n]), k == 0, k == 7)
                if mi == gw // P - 1:
                    release(slots, t)
                PS.give(bi, evac(j0 + mi, ps[:, 0:n], t))

        def lin(w, K, c0, ncols, x, n, t_x, evac, x0=0, j0=0):
            KT = K // P
            for g0 in range(0, ncols, 256):
                gw = min(256, ncols - g0)
                if KT == 8:
                    lin_block([(whole, source(w, 0, 8, c0 + g0, gw))], gw, x, x0, n, t_x, evac, j0 + g0 // P)
                    continue
                banks = [PS.take() for _ in range(gw // P)]
                for kb in range(0, KT, 8):
                    nk = min(8, KT - kb)
                    slots, wp, tw = stream([(whole, source(w, kb, nk, c0 + g0, gw))], (nk, gw))
                    for mi in range(gw // P):
                        bi, ps, free = banks[mi]
                        PE.wait(tw, t_x, free)
                        for k in range(nk):
                            kk = kb + k
                            t = mm3(ps[:, 0:n], (wp.hi[:, k, mi * P:(mi + 1) * P], wp.lo[:, k, mi * P:(mi + 1) * P]),
                                    (x.hi[:, kk, x0:x0 + n], x.lo[:, kk, x0:x0 + n]), kk == 0, kk == KT - 1)
                        if kb + nk < KT and mi == gw // P - 1:
                            t = PE.tick()
                        if mi == gw // P - 1:
                            release(slots, t)
                        if kb + nk == KT:
                            PS.give(bi, evac(j0 + g0 // P + mi, ps[:, 0:n], t))

        def tok_block(w, tw, ncols, x, x0, m, t_x, last):
            bi, ps, free = PS.take()
            PE.wait(tw, t_x, free)
            for k in range(8):
                t = mm3(ps[0:m, 0:ncols], (x.hi[:, k, x0:x0 + m], x.lo[:, k, x0:x0 + m]), (w.hi[:, k, :], w.lo[:, k, :]), k == 0, k == 7)
            return bi, ps[0:m, 0:ncols], t

        def lin_tok(view, ncols, lhs, nk, t_w, t_lhs, m):
            bi, ps, free = PS.take()
            PE.wait(t_w, t_lhs, free)
            for k in range(nk):
                f = lambda e, ps=ps, k=k, a=lhs(k), b=view(k): e.matmul(ps[0:m, 0:ncols], a, b, start=(k == 0), stop=(k == nk - 1))
                if k == nk - 1:
                    t = PE(f)
                else:
                    PE.quiet(f)
            return bi, ps[0:m, 0:ncols], t

        def mm1(ps, lhsT, rhs, *tokens, start=True, stop=True):
            return PE(lambda e, ps=ps: e.matmul(ps, lhsT, rhs, start=start, stop=stop), *tokens)

        def split(src, hi, lo, *tokens):
            t1 = S(lambda e: e.copy(hi, src), *tokens)
            return V(lambda e: e.tensor_tensor(lo, src, hi.bitcast(F32), ALU.subtract), t1)

        ident = cc("ident")
        ones = cc("ones")

        top_g = top[0]
        xin = carve(2, 1024)
        min_ = carve(1024)[0:NM, :]
        rows = carve(2, P)
        t_c = load_in(0, C[:, :], cst)
        t_x = load_in(1, xin, A["x"][0].rearrange("(a p) d -> p a d", p=P))
        t_x = load_in(1, min_, A["meta_tokens"])
        vrows, nv = {}, 0
        for key in ("pre_mix_norm", "post_mix_norm", "pre_mlp_norm", "post_mlp_norm"):
            vrows[key] = nv
            t_v = load_in(2, rows[nv:nv + 8, 0, :], A[key].rearrange("l (a p) -> (l a) p", p=P))
            nv += 8
        for key in ("ln1_g_2", "ln1_b_2", "ln2_g_2", "ln2_b_2"):
            vrows[key] = nv
            t_v = load_in(2, rows[nv:nv + 16, 0, :], A[key].rearrange("l (a p) -> (l a) p", p=P))
            nv += 16
        vrows["conv_a_2"] = nv
        t_v = load_in(2, rows[nv:nv + 18, 0, :], A["conv_a_2"].rearrange("l j (a p) -> (l j a) p", p=P))
        nv += 18
        vrows["gdn_norm"] = nv
        t_v = load_in(2, rows[nv:nv + 1, 0, :], A["gdn_norm"])
        nv += 1
        t_v = load_in(2, rows[0:96, 1, :], A["conv_w"].rearrange("l j (a p) -> (l j a) p", p=P))
        vrows["conv_w"] = 128
        dtb = small(8)
        alog = small(8)
        t_g = load_in(3, dtb, A["dt_bias"].to_broadcast([P, 8]))
        t_g = load_in(3, alog, A["a_log"].to_broadcast([P, 8]))
        posi = sb("posi", [P, SEQ], I32)
        t_pos = load_in(4, posi[:, :], A["positions_2"].to_broadcast([P, SEQ]))
        win = A["w_in"][0]
        eps6, eps5, one1 = small(1), small(1), small(1)
        zero1 = small(1)
        for ap, v in ((eps6, 1e-6), (eps5, 1e-5), (one1, 1.0), (zero1, 0.0)):
            t_eps = G(lambda e, ap=ap, v=v: e.memset(ap, v))

        for j, n in ((0, nv), (1, 96)):
            bi, ps, free = PS.take()
            t = PE(lambda e, ps=ps, j=j, n=n: e.transpose(ps[:, 0:n], rows[0:n, j, :], cc("ident")[0:n, 0:n]), t_v, t_c, free)
            t_vec = V(lambda e, ps=ps, j=j, n=n: e.tensor_copy(vec[:, 128 * j:128 * j + n], ps[:, 0:n]), t)
            PS.give(bi, t_vec)

        def vcol(name, i):
            return vec[:, vrows[name] + i:vrows[name] + i + 1]

        hT = carve(8, T)
        t_h = []
        for k in range(8):
            bi, ps, free = PS.take()
            PE.wait(t_x, t_c, free)
            PE.quiet(lambda e, ps=ps, k=k: e.transpose(ps[:, 0:NM], min_[:, k * P:(k + 1) * P], cc("ident")[0:NM, 0:NM]))
            PE.quiet(lambda e, ps=ps, k=k: e.transpose(ps[:, NM:NM + P], xin[:, 0, k * P:(k + 1) * P], ident))
            t = PE(lambda e, ps=ps, k=k: e.transpose(ps[:, NM + P:T], xin[:, 1, k * P:(k + 1) * P], ident))
            q = V if k % 2 else S
            if q is V:
                t = V(lambda e, ps=ps, k=k: e.tensor_copy(hT[:, k, :], ps[:, 0:T]), t)
            else:
                t = S(lambda e, ps=ps, k=k: e.copy(hT[:, k, :], ps[:, 0:T]), t)
            PS.give(bi, t)
            t_h.append(t)

        def inv_rms(sq, K, n, scale, eps, dst, t_sq):
            bi, ps, free = PS.take()
            PE.wait(t_sq, t_c, free)
            for k in range(K):
                f = lambda e, ps=ps, k=k, b=sq(k): e.matmul(ps[:, 0:n], ones, b, start=(k == 0), stop=(k == K - 1))
                if k == K - 1:
                    t = PE(f)
                else:
                    PE.quiet(f)
            t1 = S(lambda e, ps=ps: e.activation(dst, ps[:, 0:n], ACT.Sqrt, bias=eps, scale=scale), t, t_eps)
            PS.give(bi, t1)
            return V(lambda e: e.reciprocal(dst, dst), t1)

        def rms_scaled(src, n, gname, gi, at, t_src, put):
            m = top[0]
            top[0] = at
            sq = carve(8, n)
            r = carve(n)
            tmp = carve(8, n)
            top[0] = m
            guard = everyone()
            t = S(lambda e: e.activation(sq, src, ACT.Square), t_src, guard)
            t_r = inv_rms(lambda k: sq[:, k, :], 8, n, 1.0 / 1024, eps6, r, [t, guard])
            res = []
            for k in range(8):
                t = V(lambda e, k=k: e.scalar_tensor_tensor(out=tmp[:, k, :], in0=src[:, k, :], scalar=vcol(gname, gi + k), in1=r, op0=ALU.mult, op1=ALU.mult), t_r, t_vec, guard)
                res.append(put(k, tmp[:, k, :], t))
            return res

        def into(x):
            def put(k, src, t):
                t = S(lambda e: e.copy(x.hi[:, k, :], src), t)
                return G(lambda e: e.tensor_tensor(x.lo[:, k, :], src, x.hi[:, k, :].bitcast(F32), ALU.subtract), t)
            return put

        t_n = rms_scaled(hT, T, "pre_mix_norm", 0, top[0], t_h, into(nX))
        t_in_done = everyone()

        top[0] = top_g
        gq = carve(8, T)
        g_kv = top[0]
        gk = carve(8, T)
        gv = carve(8, T)
        mark_gdn = top[0]
        xpads = [carve(T + 3) for _ in range(4)]
        sqs = [carve(T) for _ in range(3)]
        rs_ = [carve(T) for _ in range(3)]
        XP, SQ, RR = Pool(xpads), Pool(sqs), Pool(rs_)
        t_z = None
        for x in xpads:
            t_z = G(lambda e, x=x: e.memset(x[:, 0:3], 0.0), t_in_done)

        smallT = carve(2, T)
        at = small(24)
        g3 = small(24)
        b3 = small(24)
        iw = small(16)
        t_at0 = V(lambda e: e.memset(at, 0.0))
        t_b30 = V(lambda e: e.memset(b3, 0.0))
        t_sm = []

        def evac_small(j, ps, t):
            n = (16, 8)[j]
            t = V(lambda e: e.tensor_copy(smallT[0:n, j, :], ps[0:n, :]), t, t_in_done)
            t_sm.append(t)
            return t

        lin_block([(lambda v: v[:, :, 0:P], source(win, 0, 8, C_IN["gb"], P)),
                   (lambda v: v[:, :, P:2 * P], source(win, 0, 8, C_IN["iw"], P))], 256, nX, 0, T, t_n, evac_small)
        t_g3 = []
        for c, t0, n in ((0, 16, P), (1, 16 + P, P), (2, 0, NM)):
            bi, ps, free = PS.take()
            t = PE(lambda e, ps=ps, t0=t0, n=n: e.transpose(ps[0:n, 0:16], smallT[0:16, 0, t0:t0 + n], cc("ident")[0:16, 0:16]), t_sm, free)
            if c < 2:
                t = PE(lambda e, ps=ps, t0=t0, n=n: e.transpose(ps[0:n, 16:24], smallT[0:8, 1, t0:t0 + n], cc("ident")[0:8, 0:8]), t_sm)
            t = S(lambda e, ps=ps, c=c, n=n: e.activation(b3[0:n, 8 * c:8 * c + 8], ps[0:n, 0:8], ACT.Sigmoid), t, t_b30)
            ts = [t, V(lambda e, ps=ps, c=c, n=n: e.tensor_tensor(at[0:n, 8 * c:8 * c + 8], ps[0:n, 8:16], dtb[0:n, :], ALU.add), t, t_g, t_at0)]
            if c < 2:
                ts.append(V(lambda e, ps=ps, c=c: e.tensor_scalar(iw[:, 8 * c:8 * c + 8], ps[:, 16:24], float(512 ** -0.5), None, ALU.mult), t))
            PS.give(bi, *ts)
            t_g3 += ts
        t_iw = t_g3
        na, ea = small(24), small(24)
        t = V(lambda e: e.tensor_scalar(na, at, -1.0, None, ALU.mult), t_g3)
        t = V(lambda e: e.tensor_tensor(na, na, at, ALU.min), t)
        t = S(lambda e: e.activation(ea, na, ACT.Exp), t)
        t = S(lambda e: e.activation(ea, ea, ACT.Ln, bias=one1), t, t_eps)
        t_al = S(lambda e: e.activation(alog, alog, ACT.Exp), t_g)
        t = V(lambda e: e.scalar_tensor_tensor(out=g3, in0=at, scalar=0.0, in1=ea, op0=ALU.max, op1=ALU.add), t)
        for c in range(3):
            t_g3 = V(lambda e, c=c: e.scalar_tensor_tensor(out=g3[:, 8 * c:8 * c + 8], in0=g3[:, 8 * c:8 * c + 8], scalar=-1.0, in1=alog, op0=ALU.mult, op1=ALU.mult), t, t_al)

        def conv_group(c0, w0, dst, norm):
            done = []

            def evac(j, ps, t):
                xi, xp, xfree = XP.take()
                t1 = S(lambda e, ps=ps: e.copy(xp[:, 3:3 + T], ps), t, xfree, t_z)
                d = dst[:, j, :]
                tv = V(lambda e: e.tensor_scalar(d, xp[:, 0:T], vcol("conv_w", w0 + j), None, ALU.mult), t1, t_vec, t_in_done)
                for u in range(1, 4):
                    tv = V(lambda e, u=u: e.scalar_tensor_tensor(out=d, in0=xp[:, u:u + T], scalar=vcol("conv_w", 24 * u + w0 + j), in1=d, op0=ALU.mult, op1=ALU.add), tv)
                XP.give(xi, tv)
                t2 = S(lambda e: e.activation(d, d, ACT.Silu), tv)
                done.append(t2)
                return t1

            lin(win, 1024, c0, 1024, nX, T, t_n, evac)
            if norm is None:
                return done
            fin = []
            for j in range(8):
                d = dst[:, j, :]
                si, sq, sfree = SQ.take()
                ri, r, rfree = RR.take()
                t = G(lambda e, d=d, sq=sq: e.tensor_tensor(sq, d, d, ALU.mult), done[j], sfree)
                V.wait(rfree)
                S.wait(rfree)
                t = inv_rms(lambda k, sq=sq: sq, 1, T, 1.0, eps6, r, t)
                SQ.give(si, t)
                t = V(lambda e, d=d, r=r: e.scalar_tensor_tensor(out=d, in0=d, scalar=norm, in1=r, op0=ALU.mult, op1=ALU.mult), t)
                RR.give(ri, t)
                fin.append(t)
            return fin

        t_k = conv_group(C_IN["gk"], 8, gk, 1.0)
        t_v_ = conv_group(C_IN["gv"], 16, gv, None)
        t_q = conv_group(C_IN["gq"], 0, gq, float(128 ** -0.5))
        top[0] = mark_gdn
        g0 = everyone()
        D = shaped(arena[:, g_kv:g_kv + 17 * P], (17, P))
        DT = shaped(arena[:, g_kv + 17 * P:g_kv + 34 * P], (17, P))
        dec = carve(17, P)
        AT = carve(17, P)
        nkb = carve(17, P)
        kta = carve(17, P)
        vb = carve(17, P)
        S1 = carve(8, P)
        S2 = carve(8, P)
        m_mt = top[0]
        MTs = Pool([carve(4, P) for _ in range(3)])
        Ys = Pool([carve(4, P) for _ in range(3)])
        EGs = Pool([b for b in MTs.bufs[:2]])
        kmeta, vmeta = S2[:, 0, :], S2[:, 1, :]
        for a, b, t in ((kmeta, gk, t_k), (vmeta, gv, t_v_)):
            t_meta = V(lambda e, a=a, b=b: e.tensor_copy(a.rearrange("p (h t) -> p h t", h=8), b[:, :, 0:NM]), t, g0)

        gG, gB, GC, GL = small(17), small(17), small(17), small(17)
        eg, ekt, egl, nbe = small(17), small(17), small(17), small(17)
        gmb = small(16)
        hm = small(16)
        t = V(lambda e: e.tensor_copy(gG[:, 0:16].rearrange("p (h c) -> p c h", c=2), g3[:, 0:16].rearrange("p (c h) -> p c h", c=2)), t_g3)
        t2 = V(lambda e: e.tensor_copy(gB[:, 0:16].rearrange("p (h c) -> p c h", c=2), b3[:, 0:16].rearrange("p (c h) -> p c h", c=2)), t_iw)
        t3 = V(lambda e: e.tensor_copy(gmb[:, 0:8], g3[:, 16:24]), t_g3)
        t4 = V(lambda e: e.tensor_copy(gmb[:, 8:16], b3[:, 16:24]), t_iw)
        bi, ps, free = PS.take()
        t = mm1(ps[:, 0:16], cc("Rep")[0:NM, :], gmb[0:NM, :], t, t2, t3, t4, free)
        t5 = V(lambda e, ps=ps: e.tensor_tensor(hm[:, 0:8], ps[:, 0:8], cc("hmask"), ALU.mult), t)
        t6 = V(lambda e, ps=ps: e.tensor_tensor(hm[:, 8:16], ps[:, 8:16], cc("hmask"), ALU.mult), t)
        PS.give(bi, t5, t6)
        t = V(lambda e: e.tensor_reduce(gG[:, 16:17], hm[:, 0:8], AX, ALU.add), t5)
        t_gb = V(lambda e: e.tensor_reduce(gB[:, 16:17], hm[:, 8:16], AX, ALU.add), t6)
        bi, ps, free = PS.take()
        mm1(ps[:, 0:16], cc("U"), gG[:, 0:16], t_gb, free)
        mm1(ps[:, 16:17], cc("Ub"), gG[:, 16:17])
        mm1(ps[:, 17:33], ones, gG[:, 0:16])
        t = mm1(ps[:, 33:34], cc("OB"), gG[:, 16:17])
        t1 = V(lambda e, ps=ps: e.tensor_copy(GC, ps[:, 0:17]), t)
        t2 = V(lambda e, ps=ps: e.tensor_copy(GL, ps[:, 17:34]), t)
        PS.give(bi, t1, t2)
        t3 = V(lambda e: e.tensor_tensor(ekt, GL, GC, ALU.subtract), t2)
        ta = S(lambda e: e.activation(ekt, ekt, ACT.Exp), t3)
        tb = S(lambda e: e.activation(eg, GC, ACT.Exp), t1)
        tc = S(lambda e: e.activation(egl, GL, ACT.Exp), t2)
        td = V(lambda e: e.scalar_tensor_tensor(out=nbe, in0=gB, scalar=-1.0, in1=eg, op0=ALU.mult, op1=ALU.mult), tb)
        t_gates = [ta, tb, tc, td]

        groups = [list(range(4 * i, 4 * i + 4)) for i in range(4)] + [[16]]

        def tok(x, m):
            if m == 16:
                return kmeta if x is gk else vmeta
            return x[:, m // 2, NM + P * (m % 2):NM + P * (m % 2) + P]

        def bc(ap, n):
            return ap.unsqueeze(1).to_broadcast([P, n, P])

        t_kv, t_dec, t_AT, t_att, t_qd = {}, {}, {}, {}, {}
        for g in groups:
            n = len(g) * P
            gl = slice(g[0], g[-1] + 1)
            msk = (cc("Ub"), cc("Ubs")) if g[0] == 16 else (cc("U"), cc("Us"))
            bi, ps, free = PS.take()
            PE.wait(t_k, free, g0, t_meta)
            for x, m in enumerate(g):
                t = PE(lambda e, ps=ps, x=x, m=m: e.transpose(ps[:, x * P:(x + 1) * P], tok(gk, m), ident))
            ts = []
            for x, m in enumerate(g):
                ts.append(S(lambda e, ps=ps, x=x, m=m: e.activation(nkb[:, m, :], ps[:, x * P:(x + 1) * P], ACT.Copy, scale=nbe[:, m:m + 1]), t, t_gates, g0))
            t = ts[-1]
            for x, m in enumerate(g):
                ts.append(V(lambda e, ps=ps, x=x, m=m: e.tensor_scalar(kta[:, m, :], ps[:, x * P:(x + 1) * P], ekt[:, m:m + 1], None, ALU.mult), t, t_gates, g0))
            PS.give(bi, *ts)
            bi, ps, free = PS.take()
            PE.wait(t_v_, free)
            for x, m in enumerate(g):
                t = PE(lambda e, ps=ps, x=x, m=m: e.transpose(ps[:, x * P:(x + 1) * P], tok(gv, m), ident))
            for x, m in enumerate(g):
                ts.append(S(lambda e, ps=ps, x=x, m=m: e.activation(vb[:, m, :], ps[:, x * P:(x + 1) * P], ACT.Copy, scale=gB[:, m:m + 1]), t, t_gb))
            PS.give(bi, *ts[-len(g):])
            t_kv[g[0]] = ts
            bi, ps, free = PS.take()
            PE.wait(free, t_gb)
            for x, m in enumerate(g):
                t = mm1(ps[:, x * P:(x + 1) * P], gG[:, m:m + 1].to_broadcast([P, P]), cc("Ub" if m == 16 else "U"))
            tr = []
            if g[0] != 16:
                ei, eb, efree = EGs.take()
                t = te = S(lambda e, ps=ps, eb=eb: e.activation(eb.rearrange("p a b -> p (a b)"), ps, ACT.Exp), t, efree, g0)
                h0 = g[0] // 2
                qv = gq[:, h0:h0 + 2, NM:T]
                t_qd[g[0]] = (ei, eb, te, qv)
            for x, m in enumerate(g):
                td = V(lambda e, ps=ps, x=x, m=m: e.tensor_scalar(dec[:, m, :], ps[:, x * P:(x + 1) * P], GC[:, m:m + 1], 0.0, ALU.subtract, ALU.min), t, t_gates, g0)
            tr.append(td)
            PS.give(bi, *tr)
            td = S(lambda e, gl=gl: e.activation(dec[:, gl, :], dec[:, gl, :], ACT.Exp), td)
            t_s = G(lambda e, gl=gl, k=len(g), mk=msk[1]: e.tensor_tensor(AT[:, gl, :], dec[:, gl, :], bc(mk, k), ALU.mult), td, g0)
            t_i = G(lambda e, gl=gl, k=len(g), mk=msk[0]: e.tensor_tensor(dec[:, gl, :], dec[:, gl, :], bc(mk, k), ALU.mult), t_s)
            bi, ps, free = PS.take()
            PE.wait(free, t_gb)
            for x, m in enumerate(g):
                t = mm1(ps[:, x * P:(x + 1) * P], gB[:, m:m + 1].to_broadcast([P, P]), ident)
            t = V(lambda e, ps=ps, gl=gl, n=n: e.tensor_tensor(AT[:, gl, :].rearrange("p a b -> p (a b)"), AT[:, gl, :].rearrange("p a b -> p (a b)"), ps[:, 0:n], ALU.mult), t, t_s)
            PS.give(bi, t)
            bi, ps, free = PS.take()
            PE.wait(free)
            for x, m in enumerate(g):
                t2 = mm1(ps[:, x * P:(x + 1) * P], tok(gk, m), tok(gk, m))
            t = V(lambda e, ps=ps, gl=gl, n=n: e.tensor_tensor(AT[:, gl, :].rearrange("p a b -> p (a b)"), AT[:, gl, :].rearrange("p a b -> p (a b)"), ps[:, 0:n], ALU.mult), t, t2)
            PS.give(bi, t)
            t_AT[g[0]] = t
            if g[0] != 16:
                bi, ps, free = PS.take()
                PE.wait(free, t_q)
                for x, m in enumerate(g):
                    t2 = mm1(ps[:, x * P:(x + 1) * P], tok(gk, m), tok(gq, m))
                t = V(lambda e, ps=ps, gl=gl, n=n: e.tensor_tensor(dec[:, gl, :].rearrange("p a b -> p (a b)"), dec[:, gl, :].rearrange("p a b -> p (a b)"), ps[:, 0:n], ALU.mult), t_i, t2)
                PS.give(bi, t)
                t_att[g[0]] = t
                ei, eb, te, qv = t_qd[g[0]]
                tq = G(lambda e, qv=qv, eb=eb: e.tensor_tensor(qv, qv, eb.rearrange("p (h c) b -> p h (c b)", c=2), ALU.mult), te, t2)
                EGs.give(ei, tq)
                t_qd[g[0]] = tq

        g_inv = everyone()
        t_D = {g[0]: (V(lambda e, g=g: e.tensor_copy(D[:, g[0]:g[-1] + 1, :], bc(ident, len(g))), g_inv),
                      G(lambda e, g=g: e.tensor_copy(DT[:, g[0]:g[-1] + 1, :], bc(ident, len(g))), g_inv)) for g in groups}
        MTs.free = [list(EGs.free[0]), list(EGs.free[1]), []]
        steps = [(b, g) for b in (1, 2, 4, 8, 16, 32, 64) for g in groups if b < 16 or g[0] != 16]
        live = {}

        def inv_a(i):
            b, g = steps[i]
            gl, k, n = slice(g[0], g[-1] + 1), len(g), len(g) * P
            mi, mt, mfree = MTs.take()
            yi, y, yfree = Ys.take()
            t = G(lambda e: e.tensor_tensor(mt[:, 0:k, :], AT[:, gl, :], bc(cc(f"m{b}"), k), ALU.mult), t_AT[g[0]], mfree)
            bi, ps, free = PS.take()
            PE.wait(free, t, *t_D[g[0]])
            for x, m in enumerate(g):
                t = mm1(ps[:, x * P:(x + 1) * P], mt[:, x, :], D[:, m, :])
            MTs.give(mi, t)
            t = S(lambda e, ps=ps: e.copy(y[:, 0:k, :].rearrange("p a b -> p (a b)"), ps[:, 0:n]), t, yfree, g0)
            PS.give(bi, t)
            live[i] = (yi, y, t)

        def inv_b(i):
            b, g = steps[i]
            gl, n = slice(g[0], g[-1] + 1), len(g) * P
            yi, y, ty = live.pop(i)
            lastlevel = (b == 64) or (g[0] == 16 and b == 8)
            bi, ps, free = PS.take()
            PE.wait(free, ty)
            for x, m in enumerate(g):
                t = mm1(ps[:, x * P:(x + 1) * P], y[:, x, :], DT[:, m, :])
            if not lastlevel:
                bj, ps2, free2 = PS.take()
                PE.wait(free2)
                for x, m in enumerate(g):
                    t = mm1(ps2[:, x * P:(x + 1) * P], DT[:, m, :], y[:, x, :])
            Ys.give(yi, t)
            fl = lambda a: a[:, gl, :].rearrange("p a b -> p (a b)")
            t2 = V(lambda e, ps=ps: e.tensor_tensor(fl(DT), fl(DT), ps[:, 0:n], ALU.subtract), t)
            PS.give(bi, t2)
            t1 = t2
            if not lastlevel:
                t1 = V(lambda e: e.tensor_tensor(fl(D), fl(D), ps2[:, 0:n], ALU.subtract), t)
                PS.give(bj, t1)
            t_D[g[0]] = (t1, t2)

        for i in range(len(steps) + 1):
            if i < len(steps):
                inv_a(i)
            if i >= 1:
                inv_b(i - 1)
        TT = DT
        t_T = [t_D[g[0]][1] for g in groups]
        t_kvs = [t for v in t_kv.values() for t in v]

        bi, ps, free = PS.take()
        t = mm1(ps[:, 0:P], TT[:, 16, :], vb[:, 16, :], t_T, t_kvs, free)
        vn = D
        t_vn = V(lambda e, ps=ps: e.tensor_copy(vn[:, 16, :], ps[:, 0:P]), t)
        PS.give(bi, t_vn)
        ktm = S2
        for h in range(8):
            t = G(lambda e, h=h: e.tensor_scalar(ktm[:, h, :], kta[:, 16, :], cc("hmask", h, h + 1), None, ALU.mult), t_kvs, t_T)
        t_S = []
        for q in range(2):
            bi, ps, free = PS.take()
            PE.wait(t, t_vn, free)
            for x in range(4):
                t2 = mm1(ps[:, x * P:(x + 1) * P], ktm[:, 4 * q + x, :], vn[:, 16, :])
            t_S.append(V(lambda e, ps=ps, q=q: e.tensor_copy(S1[:, 4 * q:4 * q + 4, :].rearrange("p a b -> p (a b)"), ps), t2))
            PS.give(bi, t_S[-1])
        t_ktm = t2
        t_w = {}
        wT = AT
        for g in groups[:4]:
            bi, ps, free = PS.take()
            PE.wait(free)
            for x, m in enumerate(g):
                t = mm1(ps[:, x * P:(x + 1) * P], nkb[:, m, :], TT[:, m, :])
            t_w[g[0]] = S(lambda e, ps=ps, g=g: e.copy(wT[:, g[0]:g[-1] + 1, :].rearrange("p a b -> p (a b)"), ps), t, [PE.last()], [G.last()])
            PS.give(bi, t_w[g[0]])
        oT = shaped(arena[:, m_mt:m_mt + 8 * SEQ], (8, SEQ))
        g_o1 = everyone()
        t_o = {}
        cur, t_cur = S1, {h: t_S[h // 4] for h in range(8)}
        for c in range(2):
            nxt = {}
            for hp in range(0, 8, 4):
                bi, ps, free = PS.take()
                PE.wait(free)
                for x in range(4):
                    h = hp + x
                    m = 2 * h + c
                    mm1(ps[:, x * P:(x + 1) * P], TT[:, m, :], vb[:, m, :], stop=False)
                    t = mm1(ps[:, x * P:(x + 1) * P], wT[:, m, :], cur[:, h, :], t_w[m // 4 * 4], t_cur[h], start=False)
                ms = [2 * (hp + x) + c for x in range(4)]
                vview = vn[:, ms[0]:ms[-1] + 1:2, :]
                tv = S(lambda e, ps=ps, vview=vview: e.copy(vview, ps.rearrange("p (a b) -> p a b", b=P)), t)
                PS.give(bi, tv)
                if c == 0:
                    bi, ps, free = PS.take()
                    PE.wait(free, tv)
                    for x in range(4):
                        t = mm1(ps[:, x * P:(x + 1) * P], kta[:, ms[x], :], vn[:, ms[x], :])
                    for x in range(4):
                        h = hp + x
                        nxt[h] = V(lambda e, ps=ps, x=x, h=h, m=ms[x]: e.scalar_tensor_tensor(out=S2[:, h, :], in0=S1[:, h, :], scalar=egl[:, m:m + 1], in1=ps[:, x * P:(x + 1) * P], op0=ALU.mult, op1=ALU.add), t, t_ktm, t_cur[h])
                    PS.give(bi, *nxt.values())
                bi, ps, free = PS.take()
                PE.wait(free, tv)
                for x in range(4):
                    h, m = hp + x, ms[x]
                    mm1(ps[:, x * P:(x + 1) * P], cur[:, h, :], tok(gq, m), t_qd[m // 4 * 4], stop=False)
                    t = mm1(ps[:, x * P:(x + 1) * P], vn[:, m, :], dec[:, m, :], t_att[m // 4 * 4], start=False)
                to = S(lambda e, ps=ps, hp=hp, c=c: e.copy(oT[:, hp:hp + 4, P * c:P * c + P], ps.rearrange("p (a b) -> p a b", b=P)), t, g_o1)
                PS.give(bi, to)
                t_o[(c, hp)] = to
            cur, t_cur = S2, nxt
        yg = Pair(shaped(arena_r[:, g_kv:g_kv + 8 * SEQ], (8, SEQ)), shaped(arena_r[:, g_kv + 8 * SEQ:g_kv + 16 * SEQ], (8, SEQ)))
        t_y = []
        g1 = everyone()
        gz = nkb.rearrange("p a b -> p (a b)")[:, 0:8 * SEQ].rearrange("p (a b) -> p a b", a=8)
        t_zz = []

        def evac_z(j, ps, t):
            t = S(lambda e, ps=ps: e.activation(gz[:, j, :], ps, ACT.Silu), t, g1)
            t_zz.append(t)
            return t

        lin(win, 1024, C_IN["gz"], 1024, nX, SEQ, t_n, evac_z, x0=NM)
        rr2 = [dec[:, 2 * j:2 * j + 2, :].rearrange("p a b -> p (a b)") for j in range(8)]
        sq2 = [AT[:, 2 * j:2 * j + 2, :].rearrange("p a b -> p (a b)") for j in range(8)]
        for h in range(8):
            o = oT[:, h, 0:SEQ]
            t = G(lambda e, h=h, o=o: e.tensor_tensor(sq2[h], o, o, ALU.mult), g1)
            S.wait(g1)
            t = inv_rms(lambda k, h=h: sq2[h], 1, SEQ, 1.0 / 128, eps6, rr2[h], t)
            t = V(lambda e, h=h, o=o: e.scalar_tensor_tensor(out=o, in0=o, scalar=vcol("gdn_norm", 0), in1=rr2[h], op0=ALU.mult, op1=ALU.mult), t)
            t = G(lambda e, h=h, o=o: e.tensor_tensor(o, o, gz[:, h, :], ALU.mult), t, t_zz)
            t_y.append(split(o, yg.hi[:, h, :], yg.lo[:, h, :], t, g1))
        if dbg is not None and "yg" in dbg:
            SP.quiet(lambda e: e.dma_start(dbg["yg"], oT).then_inc(s_out, 16), t_y)

        def rope(dst, src, rot, cosn, sinn, t_src, guard, tmp, scale=None):
            n = src.shape[-1]
            bi, ps, free = PS.take()
            t = mm1(ps[:, 0:n], rot, src, t_src, free)
            ti, tb, tfree = tmp.take()
            t1 = V(lambda e, ps=ps: e.tensor_tensor(tb[:, 0:n], ps[:, 0:n], sinn, ALU.mult), t, tfree, guard)
            PS.give(bi, t1)
            t2 = G(lambda e: e.tensor_tensor(src, src, cosn, ALU.mult), t, t_src)
            if scale is None:
                t3 = V(lambda e: e.tensor_tensor(dst, src, tb[:, 0:n], ALU.add), t1, t2)
            else:
                t2 = V(lambda e: e.tensor_tensor(src, src, tb[:, 0:n], ALU.add), t1, t2)
                t3 = V(lambda e: e.tensor_scalar(dst, src, scale, None, ALU.mult), t2)
            tmp.give(ti, t3)
            return t3

        top[0] = mark_gdn
        g2 = everyone()
        aq = carve(8, SEQ)
        ak = carve(2, T)
        iq = carve(4, SEQ)
        ik = carve(T)
        av = carve(3, 256)
        m_yd = top[0]
        yd = carve_pair(8, SEQ)
        rtmp = Pool([carve(T) for _ in range(3)])
        mb = carve(2, T)
        work = carve(2, T)
        m8 = carve(2, 8)
        rel = Pool([carve(T) for _ in range(3)])
        m_att = top[0]
        t_r = {}

        def roped(dst, names, rot, scale, n0):
            res = []
            t_r[id(dst)] = res

            def evac(j, ps, t):
                d = dst[:, j, :]
                t = S(lambda e, ps=ps: e.copy(d, ps), t, g2)
                res.append((d, t))
                return t
            return evac, res

        ev, raw_iq = roped(iq, None, None, None, None)
        lin(win, 1024, C_IN["iq"], 512, nX, SEQ, t_n, ev, x0=NM)
        t_raw = {}

        def plain(dst, key, guard):
            t_raw[key] = []

            def evac(j, ps, t):
                t = S(lambda e: e.copy(dst[:, j, :], ps), t, guard)
                t_raw[key].append(t)
                return t
            return evac

        ik1 = ik.unsqueeze(1)
        lin_block([(lambda v: v[:, :, 0:64], source(win, 0, 8, C_IN["ik"], 64)),
                   (lambda v: v[:, :, 64:128], source(win, 0, 8, C_IN["ik"], 64))], P, nX, 0, T, t_n, plain(ik1, "ik", g2))
        t_ik = rope(ik, ik, cc("R64"), cc("cosI"), cc("sinI"), t_raw["ik"], g2, rtmp)
        t_iq = [rope(d, d, cc("R64"), cc("cosI", NM), cc("sinI", NM), t, g2, rtmp) for d, t in raw_iq]
        lin(win, 1024, C_IN["ak"], 256, nX, T, t_n, plain(ak, "ak", g2))
        avT = work
        lin(win, 1024, C_IN["av"], 256, nX, T, t_n, plain(avT, "av", g2))
        t_av = []
        for c, (k0, n) in enumerate(((0, NM), (NM, P), (NM + P, P))):
            bi, ps, free = PS.take()
            PE.wait(free, t_raw["av"])
            for j in range(2):
                t = PE(lambda e, ps=ps, j=j, k0=k0, n=n: e.transpose(ps[0:n, j * P:(j + 1) * P], avT[:, j, k0:k0 + n], ident))
            t2 = S(lambda e, ps=ps, c=c, n=n: e.copy(av[0:n, c, :], ps[0:n, 0:256]), t, g2)
            PS.give(bi, t2)
            t_av.append(t2)
        t_turned = t
        t_ak = [rope(ak[:, j, :], ak[:, j, :], cc("R128"), cc("cosA"), cc("sinA"), t_raw["ak"][j], g2, rtmp) for j in range(2)]

        t_mb = []
        t_acc = []
        for qt in range(2):
            nk = NM + P * (qt + 1)
            acc = work[:, qt, :]
            t_a = None
            if nk < T:
                t_a = V(lambda e, acc=acc, nk=nk: e.memset(acc[:, nk:T], NEG), g2, t_turned)
            for h in range(8):
                p0 = 64 * (h % 2)
                bi, ps, free = PS.take()
                t = mm1(ps[:, 0:nk], iq[p0:p0 + 64, h // 2, qt * P:(qt + 1) * P], ik[p0:p0 + 64, 0:nk], t_iq[h // 2], t_ik, free)
                ri, r, rfree = rel.take()
                t = S(lambda e, ps=ps, r=r, nk=nk: e.activation(r[:, 0:nk], ps[:, 0:nk], ACT.Relu), t, rfree, g2)
                PS.give(bi, t)
                w1 = iw[:, 8 * qt + h:8 * qt + h + 1]
                if h == 0:
                    t_a = V(lambda e, r=r, acc=acc, nk=nk, w1=w1: e.tensor_scalar(acc[:, 0:nk], r[:, 0:nk], w1, None, ALU.mult), t, t_a, t_iw, t_turned)
                else:
                    t_a = V(lambda e, r=r, acc=acc, nk=nk, w1=w1: e.scalar_tensor_tensor(out=acc[:, 0:nk], in0=r[:, 0:nk], scalar=w1, in1=acc[:, 0:nk], op0=ALU.mult, op1=ALU.add), t, t_a)
                rel.give(ri, t_a)
            t_a = V(lambda e, acc=acc, nk=nk: e.tensor_tensor(acc[:, nk - P:nk], acc[:, nk - P:nk], cc("CB", P, 2 * P), ALU.add), t_a)
            t_acc.append(t_a)
        for it in range(8):
            for qt in range(2):
                w = work[:, qt, :]
                t = V(lambda e, w=w, qt=qt: e.max(m8[:, qt, :], w), t_acc[qt])
                t_acc[qt] = V(lambda e, w=w, qt=qt: e.match_replace(w, m8[:, qt, :], w, TAKEN), t)
        for qt in range(2):
            nk = NM + P * (qt + 1)
            t = V(lambda e, qt=qt: e.tensor_scalar(mb[:, qt, :], work[:, qt, :], -2e38, NEG, ALU.is_gt, ALU.mult), t_acc[qt])
            t_mb.append(V(lambda e, qt=qt, nk=nk: e.tensor_tensor(mb[:, qt, nk - P:nk], mb[:, qt, nk - P:nk], cc("CB", P, 2 * P), ALU.add), t))

        ev, raw_aq = roped(aq, None, None, None, None)
        lin(win, 1024, C_IN["aq"], 1024, nX, SEQ, t_n, ev, x0=NM)
        t_aq = [rope(d, d, cc("R128"), cc("cosA", NM), cc("sinA", NM), t, g2, rtmp, float(128 ** -0.5)) for d, t in raw_aq]

        def attention(units, segs, guard):
            m = top[0]
            ns = len(segs)
            mx = max(u["nk"](1) for u in units)
            Ls = Pool([carve(mx) for _ in range(3)])
            Pbs = Pool([carve(mx) for _ in range(4)])
            PTs = Pool([carve(ns, P) for _ in range(3)])
            sts = Pool([carve(4) for _ in range(4)])
            top[0] = m
            items = [(u, qt) for u in units for qt in range(2)]
            st = {}
            res = []

            def s1(i):
                u, qt = items[i]
                nk = u["nk"](qt)
                bi, ps, free = PS.take()
                t = mm1(ps[:, 0:nk], u["q"][:, qt * P:(qt + 1) * P], u["k"][:, 0:nk], u["t"], free)
                si, s, sfree = sts.take()
                pi, pb, pfree = Pbs.take()
                if u["bias"] is not None:
                    li, L, lfree = Ls.take()
                    t = V(lambda e, ps=ps: e.tensor_tensor(L[:, 0:nk], ps[:, 0:nk], u["bias"](qt), ALU.add), t, lfree, guard)
                    PS.give(bi, t)
                    src = L[:, 0:nk]
                else:
                    src = ps[:, 0:nk]
                t = V(lambda e: e.tensor_reduce(s[:, 0:1], src, AX, ALU.max, negate=True), t, sfree, guard)
                t = S(lambda e: e.activation(pb[:, 0:nk], src, ACT.Exp, bias=s[:, 0:1], accum_out=s[:, 1:2]), t, pfree, guard)
                if u["bias"] is not None:
                    Ls.give(li, t)
                else:
                    PS.give(bi, t)
                t = V(lambda e: e.reciprocal(s[:, 2:3], s[:, 1:2]), t)
                t = V(lambda e: e.tensor_scalar(pb[:, 0:nk], pb[:, 0:nk], s[:, 2:3], None, ALU.mult), t)
                sts.give(si, t)
                st[i] = (pi, pb, t)

            def s2(i):
                u, qt = items[i]
                nk = u["nk"](qt)
                pi, pb, tp = st[i]
                use = [(j, a, n) for j, (a, n) in enumerate(segs) if a < nk]
                bi, ps, free = PS.take()
                PE.wait(tp, free)
                for j, a, n in use:
                    t = PE(lambda e, ps=ps, j=j, a=a, n=n: e.transpose(ps[0:n, j * P:(j + 1) * P], pb[:, a:a + n], ident))
                Pbs.give(pi, t)
                ti, pt, tfree = PTs.take()
                ts = []
                full = [j for j, a, n in use if n == P]
                for j, a, n in use:
                    if n < P:
                        ts.append(S(lambda e, ps=ps, j=j, n=n: e.copy(pt[0:n, j, :], ps[0:n, j * P:(j + 1) * P]), t, tfree, guard))
                j0, j1 = full[0], full[-1] + 1
                ts.append(S(lambda e, ps=ps: e.copy(pt[:, j0:j1, :].rearrange("p a b -> p (a b)"), ps[:, j0 * P:j1 * P]), t, tfree, guard))
                PS.give(bi, *ts)
                st[i] = (ti, pt, ts, use)

            obank = {}

            def s3(i):
                u, qt = items[i]
                ti, pt, ts, use = st.pop(i)
                hd, p0 = u["hd"], u["p0"]
                if qt == 0:
                    obank["b"] = PS.take()
                bi, ps, free = obank["b"]
                PE.wait(free, ts)
                for x, (j, a, n) in enumerate(use):
                    t = mm1(ps[p0:p0 + hd, qt * P:(qt + 1) * P], u["v"](j)[0:n, :], pt[0:n, j, :], start=(x == 0), stop=(x == len(use) - 1))
                PTs.give(ti, t)
                if qt == 1:
                    t = split(ps[p0:p0 + hd, 0:SEQ], u["out"][0], u["out"][1], t, guard)
                    PS.give(bi, t)
                    res.append(t)

            N = len(items)
            for i in range(N + 4):
                if i < N:
                    s1(i)
                if 0 <= i - 2 < N:
                    s2(i - 2)
                if 0 <= i - 3 < N:
                    s3(i - 3)
            return res

        units = [dict(q=aq[:, h, :], k=ak[:, h // 4, :], v=lambda j, h=h: av[:, j, (h // 4) * P:(h // 4 + 1) * P],
                      bias=lambda qt: mb[:, qt, 0:NM + P * (qt + 1)], nk=lambda qt: NM + P * (qt + 1),
                      hd=P, p0=0, out=(yd.hi[:, h, :], yd.lo[:, h, :]), t=[t_aq[h], t_ak[h // 4], t_mb, t_av]) for h in range(8)]
        t_yd = attention(units, [(0, NM), (NM, P), (NM + P, P)], g2)
        if dbg is not None and "yd" in dbg:
            SP.quiet(lambda e: e.dma_start(dbg["yd"], yd.hi.bitcast(F32)).then_inc(s_out, 16), t_yd)

        top[0] = m_att
        g3_ = everyone()
        mg = carve_pair(8, SEQ)
        ta_ = [shaped(arena[:, top_g + SEQ * j:top_g + SEQ * (j + 1)], (SEQ,)) for j in range(4)]
        tb_ = [shaped(arena[:, top_g + SEQ * j:top_g + SEQ * (j + 1)], (SEQ,)) for j in range(4, 8)]
        t_mg = []
        wa1, wb1 = A["w_branch_gdn"][0], A["w_branch_dsa"][0]
        for g in range(4):
            tt = {}

            def gate(buf, key):
                def evac(j, ps, t):
                    tt[key, j] = S(lambda e: e.activation(buf[j % 4], ps, ACT.Sigmoid), t, g3_, t_mg)
                    return tt[key, j]
                return evac

            def times(buf, key):
                def evac(j, ps, t):
                    b = buf[j % 4]
                    t1 = V(lambda e: e.tensor_tensor(b, b, ps, ALU.mult), t, tt[key, j])
                    if key == "a":
                        tt[key, j] = t1
                    else:
                        t2 = G(lambda e: e.tensor_tensor(b, b, ta_[j % 4], ALU.add), t1, tt["a", j])
                        t_mg.append(split(b, mg.hi[:, j, :], mg.lo[:, j, :], t2))
                    return t1
                return evac

            lin(win, 1024, C_IN["gate_a"] + 256 * g, 256, nX, SEQ, t_n, gate(ta_, "a"), x0=NM, j0=2 * g)
            lin(wa1, 1024, 256 * g, 256, yg, SEQ, t_y, times(ta_, "a"), j0=2 * g)
            lin(win, 1024, C_IN["gate_b"] + 256 * g, 256, nX, SEQ, t_n, gate(tb_, "b"), x0=NM, j0=2 * g)
            lin(wb1, 1024, 256 * g, 256, yd, SEQ, t_yd, times(tb_, "b"), j0=2 * g)

        def keep(dst, ts, guard):
            def evac(j, ps, t):
                if j % 2:
                    t = V(lambda e: e.tensor_copy(dst[:, j, :], ps), t, guard)
                else:
                    t = S(lambda e: e.copy(dst[:, j, :], ps), t, guard)
                ts.append(t)
                return t
            return evac

        g_x = everyone()
        mix, t_mix = aq, []
        xin2 = shaped(arena[:, m_yd:m_yd + 2048], (2, 1024))
        t_x2in = load_in(8, xin2, A["x"][0].rearrange("(a p) d -> p a d", p=P), g_x)
        lin(A["w_out"][0], 1024, 0, 1024, mg, SEQ, t_mg, keep(mix, t_mix, g_x))
        top[0] = 0
        x2 = carve(8, SEQ)

        def residual(k, tmp, t):
            bi, ps, free = PS.take()
            PE.wait(free, t_x2in)
            for a in range(2):
                t2 = PE(lambda e, a=a: e.transpose(ps[:, a * P:(a + 1) * P], xin2[:, a, k * P:(k + 1) * P], ident))
            t = V(lambda e: e.tensor_tensor(x2[:, k, :], tmp, ps[:, 0:SEQ], ALU.add), t, t2)
            PS.give(bi, t)
            return t

        t_x2 = rms_scaled(mix, SEQ, "post_mix_norm", 0, m_att, t_mix, residual)
        t_n2 = rms_scaled(x2, SEQ, "pre_mlp_norm", 0, m_att, t_x2, into(X))
        g4 = everyone()
        top[0] = 2048
        u_ = carve_pair(32, SEQ)
        dn, t_dn = carve(8, SEQ), []
        ut = Pool([carve(2, SEQ) for _ in range(3)])
        t_u = []

        def evac_u(j, ps, t):
            ui, ub, ufree = ut.take()
            t1 = S(lambda e: e.activation(ub[:, 0, :], ps, ACT.Relu), t, g4, ufree)
            t2 = G(lambda e: e.tensor_tensor(ub[:, 1, :], ub[:, 0, :], ub[:, 0, :], ALU.mult), t1)
            t2 = split(ub[:, 1, :], u_.hi[:, j, :], u_.lo[:, j, :], t2, g4)
            ut.give(ui, t2)
            t_u.append(t2)
            return t1

        lin(A["w_up"][0], 1024, 0, 4096, X, SEQ, t_n2, evac_u)
        lin(A["w_down"][0], 4096, 0, 1024, u_, SEQ, t_u, keep(dn, t_dn, g4))

        def residual2(k, tmp, t):
            t = G(lambda e: e.tensor_tensor(x2[:, k, :], x2[:, k, :], tmp, ALU.add), t)
            return [t, into(X)(k, x2[:, k, :], t)]

        t_x3 = rms_scaled(dn, SEQ, "post_mlp_norm", 0, 2048, t_dn, residual2)
        if dbg is not None and "x3" in dbg:
            SP.quiet(lambda e: e.dma_start(dbg["x3"], x2).then_inc(s_out, 16), t_x3)

        g5 = everyone()
        top[0] = 2048
        xm = carve(8, SEQ)
        m_moe = top[0]
        kms = [carve(2, SEQ) for _ in range(2)]
        vms = [carve(2, 256) for _ in range(2)]
        cos2, sin2 = carve(SEQ), carve(SEQ)
        m_ffn = top[0]
        mix2 = carve_pair(8, SEQ)
        kx = carve(6, SEQ)
        vx = carve(2, 768)
        m_b2 = top[0]
        m_ln = 18500
        memT = carve_pair(8, SEQ)
        memin = carve(2, 1024)
        t_mem = load_in(6, memin, A["mem_2"][0].rearrange("(a p) d -> p a d", p=P), g5)
        t_memT = []
        for k in range(8):
            bi, ps, free = PS.take()
            PE.wait(t_mem, free)
            for a in range(2):
                t = PE(lambda e, ps=ps, a=a, k=k: e.transpose(ps[:, a * P:(a + 1) * P], memin[:, a, k * P:(k + 1) * P], ident))
            t = split(ps[:, 0:SEQ], memT.hi[:, k, :], memT.lo[:, k, :], t, g5)
            PS.give(bi, t)
            t_memT.append(t)
        ang, kf = carve(SEQ), carve(SEQ)
        ki = posi
        two_pi = 2 * np.pi
        t = V(lambda e: e.tensor_copy(ang, posi[:, :]), t_pos, g5)
        t = V(lambda e: e.tensor_scalar(ang, ang, cc("inv2"), None, ALU.mult), t)
        for big in (4096.0, 1.0):
            rest = two_pi * big
            parts = []
            for bits in (8, 8):
                sc = 2.0 ** (bits - 1 - np.floor(np.log2(rest)))
                p_ = float(np.floor(rest * sc) / sc)
                parts.append(p_)
                rest -= p_
            parts += [float(np.float32(rest))]
            t = V(lambda e, big=big: e.tensor_scalar(kf, ang, float(1.0 / (two_pi * big)), None, ALU.mult), t)
            t = V(lambda e: e.tensor_copy(ki[:, :], kf), t)
            t = V(lambda e: e.tensor_copy(kf, ki[:, :]), t)
            for p_ in parts:
                t = V(lambda e, p_=p_: e.scalar_tensor_tensor(out=ang, in0=kf, scalar=-p_, in1=ang, op0=ALU.mult, op1=ALU.add), t)
        for cmp_, sgn in ((ALU.is_gt, -two_pi), (ALU.is_lt, two_pi)):
            lim = float(np.pi) if sgn < 0 else -float(np.pi)
            t = V(lambda e, cmp_=cmp_, lim=lim, sgn=sgn: e.tensor_scalar(kf, ang, lim, float(sgn), cmp_, ALU.mult), t)
            t = V(lambda e: e.tensor_tensor(ang, ang, kf, ALU.add), t)
        t = V(lambda e: e.tensor_scalar(ang, ang, 3.1415925, -3.1415925, ALU.min, ALU.max), t)
        t_s2 = S(lambda e: e.activation(sin2, ang, ACT.Sin), t)
        t = S(lambda e: e.activation(kf, ang, ACT.Sin, scale=0.5), t)
        t = V(lambda e: e.tensor_tensor(kf, kf, kf, ALU.mult), t)
        t_rot = [t_s2, V(lambda e: e.tensor_scalar(cos2, kf, -2.0, 1.0, ALU.mult, ALU.add), t)]
        alpha = float(4 ** 0.25)
        xcur, t_xc = x2, t_x3

        def mem_kv(layer):
            w = A["w_mem_kv_2"][layer]
            km, vm = kms[layer], vms[layer]
            ts = []
            lin(w, 1024, 0, 256, memT, SEQ, t_memT, keep(km, ts, g5))
            slots, wp, tw = stream([(whole, source(w, 0, 8, 256, 256))], (8, 256))
            for c in range(2):
                bi, ps, t = tok_block(wp, tw, 256, memT, c * P, P, t_memT, c == 1)
                t2 = V(lambda e, ps=ps, c=c: e.tensor_copy(vm[:, c, :], ps), t, g5)
                PS.give(bi, t2)
                ts.append(t2)
            release(slots, t)
            return ts

        t_mkvs = [mem_kv(layer) for layer in range(2)]
        top[0] = m_b2

        def layer_norm(src, gname, bname, li, dst, t_src, pair):
            m = top[0]
            top[0] = m_ln
            mu, r, sq = carve(SEQ), carve(SEQ), carve(8, SEQ)
            top[0] = m
            guard = everyone()
            bi, ps, free = PS.take()
            PE.wait(t_src, free)
            for k in range(8):
                t = PE(lambda e, k=k, ps=ps: e.matmul(ps[:, 0:SEQ], ones, src[:, k, :], start=(k == 0), stop=(k == 7)))
            t = S(lambda e, ps=ps: e.activation(mu, ps[:, 0:SEQ], ACT.Copy, scale=1.0 / 1024), t, guard)
            PS.give(bi, t)
            tsq = []
            for k in range(8):
                tc_ = V(lambda e, k=k: e.tensor_tensor(src[:, k, :], src[:, k, :], mu, ALU.subtract), t, t_src)
                tsq.append(S(lambda e, k=k: e.activation(sq[:, k, :], src[:, k, :], ACT.Square), tc_))
            t = inv_rms(lambda k: sq[:, k, :], 8, SEQ, 1.0 / 1024, eps5, r, tsq)
            res = []
            for k in range(8):
                t1 = V(lambda e, k=k: e.scalar_tensor_tensor(out=src[:, k, :], in0=src[:, k, :], scalar=vcol(gname, 8 * li + k), in1=r, op0=ALU.mult, op1=ALU.mult), t)
                t1 = S(lambda e, k=k: e.activation(dst[:, k, :], src[:, k, :], ACT.Identity, bias=vcol(bname, 8 * li + k)), t1, guard)
                res.append([t1, into(pair)(k, dst[:, k, :], t1)] if pair is not None else t1)
            return res

        def add_alpha(base, dst, ts, guard):
            def evac(j, ps, t):
                t = V(lambda e, ps=ps: e.scalar_tensor_tensor(out=dst[:, j, :], in0=base[:, j, :], scalar=alpha, in1=ps, op0=ALU.mult, op1=ALU.add), t, guard)
                ts.append(t)
                return t
            return evac

        def memory_units(t_q, layer):
            km, vm = kms[layer], vms[layer]
            return [dict(q=qm[64 * (h % 2):64 * (h % 2) + 64, h // 2, :], k=km[64 * (h % 2):64 * (h % 2) + 64, h // 2, :],
                         v=lambda j, h=h: vm[:, j, 64 * h:64 * h + 64], bias=None, nk=lambda qt: SEQ, hd=64, p0=64 * (h % 2),
                         out=[x[64 * (h % 2):64 * (h % 2) + 64, 6 + h // 2, :] for x in (mix2.hi, mix2.lo)], t=t_q) for h in range(4)]

        segs2 = [(0, P), (P, P)]

        def scaled(dst, ts, guard, j0=0):
            def evac(j, ps, t):
                t = S(lambda e, ps=ps: e.activation(dst[:, j - j0, :], ps, ACT.Copy, scale=0.125), t, guard)
                ts.append(t)
                return t
            return evac

        for layer in range(2):
            g_l = everyone()
            t_mkv = t_mkvs[layer]
            top[0] = m_b2
            qm = carve(2, SEQ)
            if layer == 0:
                wa = A["w_in_a_2"][0]
                uc = carve(6, SEQ)
                zp = carve(6, SEQ + 2)
                t_zp = G(lambda e: e.memset(zp[:, :, 0:2], 0.0), g_l)
                tc_, tz_, tm_ = [], [], []
                lin(wa, 1024, 768, 768, X, SEQ, t_xc, keep(uc, tc_, g_l))

                def evac_h(j, ps, t):
                    t = V(lambda e, ps=ps: e.tensor_tensor(zp[:, j, 2:2 + SEQ], ps, uc[:, j, :], ALU.mult), t, tc_[j], g_l)
                    tz = V(lambda e: e.tensor_scalar(uc[:, j, :], zp[:, j, 0:SEQ], vcol("conv_a_2", j), None, ALU.mult), t, t_zp)
                    for u in (1, 2):
                        tz = V(lambda e, u=u: e.scalar_tensor_tensor(out=uc[:, j, :], in0=zp[:, j, u:u + SEQ], scalar=vcol("conv_a_2", 6 * u + j), in1=uc[:, j, :], op0=ALU.mult, op1=ALU.add), tz)
                    tz_.append(tz)
                    return t

                lin(wa, 1024, 1536, 768, X, SEQ, t_xc, evac_h)

                def evac_bb(j, ps, t):
                    t = V(lambda e, ps=ps: e.tensor_tensor(uc[:, j, :], ps, uc[:, j, :], ALU.mult), t, tz_[j], g_l)
                    tm_.append(split(uc[:, j, :], mix2.hi[:, j, :], mix2.lo[:, j, :], t))
                    return t

                t_qm = []
                lin(wa, 1024, 2304, 256, X, SEQ, t_xc, scaled(qm, t_qm, g_l))
                lin(wa, 1024, 0, 768, X, SEQ, t_xc, evac_bb)
                t_mix2 = tm_ + attention(memory_units(t_qm + t_mkv, layer), segs2, g_l)
            else:
                raw = []
                t_qm = []
                qx = carve(6, SEQ)
                rtmp2 = Pool([carve(SEQ) for _ in range(3)])
                wq = A["w_q_b_2"][0]
                lin(wq, 1024, 0, 768, X, SEQ, t_xc, keep(qx, raw, g_l))
                lin(wq, 1024, 768, 256, X, SEQ, t_xc, scaled(qm, t_qm, g_l))
                t_qx = [rope(qx[:, j, :], qx[:, j, :], cc("R16"), cos2, sin2, [raw[j], t_rot], g_l, rtmp2, 0.125) for j in range(6)]
                units = [dict(q=qx[64 * (h % 2):64 * (h % 2) + 64, h // 2, :], k=kx[64 * (h % 2):64 * (h % 2) + 64, h // 2, :],
                              v=lambda j, h=h: vx[:, j, 64 * h:64 * h + 64], bias=lambda qt: cc("CB", P, 2 * P) if qt == 0 else cc("CB"),
                              nk=lambda qt: P * (qt + 1), hd=64, p0=64 * (h % 2),
                              out=[x[64 * (h % 2):64 * (h % 2) + 64, h // 2, :] for x in (mix2.hi, mix2.lo)], t=[t_qx[h // 2], t_kx, t_vx]) for h in range(12)]
                t_mix2 = attention(memory_units(t_qm + t_mkv, layer) + units, segs2, g_l)
            t_s = []
            lin(A["w_o_2"][layer], 1024, 0, 1024, mix2, SEQ, t_mix2, add_alpha(xcur, xm, t_s, g_l))
            top[0] = m_b2
            t_xc = layer_norm(xm, "ln1_g_2", "ln1_b_2", layer, xcur, t_s, X)
            if dbg is not None and f"l{layer}a" in dbg:
                SP.quiet(lambda e, layer=layer: e.dma_start(dbg[f"l{layer}a"], xcur).then_inc(s_out, 16), t_xc)
            g_f = everyone()
            if layer == 0:
                top[0] = m_ffn
                gg = carve_pair(22, SEQ)
                gt_ = Pool([carve(SEQ) for _ in range(4)])
                t_gg = [None] * 22
                held = {}

                def evac_g(j, ps, t):
                    ti, tb, tfree = gt_.take()
                    t = S(lambda e: e.activation(tb, ps, ACT.Silu), t, g_f, tfree)
                    held[j] = (ti, tb, t)
                    return t

                def evac_u2(j, ps, t):
                    ti, tb, tg = held.pop(j)
                    t1 = V(lambda e: e.tensor_tensor(tb, tb, ps, ALU.mult), t, tg)
                    t_gg[j] = split(tb, gg.hi[:, j, :], gg.lo[:, j, :], t1)
                    gt_.give(ti, t_gg[j])
                    return t1

                wgu = A["w_gu_dense_2"][0]
                for f0 in range(0, 2816, 256):
                    lin(wgu, 1024, f0, 256, X, SEQ, t_xc, evac_g, j0=f0 // P)
                    lin(wgu, 1024, 2816 + f0, 256, X, SEQ, t_xc, evac_u2, j0=f0 // P)
                t_s = []
                lin(A["w_down_dense_2"][0], 2816, 0, 1024, gg, SEQ, t_gg, add_alpha(xcur, xm, t_s, g_f))
                t_xc = layer_norm(xm, "ln2_g_2", "ln2_b_2", layer, xcur, t_s, X)
                if dbg is not None and "l0" in dbg:
                    SP.quiet(lambda e: e.dma_start(dbg["l0"], xcur).then_inc(s_out, 16), t_xc)
                g_k = everyone()
                raw, t_vx = [], []
                top[0] = m_b2
                rtmp2 = Pool([carve(SEQ) for _ in range(3)])
                wkv = A["w_kv_shared_2"]
                lin(wkv, 1024, 0, 768, X, SEQ, t_xc, keep(kx, raw, g_k))
                t_kx = [rope(kx[:, j, :], kx[:, j, :], cc("R16"), cos2, sin2, [raw[j], t_rot], g_k, rtmp2) for j in range(6)]
                for c0 in range(0, 768, 256):
                    slots, wp, tw = stream([(whole, source(wkv, 0, 8, 768 + c0, 256))], (8, 256))
                    for c in range(2):
                        bi, ps, t = tok_block(wp, tw, 256, X, c * P, P, t_xc, c == 1)
                        t2 = V(lambda e, ps=ps, c=c, c0=c0: e.tensor_copy(vx[:, c, c0:c0 + 256], ps), t, g_k)
                        PS.give(bi, t2)
                        t_vx.append(t2)
                    release(slots, t)

        g_m = everyone()
        top[0] = m_moe
        acc = xm
        xt = carve(2, 1024)
        wr = carve(8, 8)
        t_wr = load_in(7, wr, A["w_router_2"][0].rearrange("(k p) n -> p k n", p=P), g_m)
        lg, m8b, gt2, oh = carve(2, 8), carve(2, 8), carve(2, 8), carve(2, 2, 8)
        ix = sb("ix", [P, 2, 8], U32)
        flag = sb("flag", [P, 1], I32)
        ixf, sel, ge, posm, cnt = carve(2, 8), carve(2, 8), carve(2, 8), carve(2, 8), carve(8)
        t_sel, t_ge = [], []
        for c in range(2):
            bi, ps, t = lin_tok(lambda k: wr[:, k, :], 8, lambda k, c=c: xcur[:, k, c * P:(c + 1) * P], 8, t_wr, t_xc, P)
            t = V(lambda e, ps=ps, c=c: e.tensor_copy(lg[:, c, :], ps), t, g_m)
            PS.give(bi, t)
            t = V(lambda e, c=c: e.max(m8b[:, c, :], lg[:, c, :]), t)
            t2 = V(lambda e, c=c: e.max_index(ix[:, c, :], m8b[:, c, :], lg[:, c, :]), t)
            t2 = V(lambda e, c=c: e.tensor_copy(ixf[:, c, :], ix[:, c, :]), t2)
            g_ = gt2[:, c, :]
            t = V(lambda e, c=c, g_=g_: e.tensor_tensor(g_[:, 2:3], m8b[:, c, 1:2], m8b[:, c, 0:1], ALU.subtract), t)
            t = S(lambda e, g_=g_: e.activation(g_[:, 3:4], g_[:, 2:3], ACT.Exp), t)
            t = V(lambda e, g_=g_: e.tensor_scalar(g_[:, 4:5], g_[:, 3:4], 1.0, None, ALU.add), t)
            t = V(lambda e, g_=g_: e.reciprocal(g_[:, 0:1], g_[:, 4:5]), t)
            t = V(lambda e, g_=g_: e.tensor_tensor(g_[:, 1:2], g_[:, 3:4], g_[:, 0:1], ALU.mult), t)
            for r in range(2):
                t3 = V(lambda e, c=c, r=r: e.tensor_scalar(oh[:, c, r, :], cc("iota8"), ixf[:, c, r:r + 1], None, ALU.is_equal), t2)
            t_sel.append(V(lambda e, c=c: e.tensor_tensor(sel[:, c, :], oh[:, c, 0, :], oh[:, c, 1, :], ALU.add), t3))
            t = V(lambda e, c=c, g_=g_: e.tensor_scalar(ge[:, c, :], oh[:, c, 0, :], g_[:, 0:1], None, ALU.mult), t, t3)
            t_ge.append(V(lambda e, c=c, g_=g_: e.scalar_tensor_tensor(out=ge[:, c, :], in0=oh[:, c, 1, :], scalar=g_[:, 1:2], in1=ge[:, c, :], op0=ALU.mult, op1=ALU.add), t))
        t_xt = []
        for c in range(2):
            for hf in range(2):
                bi, ps, free = PS.take()
                PE.wait(free, t_xc)
                for k in range(4):
                    t = PE(lambda e, ps=ps, k=k, hf=hf, c=c: e.transpose(ps[:, k * P:(k + 1) * P], xcur[:, 4 * hf + k, c * P:(c + 1) * P], ident))
                t = S(lambda e, ps=ps, c=c, hf=hf: e.copy(xt[:, c, 512 * hf:512 * hf + 512], ps), t, g_m)
                PS.give(bi, t)
                t_xt.append(t)
        t_pos = []
        for c in range(2):
            bi, ps, free = PS.take()
            t = mm1(ps[:, 0:8], cc("U"), sel[:, c, :], t_sel, free, stop=(c == 0))
            if c == 1:
                t = mm1(ps[:, 0:8], ones, sel[:, 0, :], start=False)
            t = V(lambda e, ps=ps, c=c: e.tensor_tensor(posm[:, c, :], ps[:, 0:8], sel[:, c, :], ALU.mult), t)
            PS.give(bi, t)
            t_pos.append(V(lambda e, c=c: e.tensor_scalar(posm[:, c, :], posm[:, c, :], -1.0, None, ALU.add), t))
        bi, ps, free = PS.take()
        mm1(ps[:, 0:8], ones, sel[:, 0, :], free, stop=False)
        t = mm1(ps[:, 0:8], ones, sel[:, 1, :], start=False)
        t = V(lambda e, ps=ps: e.tensor_reduce(cnt[:, 0:1], ps[:, 0:8], AX, ALU.max), t)
        PS.give(bi, t)
        t = V(lambda e: e.tensor_scalar(cnt[:, 1:2], cnt[:, 0:1], float(P), None, ALU.is_gt), t)
        t_flag = V(lambda e: e.tensor_copy(flag[:, :], cnt[:, 1:2]), t)

        Pm = Pool([carve(2, P) for _ in range(2)])
        GP = Pool([carve(2, P) for _ in range(2)])
        GPT = Pool([carve(SEQ) for _ in range(2)])
        XS = Pool([carve_pair(8, P) for _ in range(2)])
        YE = Pool([carve(1024) for _ in range(2)])
        hh = carve(2816)
        hp = carve_pair(22, P)
        t_acc = [V(lambda e, j=j: e.tensor_scalar(acc[:, 2 * j:2 * j + 2, :], xcur[:, 2 * j:2 * j + 2, :], alpha, None, ALU.mult), g_m, t_xc) for j in range(4)]

        def pick(q, base, t_start):
            pi, pm, pfree = Pm.take()
            gi, gp, gfree = GP.take()
            for c in range(2):
                t1 = V(lambda e, c=c: e.tensor_scalar(pm[:, c, :], cc("iota", base, base + P), posm[:, c, q:q + 1], None, ALU.is_equal), t_pos, pfree, g_m, t_start)
                t2 = V(lambda e, c=c: e.tensor_scalar(gp[:, c, :], cc("iota", base, base + P), posm[:, c, q:q + 1], ge[:, c, q:q + 1], ALU.is_equal, ALU.mult), t_pos, t_ge, gfree, g_m)
            xi, xs, xfree = XS.take()
            ts = []
            for hf in range(2):
                bi, ps, free = PS.take()
                PE.wait(free, t1, t_xt)
                for k in range(4):
                    kk = 4 * hf + k
                    for c in range(2):
                        t = mm1(ps[:, k * P:(k + 1) * P], xt[:, c, kk * P:(kk + 1) * P], pm[:, c, :], start=(c == 0), stop=(c == 1))
                tx = split(ps, *[x[:, 4 * hf:4 * hf + 4, :].rearrange("p a b -> p (a b)") for x in (xs.hi, xs.lo)], t, xfree, g_m)
                PS.give(bi, tx)
                ts.append(tx)
            Pm.give(pi, t)
            ti, gt, tfree = GPT.take()
            bi, ps, free = PS.take()
            PE.wait(free, t2)
            for c in range(2):
                t = PE(lambda e, ps=ps, c=c: e.transpose(ps[:, c * P:(c + 1) * P], gp[:, c, :], ident))
            GP.give(gi, t)
            tg = S(lambda e, ps=ps: e.copy(gt, ps[:, 0:SEQ]), t, tfree, g_m)
            PS.give(bi, tg)
            return (xi, xs, ts, ti, gt, tg)

        def expert_up(q, picked):
            xi, xs, ts, ti, gt, tg = picked
            w = A["w_gu_moe_2"][0, q]
            guard = [PE.last()]
            t_h, t_hp = {}, []

            def turn(f):
                n = min(4, 22 - f)
                bi, ps, free = PS.take()
                PE.wait(free, [t_h[x // 2] for x in range(f, f + n)])
                for x in range(n):
                    t = PE(lambda e, x=x: e.transpose(ps[:, x * P:(x + 1) * P], hh[:, (f + x) * P:(f + x + 1) * P], ident))
                t2 = split(ps[:, 0:n * P], *[x[:, f:f + n, :].rearrange("p a b -> p (a b)") for x in (hp.hi, hp.lo)], t, guard, g_m)
                PS.give(bi, t2)
                t_hp.append((t, t2))

            for j in range(11):
                for side in range(2):
                    slots, wp, tw = stream([(whole, source(w, 0, 8, 2816 * side + 256 * j, 256))], (8, 256))
                    bi, ps, t = tok_block(wp, tw, 256, xs, 0, P, ts, True)
                    release(slots, t)
                    hv = hh[:, 256 * j:256 * j + 256]
                    if side == 0:
                        t_h[j] = S(lambda e, ps=ps, hv=hv: e.activation(hv, ps, ACT.Silu), t, guard, g_m)
                    else:
                        t_h[j] = V(lambda e, ps=ps, hv=hv: e.tensor_tensor(hv, hv, ps, ALU.mult), t, t_h[j])
                    PS.give(bi, t_h[j])
                if j >= 2 and j % 2 == 0:
                    turn(2 * j - 4)
            XS.give(xi, PE.last())
            return t_hp, turn

        def expert_down(q, up):
            t_hp, turn = up
            w = A["w_down_moe_2"][0, q]
            b = [PS.take() for _ in range(2)]
            for f0 in range(0, 22, 2):
                if f0 == 2:
                    turn(20)
                slots, wp, tw = stream([(whole, w[f0 * P:(f0 + 2) * P, :].rearrange("(k p) n -> p k n", p=P))], (2, 1024))
                for hf in range(2):
                    bi, ps, free = b[hf]
                    PE.wait(tw, free, t_hp[f0 // 4][1])
                    for k in range(2):
                        f = f0 + k
                        t = mm3(ps, (hp.hi[:, f, :], hp.lo[:, f, :]), [x[:, k, 512 * hf:512 * hf + 512] for x in (wp.hi, wp.lo)], f == 0, f == 21)
                if f0 < 20:
                    t = PE.tick()
                release(slots, t)
            yi, ye, yfree = YE.take()
            ts = []
            for hf in range(2):
                bi, ps, free = b[hf]
                if hf:
                    ts.append(V(lambda e, ps=ps: e.tensor_copy(ye[:, 512:1024], ps), t, yfree, g_m))
                else:
                    ts.append(S(lambda e, ps=ps: e.copy(ye[:, 0:512], ps), t, yfree, g_m))
                PS.give(bi, ts[-1])
            return yi, ye, ts

        def spread(q,  picked, made):
            xi, xs, _, ti, gt, tg = picked
            yi, ye, ts = made
            for h2 in range(4):
                bi, ps, free = PS.take()
                PE.wait(free, ts, tg)
                for k in range(2):
                    kk = 2 * h2 + k
                    t = mm1(ps[:, k * SEQ:(k + 1) * SEQ], ye[:, kk * P:(kk + 1) * P], gt)
                av_ = acc[:, 2 * h2:2 * h2 + 2, :].rearrange("p a b -> p (a b)")
                if True:
                    t_acc[h2] = V(lambda e, ps=ps, av_=av_: e.tensor_tensor(av_, av_, ps, ALU.add), t, t_acc[h2])
                PS.give(bi, t_acc[h2])
            YE.give(yi, t)
            GPT.give(ti, t)

        def all_experts(base, t_start):
            nxt = pick(0, base, t_start)
            prev = None
            for q in range(8):
                cur_ = nxt
                up = expert_up(q, cur_)
                if prev is not None:
                    spread(q - 1, *prev)
                if q < 7:
                    nxt = pick(q + 1, base, None)
                made = expert_down(q, up)
                prev = (cur_, made)
            spread(7, *prev)

        all_experts(0, None)

        main_slots = (list(s_slot), list(n_slot))
        queues = (PE, V, S, G, SP)
        before = everyone()
        for q_, s_ in zip(queues, (sem("x_pe"), sem("x_dve"), sem("x_act"), sem("x_pool"), None)):
            q_.enter(s_)
            q_.wait(before)
        s_slot[:] = [sem(f"x_slot{i}") for i in range(NRAW)]
        n_slot[:] = [0] * NRAW
        pools = (PS, RAW, HI, Pm, GP, GPT, XS, YE)
        for p_ in pools:
            p_.free = [[] for _ in p_.bufs]
        t_acc_main = list(t_acc)
        new_segment()
        all_experts(P, None)
        done = everyone()
        for q_ in queues:
            q_.wait(done)
        for q_ in queues:
            q_.leave(flag[0:1, 0:1], t_flag, before)
        s_slot[:], n_slot[:] = main_slots
        for p_ in pools:
            p_.free = [[] for _ in p_.bufs]
        t_acc = [t_acc_main[j // 2] for j in range(8)]
        top[0] = m_b2
        t_xc = layer_norm(xm, "ln2_g_2", "ln2_b_2", 1, xcur, t_acc, None)

        g_o = everyone()
        fin = carve(2, 1024)
        for c in range(2):
            tf = []
            for hf in range(2):
                bi, ps, free = PS.take()
                PE.wait(free, t_xc)
                for k in range(4):
                    t = PE(lambda e, ps=ps, k=k, hf=hf, c=c: e.transpose(ps[:, k * P:(k + 1) * P], xcur[:, 4 * hf + k, c * P:(c + 1) * P], ident))
                if hf:
                    t = V(lambda e, ps=ps, c=c: e.tensor_copy(fin[:, c, 512:1024], ps), t, g_o)
                else:
                    t = S(lambda e, ps=ps, c=c: e.copy(fin[:, c, 0:512], ps), t, g_o)
                PS.give(bi, t)
                tf.append(t)
            SP.quiet(lambda e, c=c: e.dma_start(out[0, c * P:(c + 1) * P, :], fin[:, c, :]).then_inc(s_out, 16), tf)
        n_out = 16 * (2 + (len(dbg) if dbg is not None else 0))
        SP.quiet(lambda e: e.wait_ge(s_out, n_out))

        return (PE, V, S, G, SP), W["rec"]


INS = ["x", "meta_tokens", "pre_mix_norm", "w_in", "conv_w", "a_log", "dt_bias", "gdn_norm", "w_branch_gdn",
       "w_branch_dsa", "w_out", "post_mix_norm", "pre_mlp_norm", "w_up", "w_down", "post_mlp_norm", "mem_2",
       "positions_2", "w_in_a_2", "conv_a_2", "w_q_b_2", "w_kv_shared_2", "w_mem_kv_2", "w_o_2", "ln1_g_2",
       "ln1_b_2", "ln2_g_2", "ln2_b_2", "w_gu_dense_2", "w_down_dense_2", "w_router_2", "w_gu_moe_2",
       "w_down_moe_2"]


def kernel(**inputs):
    from concourse import bacc
    from concourse.bass_utils import run_bass_kernel_spmd

    nc = bacc.Bacc("TRN2", target_bir_lowering=False, num_devices=1)
    arrays, aps = {}, {}
    for name in INS:
        a = np.ascontiguousarray(inputs[name])
        arrays[f"in_{name}"] = a
        aps[name] = nc.dram_tensor(f"in_{name}", a.shape, mybir.dt.from_np(a.dtype), kind="ExternalInput").ap()
    table = np.ascontiguousarray(np.concatenate(list(shape_constants().values()), axis=1))
    arrays["in_table"] = table
    cst = nc.dram_tensor("in_table", table.shape, F32, kind="ExternalInput").ap()
    out = nc.dram_tensor("out_0", (1, SEQ, 1024), F32, kind="ExternalOutput").ap()
    program(nc, aps, cst, out)
    r = run_bass_kernel_spmd(nc, [arrays], core_ids=[0])
    return r.results[0]["out_0"]
```

```python
from contextlib import ExitStack

import numpy as np

import concourse.bass as bass
from concourse import mybir

F32 = mybir.dt.float32
F32R = mybir.dt.float32r
I32 = mybir.dt.int32
U32 = mybir.dt.uint32
ALU = mybir.AluOpType
ACT = mybir.ActivationFunctionType
AX = mybir.AxisListType.X

P = 128
NM = 16
SEQ = 256
T = NM + SEQ
NRAW, NHI = 6, 4
BLK = 2048
ARN = 23400
NEG = -1e30
TAKEN = -3e38

C_IN = dict(gq=0, gk=1024, gv=2048, gz=3072, gb=4096, ga=4104, aq=4112, ak=5136, av=5392,
            iq=5648, ik=6160, iw=6224, gate_a=6232, gate_b=7256)


def shape_constants():
    i = np.arange(P)
    s, c = i[:, None], i[None, :]
    f = np.float32
    out = {}
    out["ident"] = (s == c).astype(f)
    out["ones"] = np.ones((P, P), f)
    out["U"] = (s <= c).astype(f)
    out["Us"] = (s < c).astype(f)
    same = s // 16 == c // 16
    out["Ub"] = (same & (s <= c)).astype(f)
    out["Ubs"] = (same & (s < c)).astype(f)
    out["OB"] = same.astype(f)
    for b in (1, 2, 4, 8, 16, 32, 64):
        out[f"m{b}"] = ((s // (2 * b) == c // (2 * b)) & (c % (2 * b) >= b) & (s % (2 * b) < b)).astype(f)
    for name, hd, half in (("R128", 128, 64), ("R64", 64, 32), ("R16", 64, 8)):
        r = np.zeros((P, P), f)
        for m in range(P):
            if m % hd < half:
                r[m + half, m] = -1
            elif m % hd < 2 * half:
                r[m - half, m] = 1
        out[name] = r
    out["hmask"] = (s // 16 == np.arange(8)[None, :]).astype(f)
    out["Rep"] = ((s == c % 16) & (s < 16)).astype(f)
    out["CB"] = np.concatenate([np.zeros((P, P), f), np.where(c <= s, 0, NEG).astype(f)], 1)
    pos = np.arange(T, dtype=f)
    for name, dim in (("A", 128), ("I", 64)):
        inv = f(10000.0) ** (-np.arange(0, dim, 2, dtype=f) / f(dim))
        ang = pos[None, :] * inv.astype(f)[i % (dim // 2)][:, None]
        out["cos" + name] = np.cos(ang).astype(f)
        out["sin" + name] = np.sin(ang).astype(f)
    inv2 = f(500000.0) ** (-np.arange(0, 16, 2, dtype=f) / f(16))
    out["inv2"] = np.where(i % 64 < 16, inv2[i % 8], 0).astype(f)[:, None]
    out["iota"] = np.tile(np.arange(2 * P, dtype=f), (P, 1))
    out["iota8"] = np.tile(np.arange(8, dtype=f), (P, 1))
    return out


def layout():
    off, n = {}, 0
    for k, v in shape_constants().items():
        off[k] = (n, v.shape[1])
        n += v.shape[1]
    return off, n


class Queue:

    def __init__(self, name, sem):
        self.name, self.sem, self.ops, self.n, self.seen = name, sem, [], 0, {}

    def wait(self, *tokens):
        for t in tokens:
            if t is None:
                continue
            if isinstance(t, list):
                self.wait(*t)
                continue
            sem, val = t
            if self.seen.get(id(sem), 0) < val:
                self.seen[id(sem)] = val
                self.ops.append(lambda e, sem=sem, val=val: e.wait_ge(sem, val))

    def __call__(self, fn, *tokens):
        self.wait(*tokens)
        self.n += 1
        self.ops.append(lambda e, fn=fn, done=self.sem: fn(e).then_inc(done, 1))
        return (self.sem, self.n)

    def quiet(self, fn, *tokens):
        self.wait(*tokens)
        self.ops.append(fn)

    def tick(self):
        fn = self.ops.pop()
        return self(fn)

    def last(self):
        return (self.sem, self.n) if self.n else None

    def play(self, e):
        for op in self.ops:
            op(e)

    def enter(self, sem):
        self.kept = (self.ops, self.n, self.sem, self.seen)
        self.ops, self.n, self.sem, self.seen = [], 0, sem, dict(self.seen)

    def leave(self, flag, *tokens):
        body = self.ops
        self.ops, self.n, self.sem, self.seen = self.kept
        self.wait(*tokens)

        def run(e):
            with e.If(e.value_load(flag, min_val=0, max_val=1) > 0):
                for op in body:
                    op(e)

        self.ops.append(run)


class Pool:

    def __init__(self, bufs):
        self.bufs, self.free, self.i = bufs, [[] for _ in bufs], 0
        self.out = set()

    def take(self):
        i = self.i
        assert i not in self.out
        self.out.add(i)
        self.i = (i + 1) % len(self.bufs)
        return i, self.bufs[i], self.free[i]

    def give(self, i, *tokens):
        self.free[i] = list(tokens)
        self.out.discard(i)


class Pair:

    def __init__(self, hi, lo):
        self.hi, self.lo = hi, lo


def program(nc, A, cst, out):
    off, ncst = layout()
    ctx = ExitStack()
    with ctx:
        made = {}

        def sb(name, shape, dt=F32):
            if name not in made:
                made[name] = ctx.enter_context(nc.sbuf_tensor(name, shape, dt))
            return made[name]

        def sem(name):
            if name not in made:
                made[name] = ctx.enter_context(nc.semaphore(name))
            return made[name]

        arena = sb("arena", [P, ARN])
        ring = sb("ring", [P, NRAW * BLK])
        ring_r = nc.alloc_sbuf_tensor_at("ring_r", [P, NRAW * BLK], F32R, offset=nc.lookup_mloc("ring").addr)
        arena_r = nc.alloc_sbuf_tensor_at("arena_r", [P, ARN], F32R, offset=nc.lookup_mloc("arena").addr)
        C = sb("consts", [P, ncst])
        vec = sb("vec", [P, 224])
        sm = sb("sm", [P, 512])
        bank = [ctx.enter_context(nc.psum_tensor(f"bank{i}", [P, 512], F32)) for i in range(8)]
        _, plan = emit(nc, A, cst, out, sb, sem, arena, arena_r, ring, ring_r, C, vec, sm, bank, off, None)
        (PE, V, S, G, SP), _ = emit(nc, A, cst, out, sb, sem, arena, arena_r, ring, ring_r, C, vec, sm, bank, off, plan)

        block = ctx.enter_context(nc.Block())

        @block.sync
        def _(e):
            SP.play(e)

        @block.tensor
        def _(e):
            PE.play(e)

        @block.vector
        def _(e):
            V.play(e)

        @block.scalar
        def _(e):
            S.play(e)

        @block.gpsimd
        def _(e):
            G.play(e)


def emit(nc, A, cst, out, sb, sem, arena, arena_r, ring, ring_r, C, vec, sm, bank, off, plan):
    def cc(name, a=0, b=None):
        o, n = off[name]
        return C[:, o + a:o + (n if b is None else b)]

    PE = Queue("PE", sem("s_pe"))
    V = Queue("V", sem("s_dve"))
    S = Queue("S", sem("s_act"))
    G = Queue("G", sem("s_pool"))
    SP = Queue("SP", None)
    s_slot = [sem(f"s_slot{i}") for i in range(NRAW)]
    n_slot = [0] * NRAW
    s_in = [sem(f"s_in{i}") for i in range(9)]
    n_in = [0] * 9
    s_out = sem("s_out")
    PS = Pool([b[:, :] for b in bank[:7]])
    hook = [None]
    RAW = Pool(list(range(NRAW)))
    HI = Pool(list(range(NHI)))

    top = [0]

    def shaped(a, dims):
        if len(dims) == 2:
            return a.rearrange("p (a b) -> p a b", a=dims[0])
        if len(dims) == 3:
            return a.rearrange("p (a b c) -> p a b c", a=dims[0], b=dims[1])
        return a

    def carve(*dims, of=arena):
        n = int(np.prod(dims))
        a = of[:, top[0]:top[0] + n]
        top[0] += n
        assert top[0] <= ARN, top[0]
        return shaped(a, dims)

    def carve_pair(*dims):
        return Pair(carve(*dims, of=arena_r), carve(*dims, of=arena_r))

    hi_ring = sb("hi_ring", [P, NHI * BLK], F32R)
    XH = sb("XH", [P, 8, T], F32R)
    XL = sb("XL", [P, 8, T], F32R)
    nX = Pair(XH[:, :, :], XL[:, :, :])
    X = Pair(XH[:, :, 0:SEQ], XL[:, :, 0:SEQ])

    smtop = [0]

    def small(n):
        a = sm[:, smtop[0]:smtop[0] + n]
        smtop[0] += n
        assert smtop[0] <= 512
        return a

    def everyone():
        return [q.last() for q in (PE, V, S, G)]

    def load_in(which, dst, src, *tokens):
        n_in[which] += 16
        SP.quiet(lambda e: e.dma_start(dst, src).then_inc(s_in[which], 16), *tokens)
        return (s_in[which], n_in[which])

    W = dict(rec=[[]], seg=0, at=0, dma=[], cut=[])

    def block_load(i):
        parts, (k, n) = W["list"][i]
        ri, _, free = RAW.take()
        a = ri * BLK
        block = shaped(ring[:, a:a + k * n], (k, n))
        for pick, src in parts:
            n_slot[ri] += 16
            SP.quiet(lambda e, d=pick(block), s=src, done=s_slot[ri]: e.dma_start(d, s).then_inc(done, 16), *free)
        W["dma"].append((ri, (s_slot[ri], n_slot[ri])))

    def block_split(i):
        _, (k, n) = W["list"][i]
        ri, t = W["dma"][i]
        hi_, _, free = HI.take()
        a, b = ri * BLK, hi_ * BLK
        m = k * n
        t1 = S(lambda e: e.copy(hi_ring[:, b:b + m], ring[:, a:a + m]), t, *free)
        t2 = V(lambda e: e.tensor_tensor(ring_r[:, a:a + m], ring[:, a:a + m], hi_ring[:, b:b + m].bitcast(F32), ALU.subtract), t1)
        W["cut"].append((ri, hi_, Pair(shaped(hi_ring[:, b:b + m], (k, n)), shaped(ring_r[:, a:a + m], (k, n))), [t1, t2]))

    def stream(parts, shape):
        i = W["at"]
        W["at"] += 1
        rec = W["rec"][W["seg"]]
        rec.append((parts, shape))
        W["list"] = plan[W["seg"]] if plan is not None else rec
        while len(W["dma"]) < min(len(W["list"]), i + (NRAW if plan is not None else 1)):
            block_load(len(W["dma"]))
        while len(W["cut"]) < min(len(W["list"]), i + 3):
            block_split(len(W["cut"]))
        ri, hi_, pair, ts = W["cut"][i]
        return (ri, hi_), pair, ts

    def release(slots, t):
        RAW.give(slots[0], t)
        HI.give(slots[1], t)

    def new_segment():
        W["rec"].append([])
        W.update(seg=W["seg"] + 1, at=0, dma=[], cut=[])

    def mm3(ps, a, b, first, last):
        PE.quiet(lambda e: e.matmul(ps, a[0], b[0], start=first, stop=False))
        PE.quiet(lambda e: e.matmul(ps, a[0], b[1], start=False, stop=False))
        f = lambda e: e.matmul(ps, a[1], b[0], start=False, stop=last)
        if last:
            return PE(f)
        PE.quiet(f)

    def source(w, k0, nk, c0, gw):
        return w[k0 * P:(k0 + nk) * P, c0:c0 + gw].rearrange("(k p) n -> p k n", p=P)

    def whole(v):
        return v

    def wait_for(t_x, k, K):
        PE.wait(t_x[k] if isinstance(t_x, list) and len(t_x) == K else t_x)

    def lin_steps(parts, gw, x, x0, n, t_x, evac, j0=0):
        slots, w, tw = stream(parts, (8, gw))
        for mi in range(gw // P):
            bi, ps, free = PS.take()
            PE.wait(tw, free)
            for k in range(8):
                wait_for(t_x, k, 8)
                t = mm3(ps[:, 0:n], (w.hi[:, k, mi * P:(mi + 1) * P], w.lo[:, k, mi * P:(mi + 1) * P]),
                        (x.hi[:, k, x0:x0 + n], x.lo[:, k, x0:x0 + n]), k == 0, k == 7)
            if mi == gw // P - 1:
                release(slots, t)
            if hook[0] is not None:
                hook[0]()
            PS.give(bi, evac(j0 + mi, ps[:, 0:n], t))
            yield

    def lin_block(*args, **kw):
        for _ in lin_steps(*args, **kw):
            pass

    def lin(w, K, c0, ncols, x, n, t_x, evac, x0=0, j0=0):
        KT = K // P
        for g0 in range(0, ncols, 256):
            gw = min(256, ncols - g0)
            if KT == 8:
                lin_block([(whole, source(w, 0, 8, c0 + g0, gw))], gw, x, x0, n, t_x, evac, j0 + g0 // P)
                continue
            banks = [PS.take() for _ in range(gw // P)]
            for kb in range(0, KT, 8):
                nk = min(8, KT - kb)
                slots, wp, tw = stream([(whole, source(w, kb, nk, c0 + g0, gw))], (nk, gw))
                for mi in range(gw // P):
                    bi, ps, free = banks[mi]
                    PE.wait(tw, free)
                    for k in range(nk):
                        kk = kb + k
                        wait_for(t_x, kk, KT)
                        t = mm3(ps[:, 0:n], (wp.hi[:, k, mi * P:(mi + 1) * P], wp.lo[:, k, mi * P:(mi + 1) * P]),
                                (x.hi[:, kk, x0:x0 + n], x.lo[:, kk, x0:x0 + n]), kk == 0, kk == KT - 1)
                    if kb + nk < KT and mi == gw // P - 1:
                        t = PE.tick()
                    if mi == gw // P - 1:
                        release(slots, t)
                    if kb + nk == KT:
                        if hook[0] is not None:
                            hook[0]()
                        PS.give(bi, evac(j0 + g0 // P + mi, ps[:, 0:n], t))

    def tok_block(w, tw, ncols, x, x0, m, t_x, last):
        bi, ps, free = PS.take()
        PE.wait(tw, free)
        for k in range(8):
            wait_for(t_x, k, 8)
            t = mm3(ps[0:m, 0:ncols], (x.hi[:, k, x0:x0 + m], x.lo[:, k, x0:x0 + m]), (w.hi[:, k, :], w.lo[:, k, :]), k == 0, k == 7)
        return bi, ps[0:m, 0:ncols], t

    def lin_tok(view, ncols, lhs, nk, t_w, t_lhs, m):
        bi, ps, free = PS.take()
        PE.wait(t_w, t_lhs, free)
        for k in range(nk):
            f = lambda e, ps=ps, k=k, a=lhs(k), b=view(k): e.matmul(ps[0:m, 0:ncols], a, b, start=(k == 0), stop=(k == nk - 1))
            if k == nk - 1:
                t = PE(f)
            else:
                PE.quiet(f)
        return bi, ps[0:m, 0:ncols], t

    def mm1(ps, lhsT, rhs, *tokens, start=True, stop=True):
        return PE(lambda e, ps=ps: e.matmul(ps, lhsT, rhs, start=start, stop=stop), *tokens)

    def split(src, hi, lo, *tokens):
        t1 = S(lambda e: e.copy(hi, src), *tokens)
        return V(lambda e: e.tensor_tensor(lo, src, hi.bitcast(F32), ALU.subtract), t1)

    ident = cc("ident")
    ones = cc("ones")

    top_g = top[0]
    xin = carve(2, 1024)
    min_ = carve(1024)[0:NM, :]
    rows = carve(2, P)
    t_id = load_in(0, C[:, 0:2 * P], cst[:, 0:2 * P])
    t_x = load_in(1, xin, A["x"][0].rearrange("(a p) d -> p a d", p=P))
    t_x = load_in(1, min_, A["meta_tokens"])
    wr = small(64).rearrange("p (a b) -> p a b", a=8)
    vrows, nv = {}, 0
    for key in ("pre_mix_norm", "post_mix_norm", "pre_mlp_norm", "post_mlp_norm"):
        vrows[key] = nv
        t_v = load_in(2, rows[nv:nv + 8, 0, :], A[key].rearrange("l (a p) -> (l a) p", p=P))
        nv += 8
    for key in ("ln1_g_2", "ln1_b_2", "ln2_g_2", "ln2_b_2"):
        vrows[key] = nv
        t_v = load_in(2, rows[nv:nv + 16, 0, :], A[key].rearrange("l (a p) -> (l a) p", p=P))
        nv += 16
    vrows["conv_a_2"] = nv
    t_v = load_in(2, rows[nv:nv + 18, 0, :], A["conv_a_2"].rearrange("l j (a p) -> (l j a) p", p=P))
    nv += 18
    vrows["gdn_norm"] = nv
    t_v = load_in(2, rows[nv:nv + 1, 0, :], A["gdn_norm"])
    nv += 1
    t_v = load_in(2, rows[0:96, 1, :], A["conv_w"].rearrange("l j (a p) -> (l j a) p", p=P))
    vrows["conv_w"] = 128
    dtb = small(8)
    alog = small(8)
    t_g = load_in(3, dtb, A["dt_bias"].to_broadcast([P, 8]))
    t_g = load_in(3, alog, A["a_log"].to_broadcast([P, 8]))
    posi = sb("posi", [P, SEQ], I32)
    t_pos = load_in(4, posi[:, :], A["positions_2"].to_broadcast([P, SEQ]))
    win = A["w_in"][0]
    t_wr = load_in(7, wr, A["w_router_2"][0].rearrange("(k p) n -> p k n", p=P))
    eps6, eps5, one1 = small(1), small(1), small(1)
    zero1 = small(1)
    for ap, v in ((eps6, 1e-6), (eps5, 1e-5), (one1, 1.0), (zero1, 0.0)):
        t_eps = G(lambda e, ap=ap, v=v: e.memset(ap, v))

    for j, n in ((0, nv), (1, 96)):
        bi, ps, free = PS.take()
        t = PE(lambda e, ps=ps, j=j, n=n: e.transpose(ps[:, 0:n], rows[0:n, j, :], cc("ident")[0:n, 0:n]), t_v, t_id, free)
        t_vec = V(lambda e, ps=ps, j=j, n=n: e.tensor_copy(vec[:, 128 * j:128 * j + n], ps[:, 0:n]), t)
        PS.give(bi, t_vec)

    def vcol(name, i):
        return vec[:, vrows[name] + i:vrows[name] + i + 1]

    hT = carve(8, T)
    t_h = []
    for k in range(8):
        bi, ps, free = PS.take()
        PE.wait(t_x, t_id, free)
        PE.quiet(lambda e, ps=ps, k=k: e.transpose(ps[:, 0:NM], min_[:, k * P:(k + 1) * P], cc("ident")[0:NM, 0:NM]))
        PE.quiet(lambda e, ps=ps, k=k: e.transpose(ps[:, NM:NM + P], xin[:, 0, k * P:(k + 1) * P], ident))
        t = PE(lambda e, ps=ps, k=k: e.transpose(ps[:, NM + P:T], xin[:, 1, k * P:(k + 1) * P], ident))
        q = V if k % 2 else S
        if q is V:
            t = V(lambda e, ps=ps, k=k: e.tensor_copy(hT[:, k, :], ps[:, 0:T]), t)
        else:
            t = S(lambda e, ps=ps, k=k: e.copy(hT[:, k, :], ps[:, 0:T]), t)
        PS.give(bi, t)
        t_h.append(t)

    class Tally:

        free = None

        def __init__(self, n, bufs, guard):
            self.n, self.pend, self.i, self.pool, self.guard = n, [], 0, Pool(bufs), guard

        def add(self, ap, t, then=None):
            self.pend.append((ap, t, then))

        def square(self, ap, t):
            i, b, free = self.pool.take()
            t = S(lambda e: e.activation(b, ap, ACT.Square), t, free, self.guard)
            self.add(b, t, i)

        def flush(self):
            for ap, t, i in self.pend:
                f = lambda e, a=self.i, ap=ap: e.matmul(bank[7][:, 0:self.n], ones, ap, start=(a == 0), stop=(a == 7))
                self.t = PE(f, t, t_id, Tally.free if self.i == 0 else None)
                if i is not None:
                    self.pool.give(i, self.t)
                self.i += 1
            self.pend = []

        def mean(self, dst):
            self.flush()
            Tally.free = S(lambda e: e.activation(dst, bank[7][:, 0:self.n], ACT.Copy, scale=1.0 / 1024), self.t, self.guard)
            return Tally.free

        def inv_root(self, eps, dst):
            self.flush()
            Tally.free = S(lambda e: e.activation(dst, bank[7][:, 0:self.n], ACT.Sqrt, bias=eps, scale=1.0 / 1024), self.t, t_eps, self.guard)
            return V(lambda e: e.reciprocal(dst, dst), Tally.free)

    def tally_at(at, n, guard):
        m = top[0]
        top[0] = at
        bufs = [carve(n) for _ in range(4)]
        r = carve(n)
        top[0] = m
        return Tally(n, bufs, guard), r

    def rms_scaled(src, n, gname, gi, at, tl, r, guard, put):
        m = top[0]
        top[0] = at
        tmp = carve(8, n)
        top[0] = m
        t_r = tl.inv_root(eps6, r)
        res = []
        for k in range(8):
            t = V(lambda e, k=k: e.scalar_tensor_tensor(out=tmp[:, k, :], in0=src[:, k, :], scalar=vcol(gname, gi + k), in1=r, op0=ALU.mult, op1=ALU.mult), t_r, t_vec, guard)
            res.append(put(k, tmp[:, k, :], t))
        return res

    def into(x):
        def put(k, src, t):
            t = S(lambda e: e.copy(x.hi[:, k, :], src), t)
            return (G if k % 2 else V)(lambda e: e.tensor_tensor(x.lo[:, k, :], src, x.hi[:, k, :].bitcast(F32), ALU.subtract), t)
        return put

    tl, rv = tally_at(top[0], T, None)
    for k in range(8):
        tl.square(hT[:, k, :], t_h[k])
        tl.flush()
    t_n = rms_scaled(hT, T, "pre_mix_norm", 0, top[0] + 5 * T, tl, rv, None, into(nX))
    t_in_done = everyone()

    top[0] = top_g
    gq = carve(8, T)
    g_kv = top[0]
    gk = carve(8, T)
    gv = carve(8, T)
    mark_gdn = top[0]
    D = shaped(arena[:, g_kv:g_kv + 17 * P], (17, P))
    DT = shaped(arena[:, g_kv + 17 * P:g_kv + 34 * P], (17, P))
    dec = carve(17, P)
    AT = carve(17, P)
    nkb = carve(17, P)
    kta = carve(17, P)
    vb = carve(17, P)
    S1 = carve(8, P)
    S2 = carve(8, P)
    m_mt = top[0]
    MTs = Pool([carve(4, P) for _ in range(3)])
    Ys = Pool([carve(4, P) for _ in range(3)])
    ebs = [S1[:, 0:4, :], S1[:, 4:8, :], MTs.bufs[0], MTs.bufs[1]]
    kmeta, vmeta = S2[:, 0, :], S2[:, 1, :]
    smallT = shaped(S2[:, 2:8, :].rearrange("p a b -> p (a b)")[:, 0:2 * T], (2, T))
    top[0] = m_mt + 8 * P
    xpads = [carve(T + 3) for _ in range(3)]
    sqs = [carve(T) for _ in range(3)]
    rs_ = [carve(T) for _ in range(4)]
    XP, SQ, RR = Pool(xpads), Pool(sqs), Pool(rs_)
    t_z = None
    for x in xpads:
        t_z = G(lambda e, x=x: e.memset(x[:, 0:3], 0.0), t_in_done)

    at = small(24)
    g3 = small(24)
    b3 = small(24)
    iw = small(16)
    t_at0 = V(lambda e: e.memset(at, 0.0))
    t_b30 = V(lambda e: e.memset(b3, 0.0))
    t_sm = []

    def evac_small(j, ps, t):
        n = (16, 8)[j]
        t = V(lambda e: e.tensor_copy(smallT[0:n, j, :], ps[0:n, :]), t, t_in_done)
        t_sm.append(t)
        return t

    lin_block([(lambda v: v[:, :, 0:P], source(win, 0, 8, C_IN["gb"], P)),
               (lambda v: v[:, :, P:2 * P], source(win, 0, 8, C_IN["iw"], P))], 256, nX, 0, T, t_n, evac_small)
    t_c = load_in(6, C[:, 2 * P:], cst[:, 2 * P:])
    for q_ in (PE, V, S, G):
        q_.wait(t_c)
    t_g3 = []
    for c, t0, n in ((0, 16, P), (1, 16 + P, P), (2, 0, NM)):
        bi, ps, free = PS.take()
        t = PE(lambda e, ps=ps, t0=t0, n=n: e.transpose(ps[0:n, 0:16], smallT[0:16, 0, t0:t0 + n], cc("ident")[0:16, 0:16]), t_sm, free)
        if c < 2:
            t = PE(lambda e, ps=ps, t0=t0, n=n: e.transpose(ps[0:n, 16:24], smallT[0:8, 1, t0:t0 + n], cc("ident")[0:8, 0:8]), t_sm)
        t = S(lambda e, ps=ps, c=c, n=n: e.activation(b3[0:n, 8 * c:8 * c + 8], ps[0:n, 0:8], ACT.Sigmoid), t, t_b30)
        ts = [t, V(lambda e, ps=ps, c=c, n=n: e.tensor_tensor(at[0:n, 8 * c:8 * c + 8], ps[0:n, 8:16], dtb[0:n, :], ALU.add), t, t_g, t_at0)]
        if c < 2:
            ts.append(V(lambda e, ps=ps, c=c: e.tensor_scalar(iw[:, 8 * c:8 * c + 8], ps[:, 16:24], float(512 ** -0.5), None, ALU.mult), t))
        PS.give(bi, *ts)
        t_g3 += ts
    t_iw = t_g3
    na, ea = small(24), small(24)
    t = V(lambda e: e.tensor_scalar(na, at, -1.0, None, ALU.mult), t_g3)
    t = V(lambda e: e.tensor_tensor(na, na, at, ALU.min), t)
    t = S(lambda e: e.activation(ea, na, ACT.Exp), t)
    t = S(lambda e: e.activation(ea, ea, ACT.Ln, bias=one1), t, t_eps)
    t_al = S(lambda e: e.activation(alog, alog, ACT.Exp), t_g)
    t = V(lambda e: e.scalar_tensor_tensor(out=g3, in0=at, scalar=0.0, in1=ea, op0=ALU.max, op1=ALU.add), t)
    for c in range(3):
        t_g3 = V(lambda e, c=c: e.scalar_tensor_tensor(out=g3[:, 8 * c:8 * c + 8], in0=g3[:, 8 * c:8 * c + 8], scalar=-1.0, in1=alog, op0=ALU.mult, op1=ALU.mult), t, t_al)

    gG, gB, GC, GL = small(17), small(17), small(17), small(17)
    eg, ekt, egl, nbe = small(17), small(17), small(17), small(17)
    gmb = small(16)
    hm = small(16)
    t = V(lambda e: e.tensor_copy(gG[:, 0:16].rearrange("p (h c) -> p c h", c=2), g3[:, 0:16].rearrange("p (c h) -> p c h", c=2)), t_g3)
    t2 = V(lambda e: e.tensor_copy(gB[:, 0:16].rearrange("p (h c) -> p c h", c=2), b3[:, 0:16].rearrange("p (c h) -> p c h", c=2)), t_iw)
    t3 = V(lambda e: e.tensor_copy(gmb[:, 0:8], g3[:, 16:24]), t_g3)
    t4 = V(lambda e: e.tensor_copy(gmb[:, 8:16], b3[:, 16:24]), t_iw)
    bi, ps, free = PS.take()
    t = mm1(ps[:, 0:16], cc("Rep")[0:NM, :], gmb[0:NM, :], t, t2, t3, t4, free)
    t5 = V(lambda e, ps=ps: e.tensor_tensor(hm[:, 0:8], ps[:, 0:8], cc("hmask"), ALU.mult), t)
    t6 = V(lambda e, ps=ps: e.tensor_tensor(hm[:, 8:16], ps[:, 8:16], cc("hmask"), ALU.mult), t)
    PS.give(bi, t5, t6)
    t = V(lambda e: e.tensor_reduce(gG[:, 16:17], hm[:, 0:8], AX, ALU.add), t5)
    t_gb = V(lambda e: e.tensor_reduce(gB[:, 16:17], hm[:, 8:16], AX, ALU.add), t6)
    bi, ps, free = PS.take()
    mm1(ps[:, 0:16], cc("U"), gG[:, 0:16], t_gb, free)
    mm1(ps[:, 16:17], cc("Ub"), gG[:, 16:17])
    mm1(ps[:, 17:33], ones, gG[:, 0:16])
    t = mm1(ps[:, 33:34], cc("OB"), gG[:, 16:17])
    t1 = V(lambda e, ps=ps: e.tensor_copy(GC, ps[:, 0:17]), t)
    t2 = V(lambda e, ps=ps: e.tensor_copy(GL, ps[:, 17:34]), t)
    PS.give(bi, t1, t2)
    t3 = V(lambda e: e.tensor_tensor(ekt, GL, GC, ALU.subtract), t2)
    ta = S(lambda e: e.activation(ekt, ekt, ACT.Exp), t3)
    tb = S(lambda e: e.activation(eg, GC, ACT.Exp), t1)
    tc = S(lambda e: e.activation(egl, GL, ACT.Exp), t2)
    td = V(lambda e: e.scalar_tensor_tensor(out=nbe, in0=gB, scalar=-1.0, in1=eg, op0=ALU.mult, op1=ALU.mult), tb)
    t_gates = [ta, tb, tc, td]

    waiting = []

    def late(fn=None):
        for f in waiting:
            f()
        waiting[:] = [fn] if fn is not None else []

    def conv_block(c0, w0, dst, i, done):

        def evac(j, ps, t):
            xi, xp, xfree = XP.take()
            t1 = S(lambda e, ps=ps: e.copy(xp[:, 3:3 + T], ps), t, xfree, t_z)
            d = dst[:, j, :]
            tv = V(lambda e: e.tensor_scalar(d, xp[:, 0:T], vcol("conv_w", w0 + j), None, ALU.mult), t1, t_vec, t_in_done)
            for u in range(1, 4):
                tv = V(lambda e, u=u: e.scalar_tensor_tensor(out=d, in0=xp[:, u:u + T], scalar=vcol("conv_w", 24 * u + w0 + j), in1=d, op0=ALU.mult, op1=ALU.add), tv)
            XP.give(xi, tv)
            late(lambda: done.__setitem__(j, S(lambda e: e.activation(d, d, ACT.Silu), tv)))
            return t1

        lin(win, 1024, c0 + 256 * i, 256, nX, T, t_n, evac, j0=2 * i)

    def l2_four(dst, i, norm, done):
        late()
        st = []
        for j in range(4 * i, 4 * i + 4):
            si, sq, sfree = SQ.take()
            ri, r, rfree = RR.take()
            d = dst[:, j, :]
            t = G(lambda e, d=d, sq=sq: e.tensor_tensor(sq, d, d, ALU.mult), done[j], sfree)
            bi, ps, free = PS.take()
            t = mm1(ps[:, 0:T], ones, sq, t, t_id, free)
            SQ.give(si, t)
            st.append([j, d, ri, r, rfree, t, bi, ps])
        for x in st:
            j, d, ri, r, rfree, t, bi, ps = x
            x[5] = S(lambda e, r=r, ps=ps: e.activation(r, ps[:, 0:T], ACT.Sqrt, bias=eps6), t, t_eps, rfree)
            PS.give(bi, x[5])

        def finish():
            for j, d, ri, r, rfree, t, bi, ps in st:
                t = V(lambda e, r=r: e.reciprocal(r, r), t, rfree)
                done[j] = V(lambda e, d=d, r=r: e.scalar_tensor_tensor(out=d, in0=d, scalar=norm, in1=r, op0=ALU.mult, op1=ALU.mult), t)
                RR.give(ri, done[j])

        return finish

    groups = [list(range(4 * i, 4 * i + 4)) for i in range(4)] + [[16]]

    def tok(x, m):
        if m == 16:
            return kmeta if x is gk else vmeta
        return x[:, m // 2, NM + P * (m % 2):NM + P * (m % 2) + P]

    def bc(ap, n):
        return ap.unsqueeze(1).to_broadcast([P, n, P])

    t_kv, t_s, t_i, t_AT, t_att, t_qd, t_eb = {}, {}, {}, {}, {}, {}, {}
    t_k, t_v_, t_q = {}, {}, {}
    fl = lambda a, g: a[:, g[0]:g[-1] + 1, :].rearrange("p a b -> p (a b)")

    def decays(g):
        n = len(g) * P
        gl = slice(g[0], g[-1] + 1)
        msk = (cc("Ub"), cc("Ubs")) if g[0] == 16 else (cc("U"), cc("Us"))
        bi, ps, free = PS.take()
        PE.wait(free, t_gb)
        for x, m in enumerate(g):
            t = mm1(ps[:, x * P:(x + 1) * P], gG[:, m:m + 1].to_broadcast([P, P]), cc("Ub" if m == 16 else "U"))
        if g[0] != 16:
            eb = ebs[g[0] // 4]
            t = t_eb[g[0]] = S(lambda e, ps=ps: e.activation(eb.rearrange("p a b -> p (a b)"), ps, ACT.Exp), t, t_in_done)
        for x, m in enumerate(g):
            td = V(lambda e, ps=ps, x=x, m=m: e.tensor_scalar(dec[:, m, :], ps[:, x * P:(x + 1) * P], GC[:, m:m + 1], 0.0, ALU.subtract, ALU.min), t, t_gates, t_in_done)
        PS.give(bi, td)
        td = S(lambda e: e.activation(dec[:, gl, :], dec[:, gl, :], ACT.Exp), td)
        t_s[g[0]] = G(lambda e: e.tensor_tensor(AT[:, gl, :], dec[:, gl, :], bc(msk[1], len(g)), ALU.mult), td, t_in_done)
        t_i[g[0]] = G(lambda e: e.tensor_tensor(dec[:, gl, :], dec[:, gl, :], bc(msk[0], len(g)), ALU.mult), t_s[g[0]])

    def betas(g):
        n = len(g) * P
        bi, ps, free = PS.take()
        PE.wait(free)
        for x, m in enumerate(g):
            t = mm1(ps[:, x * P:(x + 1) * P], gB[:, m:m + 1].to_broadcast([P, P]), ident)
        t_s[g[0]] = V(lambda e, ps=ps: e.tensor_tensor(fl(AT, g), fl(AT, g), ps[:, 0:n], ALU.mult), t, t_s[g[0]])
        PS.give(bi, t_s[g[0]])

    def keys(g):
        n = len(g) * P
        need = t_meta if g[0] == 16 else [t_k[g[0] // 2], t_k[g[0] // 2 + 1]]
        bi, ps, free = PS.take()
        PE.wait(need, free)
        for x, m in enumerate(g):
            t = PE(lambda e, ps=ps, x=x, m=m: e.transpose(ps[:, x * P:(x + 1) * P], tok(gk, m), ident))
        ts = []
        for x, m in enumerate(g):
            ts.append(S(lambda e, ps=ps, x=x, m=m: e.activation(nkb[:, m, :], ps[:, x * P:(x + 1) * P], ACT.Copy, scale=nbe[:, m:m + 1]), t, t_gates, t_in_done))
        bk, pk, t_nkb = bi, ps, ts[-1]
        bi, ps, free = PS.take()
        PE.wait(free)
        for x, m in enumerate(g):
            t = mm1(ps[:, x * P:(x + 1) * P], tok(gk, m), tok(gk, m))
        t_AT[g[0]] = V(lambda e, ps=ps: e.tensor_tensor(fl(AT, g), fl(AT, g), ps[:, 0:n], ALU.mult), t, t_s[g[0]])
        PS.give(bi, t_AT[g[0]])
        for x, m in enumerate(g):
            ts.append(V(lambda e, x=x, m=m: e.tensor_scalar(kta[:, m, :], pk[:, x * P:(x + 1) * P], ekt[:, m:m + 1], None, ALU.mult), t_nkb, t_gates, t_in_done))
        PS.give(bk, *ts)
        t_kv[g[0]] = ts

    def values(g):
        need = t_meta if g[0] == 16 else [t_v_[g[0] // 2], t_v_[g[0] // 2 + 1]]
        bi, ps, free = PS.take()
        PE.wait(need, free)
        for x, m in enumerate(g):
            t = PE(lambda e, ps=ps, x=x, m=m: e.transpose(ps[:, x * P:(x + 1) * P], tok(gv, m), ident))
        for x, m in enumerate(g):
            t_kv[g[0]].append(S(lambda e, ps=ps, x=x, m=m: e.activation(vb[:, m, :], ps[:, x * P:(x + 1) * P], ACT.Copy, scale=gB[:, m:m + 1]), t, t_gb, t_in_done))
        PS.give(bi, t_kv[g[0]][-1])

    def queries(g):
        bi, ps, free = PS.take()
        PE.wait(free, t_q[g[0] // 2], t_q[g[0] // 2 + 1])
        for x, m in enumerate(g):
            t2 = mm1(ps[:, x * P:(x + 1) * P], tok(gk, m), tok(gq, m))
        t_att[g[0]] = V(lambda e, ps=ps: e.tensor_tensor(fl(dec, g), fl(dec, g), ps, ALU.mult), t_i[g[0]], t2)
        PS.give(bi, t_att[g[0]])
        h0 = g[0] // 2
        qv = gq[:, h0:h0 + 2, NM:T]
        eb = ebs[g[0] // 4].rearrange("p (h c) b -> p h (c b)", c=2)
        t_qd[g[0]] = G(lambda e: e.tensor_tensor(qv, qv, eb, ALU.mult), t_eb[g[0]], t2)

    for i in range(5):
        decays(groups[i])
        if i:
            betas(groups[i - 1])
    betas(groups[4])
    for i in range(4):
        conv_block(C_IN["gk"], 8, gk, i, t_k)
    l2_four(gk, 0, 1.0, t_k)()
    for i in range(4):
        conv_block(C_IN["gq"], 0, gq, i, t_q)
        if i == 1:
            fin = l2_four(gk, 1, 1.0, t_k)
            keys(groups[1])
            fin()
            t_meta = V(lambda e: e.tensor_copy(kmeta.rearrange("p (h t) -> p h t", h=8), gk[:, :, 0:NM]), *t_k.values(), t_in_done)
        elif i == 3:
            fin = l2_four(gq, 0, float(128 ** -0.5), t_q)
            keys(groups[3])
            fin()
        else:
            keys(groups[i])
    for i in range(4):
        conv_block(C_IN["gv"], 16, gv, i, t_v_)
        if i == 0:
            keys(groups[4])
        elif i == 1:
            fin = l2_four(gq, 1, float(128 ** -0.5), t_q)
            values(groups[0])
            fin()
        else:
            values(groups[i - 1])
        queries(groups[i])
    late()
    values(groups[3])
    t_meta = V(lambda e: e.tensor_copy(vmeta.rearrange("p (h t) -> p h t", h=8), gv[:, :, 0:NM]), *t_v_.values(), t_in_done)
    values(groups[4])

    g_inv = everyone()
    t_D = {}
    MTs.free = [g_inv, g_inv, g_inv]
    Ys.free = [g_inv, g_inv, g_inv]
    steps = [(b, g) for b in (1, 2, 4, 8, 16, 32, 64) for g in groups if b < 16 or g[0] != 16]
    live = {}

    def inv_a(i):
        b, g = steps[i]
        gl, k, n = slice(g[0], g[-1] + 1), len(g), len(g) * P
        mi, mt, mfree = MTs.take()
        t = G(lambda e: e.tensor_tensor(mt[:, 0:k, :], AT[:, gl, :], bc(cc(f"m{b}"), k), ALU.mult), t_AT[g[0]], mfree)
        bi, ps, free = PS.take()
        if b == 1:
            PE.wait(free, t)
            for x, m in enumerate(g):
                t2 = PE(lambda e, ps=ps, x=x: e.transpose(ps[:, x * P:(x + 1) * P], mt[:, x, :], ident))
            t1 = V(lambda e: e.tensor_tensor(DT[:, gl, :], bc(ident, k), mt[:, 0:k, :], ALU.subtract), t, g_inv)
            t2 = V(lambda e: e.tensor_tensor(D[:, gl, :], bc(ident, k), ps[:, 0:n].rearrange("p (a b) -> p a b", b=P), ALU.subtract), t2)
            PS.give(bi, t2)
            MTs.give(mi, t2)
            t_D[g[0]] = (t2, t1)
            return
        PE.wait(free, t, *t_D[g[0]])
        for x, m in enumerate(g):
            t = mm1(ps[:, x * P:(x + 1) * P], mt[:, x, :], D[:, m, :])
        MTs.give(mi, t)
        yi, y, yfree = Ys.take()
        t = S(lambda e, ps=ps: e.copy(y[:, 0:k, :].rearrange("p a b -> p (a b)"), ps[:, 0:n]), t, yfree)
        PS.give(bi, t)
        live[i] = (yi, y, t)

    def inv_b(i):
        b, g = steps[i]
        if b == 1:
            return
        gl, n = slice(g[0], g[-1] + 1), len(g) * P
        yi, y, ty = live.pop(i)
        lastlevel = (b == 64) or (g[0] == 16 and b == 8)
        bi, ps, free = PS.take()
        PE.wait(free, ty)
        for x, m in enumerate(g):
            t = mm1(ps[:, x * P:(x + 1) * P], y[:, x, :], DT[:, m, :])
        if not lastlevel:
            bj, ps2, free2 = PS.take()
            PE.wait(free2)
            for x, m in enumerate(g):
                t = mm1(ps2[:, x * P:(x + 1) * P], DT[:, m, :], y[:, x, :])
        Ys.give(yi, t)
        fl = lambda a: a[:, gl, :].rearrange("p a b -> p (a b)")
        t2 = V(lambda e, ps=ps: e.tensor_tensor(fl(DT), fl(DT), ps[:, 0:n], ALU.subtract), t)
        PS.give(bi, t2)
        t1 = t2
        if not lastlevel:
            t1 = V(lambda e: e.tensor_tensor(fl(D), fl(D), ps2[:, 0:n], ALU.subtract), t)
            PS.give(bj, t1)
        t_D[g[0]] = (t1, t2)

    for i in range(len(steps) + 1):
        if i < len(steps):
            inv_a(i)
        if i >= 1:
            inv_b(i - 1)
    TT = DT
    t_T = [t_D[g[0]][1] for g in groups]
    t_kvs = [t for v in t_kv.values() for t in v]

    bi, ps, free = PS.take()
    t = mm1(ps[:, 0:P], TT[:, 16, :], vb[:, 16, :], t_T, t_kvs, free)
    vn = D
    t_vn = V(lambda e, ps=ps: e.tensor_copy(vn[:, 16, :], ps[:, 0:P]), t)
    PS.give(bi, t_vn)
    ktm = S2
    for h in range(8):
        t = G(lambda e, h=h: e.tensor_scalar(ktm[:, h, :], kta[:, 16, :], cc("hmask", h, h + 1), None, ALU.mult), t_kvs, t_T)
    t_S = []
    for q in range(2):
        bi, ps, free = PS.take()
        PE.wait(t, t_vn, free)
        for x in range(4):
            t2 = mm1(ps[:, x * P:(x + 1) * P], ktm[:, 4 * q + x, :], vn[:, 16, :])
        t_S.append(V(lambda e, ps=ps, q=q: e.tensor_copy(S1[:, 4 * q:4 * q + 4, :].rearrange("p a b -> p (a b)"), ps), t2))
        PS.give(bi, t_S[-1])
    t_ktm = t2
    t_w = {}
    wT = AT
    for g in groups[:4]:
        bi, ps, free = PS.take()
        PE.wait(free)
        for x, m in enumerate(g):
            t = mm1(ps[:, x * P:(x + 1) * P], nkb[:, m, :], TT[:, m, :])
        t_w[g[0]] = S(lambda e, ps=ps, g=g: e.copy(wT[:, g[0]:g[-1] + 1, :].rearrange("p a b -> p (a b)"), ps), t, [PE.last()], [G.last()])
        PS.give(bi, t_w[g[0]])
    oT = shaped(arena[:, m_mt:m_mt + 8 * SEQ], (8, SEQ))
    g_o1 = everyone()
    gz = shaped(arena[:, mark_gdn + 2 * 17 * P:mark_gdn + 2 * 17 * P + 8 * SEQ], (8, SEQ))
    t_zz = []

    def evac_z(j, ps, t):
        t = S(lambda e, ps=ps: e.activation(gz[:, j, :], ps, ACT.Silu), t, g_o1)
        t_zz.append(t)
        return t

    t_o = {}
    cur, t_cur = S1, {h: t_S[h // 4] for h in range(8)}
    for c in range(2):
        nxt = {}
        for hp in range(0, 8, 4):
            bi, ps, free = PS.take()
            PE.wait(free)
            for x in range(4):
                h = hp + x
                m = 2 * h + c
                mm1(ps[:, x * P:(x + 1) * P], TT[:, m, :], vb[:, m, :], stop=False)
                t = mm1(ps[:, x * P:(x + 1) * P], wT[:, m, :], cur[:, h, :], t_w[m // 4 * 4], t_cur[h], start=False)
            ms = [2 * (hp + x) + c for x in range(4)]
            vview = vn[:, ms[0]:ms[-1] + 1:2, :]
            tv = S(lambda e, ps=ps, vview=vview: e.copy(vview, ps.rearrange("p (a b) -> p a b", b=P)), t)
            PS.give(bi, tv)
            zi = 2 * c + hp // 4
            lin(win, 1024, C_IN["gz"] + 256 * zi, 256, nX, SEQ, t_n, evac_z, x0=NM, j0=2 * zi)
            if c == 0:
                bi, ps, free = PS.take()
                PE.wait(free, tv)
                for x in range(4):
                    t = mm1(ps[:, x * P:(x + 1) * P], kta[:, ms[x], :], vn[:, ms[x], :])
                for x in range(4):
                    h = hp + x
                    nxt[h] = V(lambda e, ps=ps, x=x, h=h, m=ms[x]: e.scalar_tensor_tensor(out=S2[:, h, :], in0=S1[:, h, :], scalar=egl[:, m:m + 1], in1=ps[:, x * P:(x + 1) * P], op0=ALU.mult, op1=ALU.add), t, t_ktm, t_cur[h])
                PS.give(bi, *nxt.values())
            bi, ps, free = PS.take()
            PE.wait(free, tv)
            for x in range(4):
                h, m = hp + x, ms[x]
                mm1(ps[:, x * P:(x + 1) * P], cur[:, h, :], tok(gq, m), t_qd[m // 4 * 4], stop=False)
                t = mm1(ps[:, x * P:(x + 1) * P], vn[:, m, :], dec[:, m, :], t_att[m // 4 * 4], start=False)
            to = S(lambda e, ps=ps, hp=hp, c=c: e.copy(oT[:, hp:hp + 4, P * c:P * c + P], ps.rearrange("p (a b) -> p a b", b=P)), t, g_o1)
            PS.give(bi, to)
            t_o[(c, hp)] = to
        cur, t_cur = S2, nxt
    yg = Pair(shaped(arena_r[:, g_kv:g_kv + 8 * SEQ], (8, SEQ)), shaped(arena_r[:, g_kv + 8 * SEQ:g_kv + 16 * SEQ], (8, SEQ)))
    t_y = []
    g1 = everyone()
    rr2 = [dec[:, 2 * j:2 * j + 2, :].rearrange("p a b -> p (a b)") for j in range(8)]
    sq2 = [AT[:, 2 * j:2 * j + 2, :].rearrange("p a b -> p (a b)") for j in range(8)]
    t_sq = [G(lambda e, h=h: e.tensor_tensor(sq2[h], oT[:, h, :], oT[:, h, :], ALU.mult), g1) for h in range(8)]

    def head_norms(q):
        S.wait(g1)
        ts = []
        for h in (2 * q, 2 * q + 1):
            bi, ps, free = PS.take()
            t = mm1(ps[:, 0:SEQ], ones, sq2[h], t_sq[h], free)
            ts.append(S(lambda e, ps=ps, h=h: e.activation(rr2[h], ps[:, 0:SEQ], ACT.Sqrt, bias=eps6, scale=1.0 / 128), t, t_eps))
            PS.give(bi, ts[-1])
        for h, t in zip((2 * q, 2 * q + 1), ts):
            o = oT[:, h, 0:SEQ]
            t = V(lambda e, h=h: e.reciprocal(rr2[h], rr2[h]), t)
            t = V(lambda e, h=h, o=o: e.scalar_tensor_tensor(out=o, in0=o, scalar=vcol("gdn_norm", 0), in1=rr2[h], op0=ALU.mult, op1=ALU.mult), t)
            t_go[h] = G(lambda e, h=h, o=o: e.tensor_tensor(o, o, gz[:, h, :], ALU.mult), t, t_zz)

    def head_splits(q):
        for h in (2 * q, 2 * q + 1):
            t_y.append(split(oT[:, h, :], yg.hi[:, h, :], yg.lo[:, h, :], t_go[h], g1))

    t_go = {}

    def ropes(items, guard, tmp):
        res = []
        for i in range(0, len(items), 3):
            part = []
            for d, rot, cosn, sinn, t_src in items[i:i + 3]:
                n = d.shape[-1]
                bi, ps, free = PS.take()
                t = mm1(ps[:, 0:n], rot, d, t_src, free)
                ti, tb, tfree = tmp.take()
                t1 = V(lambda e, ps=ps, tb=tb, n=n, sinn=sinn: e.tensor_tensor(tb[:, 0:n], ps[:, 0:n], sinn, ALU.mult), t, tfree, guard)
                PS.give(bi, t1)
                t2 = G(lambda e, d=d, cosn=cosn: e.tensor_tensor(d, d, cosn, ALU.mult), t, t_src)
                part.append((d, tb, n, ti, t1, t2))
            for d, tb, n, ti, t1, t2 in part:
                t3 = V(lambda e, d=d, tb=tb, n=n: e.tensor_tensor(d, d, tb[:, 0:n], ALU.add), t1, t2)
                tmp.give(ti, t3)
                res.append(t3)
        return res

    g2 = g1
    aq = shaped(arena[:, mark_gdn:mark_gdn + 2048], (8, SEQ))
    m_yd = mark_gdn + 2048
    top[0] = m_yd
    yd = carve_pair(8, SEQ)
    m_free = mark_gdn + 3 * 17 * P
    top[0] = m_free
    iq = carve(4, SEQ)
    ik = carve(T)
    ak = carve(2, T)
    av = carve(3, 256)
    mb = carve(2, T)
    m8 = carve(2, 8)
    work = carve(2, T)
    rtmp = Pool([carve(T) for _ in range(3)])
    m_att = top[0]
    rel = Pool([carve(T) for _ in range(3)])
    assert top[0] <= m_mt
    def roped(dst, scale=1.0):
        res = []

        def evac(j, ps, t):
            d = dst[:, j, :]
            t = S(lambda e, ps=ps: e.activation(d, ps, ACT.Copy, scale=scale), t, g2)
            res.append((d, t))
            return t
        return evac, res

    ev, raw_iq = roped(iq)
    for q in range(2):
        lin(win, 1024, C_IN["iq"] + 256 * q, 256, nX, SEQ, t_n, ev, x0=NM, j0=2 * q)
        head_norms(q)
        if q:
            head_splits(0)
    t_raw = {}

    def plain(dst, key, guard):
        t_raw[key] = []

        def evac(j, ps, t):
            t = S(lambda e: e.copy(dst[:, j, :], ps), t, guard)
            t_raw[key].append(t)
            return t
        return evac

    ik1 = ik.unsqueeze(1)
    lin_block([(lambda v: v[:, :, 0:64], source(win, 0, 8, C_IN["ik"], 64)),
               (lambda v: v[:, :, 64:128], source(win, 0, 8, C_IN["ik"], 64))], P, nX, 0, T, t_n, plain(ik1, "ik", g2))
    t_ik, *t_iq = ropes([(ik, cc("R64"), cc("cosI"), cc("sinI"), t_raw["ik"])] +
                        [(d, cc("R64"), cc("cosI", NM), cc("sinI", NM), t) for d, t in raw_iq], g2, rtmp)
    head_norms(2)
    head_splits(1)
    lin(win, 1024, C_IN["ak"], 256, nX, T, t_n, plain(ak, "ak", g2))
    head_norms(3)
    head_splits(2)
    avT = work
    lin(win, 1024, C_IN["av"], 256, nX, T, t_n, plain(avT, "av", g2))
    head_splits(3)
    t_av = []
    for c, (k0, n) in enumerate(((0, NM), (NM, P), (NM + P, P))):
        bi, ps, free = PS.take()
        PE.wait(free, t_raw["av"])
        for j in range(2):
            t = PE(lambda e, ps=ps, j=j, k0=k0, n=n: e.transpose(ps[0:n, j * P:(j + 1) * P], avT[:, j, k0:k0 + n], ident))
        t2 = S(lambda e, ps=ps, c=c, n=n: e.copy(av[0:n, c, :], ps[0:n, 0:256]), t, g2)
        PS.give(bi, t2)
        t_av.append(t2)
    t_turned = t
    t_ak = ropes([(ak[:, j, :], cc("R128"), cc("cosA"), cc("sinA"), t_raw["ak"][j]) for j in range(2)], g2, rtmp)

    t_mb = []
    t_acc = []
    for qt in range(2):
        nk = NM + P * (qt + 1)
        acc = work[:, qt, :]
        t_a = None
        if nk < T:
            t_a = V(lambda e, acc=acc, nk=nk: e.memset(acc[:, nk:T], NEG), g2, t_turned)
        for h in range(8):
            p0 = 64 * (h % 2)
            bi, ps, free = PS.take()
            t = mm1(ps[:, 0:nk], iq[p0:p0 + 64, h // 2, qt * P:(qt + 1) * P], ik[p0:p0 + 64, 0:nk], t_iq[h // 2], t_ik, free)
            ri, r, rfree = rel.take()
            t = S(lambda e, ps=ps, r=r, nk=nk: e.activation(r[:, 0:nk], ps[:, 0:nk], ACT.Relu), t, rfree, g2)
            PS.give(bi, t)
            w1 = iw[:, 8 * qt + h:8 * qt + h + 1]
            if h == 0:
                t_a = V(lambda e, r=r, acc=acc, nk=nk, w1=w1: e.tensor_scalar(acc[:, 0:nk], r[:, 0:nk], w1, None, ALU.mult), t, t_a, t_iw, t_turned)
            else:
                t_a = V(lambda e, r=r, acc=acc, nk=nk, w1=w1: e.scalar_tensor_tensor(out=acc[:, 0:nk], in0=r[:, 0:nk], scalar=w1, in1=acc[:, 0:nk], op0=ALU.mult, op1=ALU.add), t, t_a)
            rel.give(ri, t_a)
        t_a = V(lambda e, acc=acc, nk=nk: e.tensor_tensor(acc[:, nk - P:nk], acc[:, nk - P:nk], cc("CB", P, 2 * P), ALU.add), t_a)
        t_acc.append(t_a)
    for it in range(8):
        for qt in range(2):
            w = work[:, qt, :]
            t = V(lambda e, w=w, qt=qt: e.max(m8[:, qt, :], w), t_acc[qt])
            t_acc[qt] = V(lambda e, w=w, qt=qt: e.match_replace(w, m8[:, qt, :], w, TAKEN), t)
    for qt in range(2):
        nk = NM + P * (qt + 1)
        t = V(lambda e, qt=qt: e.tensor_scalar(mb[:, qt, :], work[:, qt, :], -2e38, NEG, ALU.is_gt, ALU.mult), t_acc[qt])
        t_mb.append(V(lambda e, qt=qt, nk=nk: e.tensor_tensor(mb[:, qt, nk - P:nk], mb[:, qt, nk - P:nk], cc("CB", P, 2 * P), ALU.add), t))

    g2 = everyone()
    ev, raw_aq = roped(aq, float(128 ** -0.5))
    lin(win, 1024, C_IN["aq"], 1024, nX, SEQ, t_n, ev, x0=NM)
    t_aq = ropes([(d, cc("R128"), cc("cosA", NM), cc("sinA", NM), t) for d, t in raw_aq], g2, rtmp)

    def attention(units, segs, guard, filler=iter(())):
        m = top[0]
        ns = len(segs)
        mx = max(u["nk"](1) for u in units)
        Ls = Pool([carve(mx) for _ in range(3)])
        Pbs = Pool([carve(mx) for _ in range(4)])
        PTs = Pool([carve(ns, P) for _ in range(3)])
        sts = Pool([carve(4) for _ in range(4)])
        top[0] = m
        items = [(u, qt) for u in units for qt in range(2)]
        st = {}
        res = []

        def s1(i):
            u, qt = items[i]
            nk = u["nk"](qt)
            bi, ps, free = PS.take()
            t = mm1(ps[:, 0:nk], u["q"][:, qt * P:(qt + 1) * P], u["k"][:, 0:nk], u["t"], free)
            si, s, sfree = sts.take()
            pi, pb, pfree = Pbs.take()
            if u["bias"] is not None:
                li, L, lfree = Ls.take()
                t = V(lambda e, ps=ps: e.tensor_tensor(L[:, 0:nk], ps[:, 0:nk], u["bias"](qt), ALU.add), t, lfree, guard)
                PS.give(bi, t)
                src = L[:, 0:nk]
            else:
                src = ps[:, 0:nk]
            t = V(lambda e: e.tensor_reduce(s[:, 0:1], src, AX, ALU.max, negate=True), t, sfree, guard)
            t = S(lambda e: e.activation(pb[:, 0:nk], src, ACT.Exp, bias=s[:, 0:1], accum_out=s[:, 1:2]), t, pfree, guard)
            if u["bias"] is not None:
                Ls.give(li, t)
            else:
                PS.give(bi, t)
            st[i] = (pi, pb, t, si, s)

        def normalise(i):
            u, qt = items[i]
            nk = u["nk"](qt)
            pi, pb, t, si, s = st[i]
            t = V(lambda e: e.reciprocal(s[:, 2:3], s[:, 1:2]), t)
            t = V(lambda e: e.tensor_scalar(pb[:, 0:nk], pb[:, 0:nk], s[:, 2:3], None, ALU.mult), t)
            sts.give(si, t)
            st[i] = (pi, pb, t)

        def s2(i):
            u, qt = items[i]
            nk = u["nk"](qt)
            pi, pb, tp = st[i]
            use = [(j, a, n) for j, (a, n) in enumerate(segs) if a < nk]
            bi, ps, free = PS.take()
            PE.wait(tp, free)
            for j, a, n in use:
                t = PE(lambda e, ps=ps, j=j, a=a, n=n: e.transpose(ps[0:n, j * P:(j + 1) * P], pb[:, a:a + n], ident))
            Pbs.give(pi, t)
            ti, pt, tfree = PTs.take()
            ts = []
            full = [j for j, a, n in use if n == P]
            for j, a, n in use:
                if n < P:
                    ts.append(S(lambda e, ps=ps, j=j, n=n: e.copy(pt[0:n, j, :], ps[0:n, j * P:(j + 1) * P]), t, tfree, guard))
            j0, j1 = full[0], full[-1] + 1
            ts.append(S(lambda e, ps=ps: e.copy(pt[:, j0:j1, :].rearrange("p a b -> p (a b)"), ps[:, j0 * P:j1 * P]), t, tfree, guard))
            PS.give(bi, *ts)
            st[i] = (ti, pt, ts, use)

        obank = {}

        def s3(i):
            u, qt = items[i]
            ti, pt, ts, use = st.pop(i)
            hd, p0 = u["hd"], u["p0"]
            if qt == 0:
                obank["b"] = PS.take()
            bi, ps, free = obank["b"]
            PE.wait(free, ts)
            for x, (j, a, n) in enumerate(use):
                t = mm1(ps[p0:p0 + hd, qt * P:(qt + 1) * P], u["v"](j)[0:n, :], pt[0:n, j, :], start=(x == 0), stop=(x == len(use) - 1))
            PTs.give(ti, t)
            if qt == 1:
                src, (hi, lo) = ps[p0:p0 + hd, 0:SEQ], u["out"]
                obank["hi"] = (bi, src, hi, lo, S(lambda e: e.copy(hi, src), t, guard))

        def low_part():
            if "hi" in obank:
                bi, src, hi, lo, t = obank.pop("hi")
                res.append(V(lambda e: e.tensor_tensor(lo, src, hi.bitcast(F32), ALU.subtract), t, guard))
                PS.give(bi, res[-1])

        N = len(items)
        for i in range(N + 5):
            low_part()
            if i < N:
                s1(i)
            if 0 <= i - 1 < N:
                normalise(i - 1)
            if 0 <= i - 3 < N:
                s2(i - 3)
            if 0 <= i - 4 < N:
                s3(i - 4)
            next(filler, None)
        low_part()
        for _ in filler:
            pass
        return res

    units = [dict(q=aq[:, h, :], k=ak[:, h // 4, :], v=lambda j, h=h: av[:, j, (h // 4) * P:(h // 4 + 1) * P],
                  bias=lambda qt: mb[:, qt, 0:NM + P * (qt + 1)], nk=lambda qt: NM + P * (qt + 1),
                  hd=P, p0=0, out=(yd.hi[:, h, :], yd.lo[:, h, :]), t=[t_aq[h], t_ak[h // 4], t_mb, t_av]) for h in range(8)]
    top[0] = m_att + 3072
    t_gate, g_g = {}, everyone()
    gate_a = carve(8, SEQ)
    gate_b = shaped(arena[:, top_g:top_g + 2048], (8, SEQ))
    top[0] = m_att

    def held(dst, key):
        def evac(j, ps, t):
            t_gate[key] = V(lambda e: e.tensor_copy(dst[:, j, :], ps), t, g_g)
            return t_gate[key]
        return evac

    def gates():
        for key, dst in (("gate_a", gate_a), ("gate_b", gate_b)):
            for q in range(4):
                yield from lin_steps([(whole, source(win, 0, 8, C_IN[key] + 256 * q, 256))], 256, nX, NM, SEQ, t_n, held(dst, key), j0=2 * q)

    t_yd = attention(units, [(0, NM), (NM, P), (NM + P, P)], everyone(), gates())

    g3_ = everyone()
    t_gate = {key: S(lambda e, dst=dst: e.activation(dst, dst, ACT.Sigmoid), t_gate[key])
              for key, dst in (("gate_a", gate_a), ("gate_b", gate_b))}
    top[0] = m_free
    mg = carve_pair(8, SEQ)
    xin2 = carve(2, 1024)
    t_x2in = load_in(8, xin2, A["x"][0].rearrange("(a p) d -> p a d", p=P), g3_)
    t_mg, t_ta = [], {}

    def times_a(j, ps, t):
        t_ta[j] = V(lambda e: e.tensor_tensor(gate_a[:, j, :], gate_a[:, j, :], ps, ALU.mult), t, t_gate["gate_a"])
        return t_ta[j]

    def times_b(j, ps, t):
        b = gate_b[:, j, :]
        t1 = V(lambda e: e.tensor_tensor(b, b, ps, ALU.mult), t, t_gate["gate_b"])
        t2 = V(lambda e: e.tensor_tensor(b, b, gate_a[:, j, :], ALU.add), t1, t_ta[j])
        t_mg.append(split(b, mg.hi[:, j, :], mg.lo[:, j, :], t2, g3_))
        return t1

    lin(A["w_branch_gdn"][0], 1024, 0, 1024, yg, SEQ, t_y, times_a)
    lin(A["w_branch_dsa"][0], 1024, 0, 1024, yd, SEQ, t_yd, times_b)

    def keep(dst, ts, guard):
        def evac(j, ps, t):
            if j % 2:
                t = V(lambda e: e.tensor_copy(dst[:, j, :], ps), t, guard)
            else:
                t = S(lambda e: e.copy(dst[:, j, :], ps), t, guard)
            ts.append(t)
            return t
        return evac

    g_x = everyone()
    mix, t_mix = aq, []
    tl, rv = tally_at(m_yd + 2048, SEQ, g_x)

    def tallied(dst, ts, guard, tl):
        ev = keep(dst, ts, guard)

        def evac(j, ps, t):
            t = ev(j, ps, t)
            tl.square(dst[:, j, :], t)
            return t
        return evac

    hook[0] = tl.flush
    lin(A["w_out"][0], 1024, 0, 1024, mg, SEQ, t_mg, tallied(mix, t_mix, g_x, tl))
    hook[0] = None
    tl2, rv2 = tally_at(m_mt, SEQ, g_x)
    top[0] = 0
    x2 = carve(8, SEQ)

    def residual(k, tmp, t):
        bi, ps, free = PS.take()
        PE.wait(free, t_x2in)
        for a in range(2):
            t2 = PE(lambda e, a=a: e.transpose(ps[:, a * P:(a + 1) * P], xin2[:, a, k * P:(k + 1) * P], ident))
        t = V(lambda e: e.tensor_tensor(x2[:, k, :], tmp, ps[:, 0:SEQ], ALU.add), t, t2)
        PS.give(bi, t)
        tl2.square(x2[:, k, :], t)
        if k:
            tl2.flush()
        return t

    rms_scaled(mix, SEQ, "post_mix_norm", 0, m_yd, tl, rv, g_x, residual)
    t_n2 = rms_scaled(x2, SEQ, "pre_mlp_norm", 0, m_yd, tl2, rv2, None, into(X))
    g4 = everyone()
    top[0] = 2048
    u_ = carve_pair(32, SEQ)
    dn, t_dn = carve(8, SEQ), []
    ut = Pool([carve(2, SEQ) for _ in range(3)])
    t_u = []

    def evac_u(j, ps, t):
        ui, ub, ufree = ut.take()
        t1 = S(lambda e: e.activation(ub[:, 0, :], ps, ACT.Relu), t, g4, ufree)
        t2 = G(lambda e: e.tensor_tensor(ub[:, 1, :], ub[:, 0, :], ub[:, 0, :], ALU.mult), t1)
        t2 = split(ub[:, 1, :], u_.hi[:, j, :], u_.lo[:, j, :], t2, g4)
        ut.give(ui, t2)
        t_u.append(t2)
        return t1

    lin(A["w_up"][0], 1024, 0, 4096, X, SEQ, t_n2, evac_u)
    tl, rv = tally_at(top[0], SEQ, g4)
    hook[0] = tl.flush
    lin(A["w_down"][0], 4096, 0, 1024, u_, SEQ, t_u, tallied(dn, t_dn, g4, tl))
    hook[0] = None

    g5 = everyone()

    def residual2(k, tmp, t):
        t = G(lambda e: e.tensor_tensor(x2[:, k, :], x2[:, k, :], tmp, ALU.add), t)
        return [t, into(X)(k, x2[:, k, :], t)]

    t_x3 = rms_scaled(dn, SEQ, "post_mlp_norm", 0, 2048, tl, rv, everyone(), residual2)

    top[0] = 2048
    xm = carve(8, SEQ)
    m_moe = top[0]
    kms = [carve(2, SEQ) for _ in range(2)]
    vms = [carve(2, 256) for _ in range(2)]
    cos2, sin2 = carve(SEQ), carve(SEQ)
    m_ffn = top[0]
    mix2 = carve_pair(8, SEQ)
    kx = carve(6, SEQ)
    vx = carve(2, 768)
    m_b2 = top[0]
    m_ln = 20000
    memT = carve_pair(8, SEQ)
    memin = shaped(arena[:, m_ffn + 4096:m_ffn + 6144], (2, 1024))
    t_mem = load_in(6, memin, A["mem_2"][0].rearrange("(a p) d -> p a d", p=P), g5)
    t_memT = []
    for k in range(8):
        bi, ps, free = PS.take()
        PE.wait(t_mem, free)
        for a in range(2):
            t = PE(lambda e, ps=ps, a=a, k=k: e.transpose(ps[:, a * P:(a + 1) * P], memin[:, a, k * P:(k + 1) * P], ident))
        t = split(ps[:, 0:SEQ], memT.hi[:, k, :], memT.lo[:, k, :], t, g5)
        PS.give(bi, t)
        t_memT.append(t)
    ang, kf = carve(SEQ), carve(SEQ)
    ki = posi
    two_pi = 2 * np.pi
    t = V(lambda e: e.tensor_copy(ang, posi[:, :]), t_pos, g5)
    t = V(lambda e: e.tensor_scalar(ang, ang, cc("inv2"), None, ALU.mult), t)
    for big in (4096.0, 1.0):
        rest = two_pi * big
        parts = []
        for bits in (8, 8):
            sc = 2.0 ** (bits - 1 - np.floor(np.log2(rest)))
            p_ = float(np.floor(rest * sc) / sc)
            parts.append(p_)
            rest -= p_
        parts += [float(np.float32(rest))]
        t = V(lambda e, big=big: e.tensor_scalar(kf, ang, float(1.0 / (two_pi * big)), None, ALU.mult), t)
        t = V(lambda e: e.tensor_copy(ki[:, :], kf), t)
        t = V(lambda e: e.tensor_copy(kf, ki[:, :]), t)
        for p_ in parts:
            t = V(lambda e, p_=p_: e.scalar_tensor_tensor(out=ang, in0=kf, scalar=-p_, in1=ang, op0=ALU.mult, op1=ALU.add), t)
    for cmp_, sgn in ((ALU.is_gt, -two_pi), (ALU.is_lt, two_pi)):
        lim = float(np.pi) if sgn < 0 else -float(np.pi)
        t = V(lambda e, cmp_=cmp_, lim=lim, sgn=sgn: e.tensor_scalar(kf, ang, lim, float(sgn), cmp_, ALU.mult), t)
        t = V(lambda e: e.tensor_tensor(ang, ang, kf, ALU.add), t)
    t = V(lambda e: e.tensor_scalar(ang, ang, 3.1415925, -3.1415925, ALU.min, ALU.max), t)
    t_s2 = S(lambda e: e.activation(sin2, ang, ACT.Sin), t)
    t = S(lambda e: e.activation(kf, ang, ACT.Sin, scale=0.5), t)
    t = V(lambda e: e.tensor_tensor(kf, kf, kf, ALU.mult), t)
    t_rot = [t_s2, V(lambda e: e.tensor_scalar(cos2, kf, -2.0, 1.0, ALU.mult, ALU.add), t)]
    alpha = float(4 ** 0.25)
    xcur, t_xc = x2, t_x3

    def mem_kv(layer):
        w = A["w_mem_kv_2"][layer]
        km, vm = kms[layer], vms[layer]
        ts = []
        lin(w, 1024, 0, 256, memT, SEQ, t_memT, keep(km, ts, g5))
        slots, wp, tw = stream([(whole, source(w, 0, 8, 256, 256))], (8, 256))
        for c in range(2):
            bi, ps, t = tok_block(wp, tw, 256, memT, c * P, P, t_memT, c == 1)
            t2 = V(lambda e, ps=ps, c=c: e.tensor_copy(vm[:, c, :], ps), t, g5)
            PS.give(bi, t2)
            ts.append(t2)
        release(slots, t)
        return ts

    t_mkvs = [mem_kv(layer) for layer in range(2)]
    top[0] = m_b2

    def layer_norm(src, gname, bname, li, dst, tl, mu, guard, pair):
        t = tl.mean(mu)
        tl, r = tally_at(m_ln, SEQ, guard)
        for k in range(8):
            tc_ = V(lambda e, k=k: e.tensor_tensor(src[:, k, :], src[:, k, :], mu, ALU.subtract), t)
            tl.square(src[:, k, :], tc_)
            tl.flush()
        t = tl.inv_root(eps5, r)
        res = []
        for k in range(8):
            t1 = V(lambda e, k=k: e.scalar_tensor_tensor(out=src[:, k, :], in0=src[:, k, :], scalar=vcol(gname, 8 * li + k), in1=r, op0=ALU.mult, op1=ALU.mult), t)
            t1 = S(lambda e, k=k: e.activation(dst[:, k, :], src[:, k, :], ACT.Identity, bias=vcol(bname, 8 * li + k)), t1, guard)
            res.append([t1, into(pair)(k, dst[:, k, :], t1)] if pair is not None else t1)
        return res

    def sums(guard):
        return Tally(SEQ, [], guard), shaped(arena[:, m_ln + 5 * SEQ:m_ln + 6 * SEQ], (SEQ,))

    def add_alpha(base, dst, tl, guard):
        def evac(j, ps, t):
            t = V(lambda e, ps=ps: e.scalar_tensor_tensor(out=dst[:, j, :], in0=base[:, j, :], scalar=alpha, in1=ps, op0=ALU.mult, op1=ALU.add), t, guard)
            tl.add(dst[:, j, :], t)
            return t
        return evac

    def memory_units(t_q, layer):
        km, vm = kms[layer], vms[layer]
        return [dict(q=qm[64 * (h % 2):64 * (h % 2) + 64, h // 2, :], k=km[64 * (h % 2):64 * (h % 2) + 64, h // 2, :],
                     v=lambda j, h=h: vm[:, j, 64 * h:64 * h + 64], bias=None, nk=lambda qt: SEQ, hd=64, p0=64 * (h % 2),
                     out=[x[64 * (h % 2):64 * (h % 2) + 64, 6 + h // 2, :] for x in (mix2.hi, mix2.lo)], t=t_q) for h in range(4)]

    segs2 = [(0, P), (P, P)]

    def scaled(dst, ts, guard, j0=0):
        def evac(j, ps, t):
            t = S(lambda e, ps=ps: e.activation(dst[:, j - j0, :], ps, ACT.Copy, scale=0.125), t, guard)
            ts.append(t)
            return t
        return evac

    for layer in range(2):
        g_l = everyone()
        t_mkv = t_mkvs[layer]
        top[0] = m_b2
        qm = carve(2, SEQ)
        if layer == 0:
            wa = A["w_in_a_2"][0]
            uc = carve(6, SEQ)
            zp = carve(6, SEQ + 2)
            t_zp = G(lambda e: e.memset(zp[:, :, 0:2], 0.0), g_l)
            tc_, tz_, tm_ = [], [], []
            lin(wa, 1024, 768, 768, X, SEQ, t_xc, keep(uc, tc_, g_l))

            def evac_h(j, ps, t):
                t = V(lambda e, ps=ps: e.tensor_tensor(zp[:, j, 2:2 + SEQ], ps, uc[:, j, :], ALU.mult), t, tc_[j], g_l)
                tz = V(lambda e: e.tensor_scalar(uc[:, j, :], zp[:, j, 0:SEQ], vcol("conv_a_2", j), None, ALU.mult), t, t_zp)
                for u in (1, 2):
                    tz = V(lambda e, u=u: e.scalar_tensor_tensor(out=uc[:, j, :], in0=zp[:, j, u:u + SEQ], scalar=vcol("conv_a_2", 6 * u + j), in1=uc[:, j, :], op0=ALU.mult, op1=ALU.add), tz)
                tz_.append(tz)
                return t

            lin(wa, 1024, 1536, 768, X, SEQ, t_xc, evac_h)

            def evac_bb(j, ps, t):
                t = V(lambda e, ps=ps: e.tensor_tensor(uc[:, j, :], ps, uc[:, j, :], ALU.mult), t, tz_[j], g_l)
                tm_.append(split(uc[:, j, :], mix2.hi[:, j, :], mix2.lo[:, j, :], t))
                return t

            t_qm = []
            lin(wa, 1024, 2304, 256, X, SEQ, t_xc, scaled(qm, t_qm, g_l))
            lin(wa, 1024, 0, 768, X, SEQ, t_xc, evac_bb)
            ta = attention(memory_units(t_qm + t_mkv, layer), segs2, g_l)
            t_mix2 = tm_ + [ta[0:2], ta[2:4]]
        else:
            raw = []
            t_qm = []
            qx = carve(6, SEQ)
            rtmp2 = Pool([carve(SEQ) for _ in range(3)])
            wq = A["w_q_b_2"][0]
            lin(wq, 1024, 0, 768, X, SEQ, t_xc, scaled(qx, raw, g_l))
            lin(wq, 1024, 768, 256, X, SEQ, t_xc, scaled(qm, t_qm, g_l))
            t_qx = ropes([(qx[:, j, :], cc("R16"), cos2, sin2, [raw[j], t_rot]) for j in range(6)], g_l, rtmp2)
            units = [dict(q=qx[64 * (h % 2):64 * (h % 2) + 64, h // 2, :], k=kx[64 * (h % 2):64 * (h % 2) + 64, h // 2, :],
                          v=lambda j, h=h: vx[:, j, 64 * h:64 * h + 64], bias=lambda qt: cc("CB", P, 2 * P) if qt == 0 else cc("CB"),
                          nk=lambda qt: P * (qt + 1), hd=64, p0=64 * (h % 2),
                          out=[x[64 * (h % 2):64 * (h % 2) + 64, h // 2, :] for x in (mix2.hi, mix2.lo)], t=[t_qx[h // 2], t_kx, t_vx]) for h in range(12)]
            ta = attention(memory_units(t_qm + t_mkv, layer) + units, segs2, g_l)
            t_mix2 = [ta[4 + 2 * k:6 + 2 * k] for k in range(6)] + [ta[0:2], ta[2:4]]
        g_n = everyone()
        tl, mu = sums(g_n)
        hook[0] = tl.flush
        lin(A["w_o_2"][layer], 1024, 0, 1024, mix2, SEQ, t_mix2, add_alpha(xcur, xm, tl, g_l))
        hook[0] = None
        top[0] = m_b2
        t_xc = layer_norm(xm, "ln1_g_2", "ln1_b_2", layer, xcur, tl, mu, g_n, X)
        g_f = everyone()
        if layer == 0:
            top[0] = m_ffn
            gg = carve_pair(22, SEQ)
            gt_ = Pool([carve(SEQ) for _ in range(4)])
            t_gg = [None] * 22
            held = {}

            def evac_g(j, ps, t):
                ti, tb, tfree = gt_.take()
                t = S(lambda e: e.activation(tb, ps, ACT.Silu), t, g_f, tfree)
                held[j] = (ti, tb, t)
                return t

            def evac_u2(j, ps, t):
                ti, tb, tg = held.pop(j)
                t1 = V(lambda e: e.tensor_tensor(tb, tb, ps, ALU.mult), t, tg)
                t_gg[j] = split(tb, gg.hi[:, j, :], gg.lo[:, j, :], t1)
                gt_.give(ti, t_gg[j])
                return t1

            wgu = A["w_gu_dense_2"][0]
            for f0 in range(0, 2816, 256):
                lin(wgu, 1024, f0, 256, X, SEQ, t_xc, evac_g, j0=f0 // P)
                lin(wgu, 1024, 2816 + f0, 256, X, SEQ, t_xc, evac_u2, j0=f0 // P)
            tl, mu = sums(g_f)
            hook[0] = tl.flush
            lin(A["w_down_dense_2"][0], 2816, 0, 1024, gg, SEQ, t_gg, add_alpha(xcur, xm, tl, g_f))
            hook[0] = None
            t_xc = layer_norm(xm, "ln2_g_2", "ln2_b_2", layer, xcur, tl, mu, g_f, X)
            g_k = everyone()
            raw, t_vx = [], []
            top[0] = m_b2
            rtmp2 = Pool([carve(SEQ) for _ in range(3)])
            wkv = A["w_kv_shared_2"]
            lin(wkv, 1024, 0, 768, X, SEQ, t_xc, keep(kx, raw, g_k))
            for c0 in range(0, 768, 256):
                slots, wp, tw = stream([(whole, source(wkv, 0, 8, 768 + c0, 256))], (8, 256))
                for c in range(2):
                    bi, ps, t = tok_block(wp, tw, 256, X, c * P, P, t_xc, c == 1)
                    t2 = V(lambda e, ps=ps, c=c, c0=c0: e.tensor_copy(vx[:, c, c0:c0 + 256], ps), t, g_k)
                    PS.give(bi, t2)
                    t_vx.append(t2)
                release(slots, t)
            t_kx = ropes([(kx[:, j, :], cc("R16"), cos2, sin2, [raw[j], t_rot]) for j in range(6)], g_k, rtmp2)

    g_m = everyone()
    top[0] = m_moe
    acc = xm
    xt = carve_pair(2, 1024)
    lg, m8b, gt2, oh = carve(2, 8), carve(2, 8), carve(2, 8), carve(2, 2, 8)
    ix = sb("ix", [P, 2, 8], U32)
    flag = sb("flag", [P, 1], I32)
    ixf, sel, ge, posm, cnt = carve(2, 8), carve(2, 8), carve(2, 8), carve(2, 8), carve(8)
    t_sel, t_ge, t_m8, t_oh = [], [], [], []
    lgT = carve(SEQ)
    bi, ps, free = PS.take()
    PE.wait(t_wr, free)
    for k in range(8):
        wait_for(t_xc, k, 8)
        t = mm1(ps[0:8, 0:SEQ], wr[:, k, :], xcur[:, k, :], start=(k == 0), stop=(k == 7))
    t = S(lambda e, ps=ps: e.copy(lgT[0:8, :], ps[0:8, 0:SEQ]), t, g_m)
    PS.give(bi, t)
    bi, ps, free = PS.take()
    PE.wait(t, free)
    for c in range(2):
        t = PE(lambda e, ps=ps, c=c: e.transpose(ps[:, 8 * c:8 * c + 8], lgT[0:8, c * P:(c + 1) * P], cc("ident")[0:8, 0:8]))
    t = V(lambda e, ps=ps: e.tensor_copy(lg.rearrange("p a b -> p (a b)"), ps[:, 0:16]), t, g_m)
    PS.give(bi, t)
    t_m8 = [V(lambda e, c=c: e.max(m8b[:, c, :], lg[:, c, :]), t) for c in range(2)]
    t2 = [V(lambda e, c=c: e.max_index(ix[:, c, :], m8b[:, c, :], lg[:, c, :]), t_m8[c]) for c in range(2)]
    t2 = [V(lambda e, c=c: e.tensor_copy(ixf[:, c, :], ix[:, c, :]), t2[c]) for c in range(2)]
    for c in range(2):
        t_oh += [V(lambda e, c=c, r=r: e.tensor_scalar(oh[:, c, r, :], cc("iota8"), ixf[:, c, r:r + 1], None, ALU.is_equal), t2[c]) for r in range(2)]
    t_sel = [V(lambda e, c=c: e.tensor_tensor(sel[:, c, :], oh[:, c, 0, :], oh[:, c, 1, :], ALU.add), t_oh) for c in range(2)]
    t_xt = []
    for c in range(2):
        for hf in range(2):
            bi, ps, free = PS.take()
            PE.wait(free, t_xc)
            for k in range(4):
                t = PE(lambda e, ps=ps, k=k, hf=hf, c=c: e.transpose(ps[:, k * P:(k + 1) * P], xcur[:, 4 * hf + k, c * P:(c + 1) * P], ident))
            t = split(ps, *[x[:, c, 512 * hf:512 * hf + 512] for x in (xt.hi, xt.lo)], t, g_m)
            PS.give(bi, t)
            t_xt.append(t)
    t_pos = []
    for c in range(2):
        bi, ps, free = PS.take()
        t = mm1(ps[:, 0:8], cc("U"), sel[:, c, :], t_sel, free, stop=(c == 0))
        if c == 1:
            t = mm1(ps[:, 0:8], ones, sel[:, 0, :], start=False)
        t = V(lambda e, ps=ps, c=c: e.tensor_tensor(posm[:, c, :], ps[:, 0:8], sel[:, c, :], ALU.mult), t)
        PS.give(bi, t)
        t_pos.append(V(lambda e, c=c: e.tensor_scalar(posm[:, c, :], posm[:, c, :], -1.0, None, ALU.add), t))
    for c in range(2):
        g_ = gt2[:, c, :]
        t = V(lambda e, c=c, g_=g_: e.tensor_tensor(g_[:, 2:3], m8b[:, c, 1:2], m8b[:, c, 0:1], ALU.subtract), t_m8)
        t = S(lambda e, g_=g_: e.activation(g_[:, 3:4], g_[:, 2:3], ACT.Exp), t)
        t = V(lambda e, g_=g_: e.tensor_scalar(g_[:, 4:5], g_[:, 3:4], 1.0, None, ALU.add), t)
        t = V(lambda e, g_=g_: e.reciprocal(g_[:, 0:1], g_[:, 4:5]), t)
        t = V(lambda e, g_=g_: e.tensor_tensor(g_[:, 1:2], g_[:, 3:4], g_[:, 0:1], ALU.mult), t)
        t = V(lambda e, c=c, g_=g_: e.tensor_scalar(ge[:, c, :], oh[:, c, 0, :], g_[:, 0:1], None, ALU.mult), t)
        t_ge.append(V(lambda e, c=c, g_=g_: e.scalar_tensor_tensor(out=ge[:, c, :], in0=oh[:, c, 1, :], scalar=g_[:, 1:2], in1=ge[:, c, :], op0=ALU.mult, op1=ALU.add), t))
    bi, ps, free = PS.take()
    mm1(ps[:, 0:8], ones, sel[:, 0, :], free, stop=False)
    t = mm1(ps[:, 0:8], ones, sel[:, 1, :], start=False)
    t = V(lambda e, ps=ps: e.tensor_reduce(cnt[:, 0:1], ps[:, 0:8], AX, ALU.max), t)
    PS.give(bi, t)
    t = V(lambda e: e.tensor_scalar(cnt[:, 1:2], cnt[:, 0:1], float(P), None, ALU.is_gt), t)
    t_flag = V(lambda e: e.tensor_copy(flag[:, :], cnt[:, 1:2]), t)

    pm = carve(2, 2 * P, of=arena_r)
    GP = Pool([carve(2, P) for _ in range(2)])
    GPT = Pool([carve(SEQ) for _ in range(4)])
    xs2 = carve_pair(8, 2 * P)
    hh = carve(2816)
    hp = carve_pair(22, P)
    t_acc = [V(lambda e, j=j: e.tensor_scalar(acc[:, 2 * j:2 * j + 2, :], xcur[:, 2 * j:2 * j + 2, :], alpha, None, ALU.mult), g_m, t_xc) for j in range(4)]

    g_y = everyone()
    YE = Pool([shaped(arena[:, 1024 * j:1024 * (j + 1)], (1024,)) for j in range(2)])

    def pick(q, base):
        t_free = PE.last()
        out_ = []
        for y in range(2):
            for c in range(2):
                t1 = V(lambda e, c=c, y=y: e.tensor_scalar(pm[:, c, P * y:P * y + P], cc("iota", base, base + P), posm[:, c, q + y:q + y + 1], None, ALU.is_equal), t_pos, t_free, g_m)
        for y in range(2):
            gi, gp, gfree = GP.take()
            for c in range(2):
                t2 = V(lambda e, c=c, y=y, gp=gp: e.tensor_scalar(gp[:, c, :], cc("iota", base, base + P), posm[:, c, q + y:q + y + 1], ge[:, c, q + y:q + y + 1], ALU.is_equal, ALU.mult), t_pos, t_ge, gfree, g_m)
            out_.append([gi, gp, t2])
        ts = []
        for k in range(8):
            bi, ps, free = PS.take()
            PE.wait(free, t1, t_xt)
            for part, x in enumerate((xt.hi, xt.lo)):
                for c in range(2):
                    t = PE(lambda e, ps=ps, part=part, x=x, c=c, k=k: e.matmul(ps[:, 2 * P * part:2 * P * (part + 1)], x[:, c, k * P:(k + 1) * P], pm[:, c, :], start=(c == 0), stop=(c == 1)))
            t3 = S(lambda e, ps=ps, k=k: e.copy(xs2.hi[:, k, :], ps[:, 0:2 * P]), t, t_free, g_m)
            t4 = V(lambda e, ps=ps, k=k: e.tensor_copy(xs2.lo[:, k, :], ps[:, 2 * P:4 * P]), t3, t_free, g_m)
            PS.give(bi, t4)
            ts.append(t4)
        res = []
        for y in range(2):
            gi, gp, t2 = out_[y]
            ti, gt, tfree = GPT.take()
            bi, ps, free = PS.take()
            PE.wait(free, t2)
            for c in range(2):
                t = PE(lambda e, ps=ps, c=c, gp=gp: e.transpose(ps[:, c * P:(c + 1) * P], gp[:, c, :], ident))
            GP.give(gi, t)
            tg = S(lambda e, ps=ps, gt=gt: e.copy(gt, ps[:, 0:SEQ]), t, tfree, g_m)
            PS.give(bi, tg)
            xs = Pair(xs2.hi[:, :, P * y:P * y + P], xs2.lo[:, :, P * y:P * y + P])
            res.append((xs, ts, ti, gt, tg))
        return res

    def expert_up(q, picked):
        xs, ts, ti, gt, tg = picked
        w = A["w_gu_moe_2"][0, q]
        guard = [PE.last()]
        t_h, t_hp = {}, []

        def turn(f):
            n = min(4, 22 - f)
            bi, ps, free = PS.take()
            PE.wait(free, [t_h[x // 2] for x in range(f, f + n)])
            for x in range(n):
                t = PE(lambda e, x=x: e.transpose(ps[:, x * P:(x + 1) * P], hh[:, (f + x) * P:(f + x + 1) * P], ident))
            t2 = split(ps[:, 0:n * P], *[x[:, f:f + n, :].rearrange("p a b -> p (a b)") for x in (hp.hi, hp.lo)], t, guard, g_m)
            PS.give(bi, t2)
            t_hp.append((t, t2))

        for j in range(11):
            for side in range(2):
                slots, wp, tw = stream([(whole, source(w, 0, 8, 2816 * side + 256 * j, 256))], (8, 256))
                bi, ps, t = tok_block(wp, tw, 256, xs, 0, P, ts, True)
                release(slots, t)
                hv = hh[:, 256 * j:256 * j + 256]
                if side == 0:
                    t_h[j] = S(lambda e, ps=ps, hv=hv: e.activation(hv, ps, ACT.Silu), t, guard, g_m)
                else:
                    t_h[j] = V(lambda e, ps=ps, hv=hv: e.tensor_tensor(hv, hv, ps, ALU.mult), t, t_h[j])
                PS.give(bi, t_h[j])
            if j >= 2 and j % 2 == 0:
                turn(2 * j - 4)
        return t_hp, turn

    def expert_down(q, up):
        t_hp, turn = up
        w = A["w_down_moe_2"][0, q]
        b = [PS.take() for _ in range(2)]
        for f0 in range(0, 22, 2):
            if f0 == 2:
                turn(20)
            slots, wp, tw = stream([(whole, w[f0 * P:(f0 + 2) * P, :].rearrange("(k p) n -> p k n", p=P))], (2, 1024))
            for hf in range(2):
                bi, ps, free = b[hf]
                PE.wait(tw, free, t_hp[f0 // 4][1])
                for k in range(2):
                    f = f0 + k
                    t = mm3(ps, (hp.hi[:, f, :], hp.lo[:, f, :]), [x[:, k, 512 * hf:512 * hf + 512] for x in (wp.hi, wp.lo)], f == 0, f == 21)
            if f0 < 20:
                t = PE.tick()
            release(slots, t)
        yi, ye, yfree = YE.take()
        ts = []
        for hf in range(2):
            bi, ps, free = b[hf]
            if hf:
                ts.append(V(lambda e, ps=ps: e.tensor_copy(ye[:, 512:1024], ps), t, yfree, g_y))
            else:
                ts.append(S(lambda e, ps=ps: e.copy(ye[:, 0:512], ps), t, yfree, g_y))
            PS.give(bi, ts[-1])
        return yi, ye, ts

    def spread(q,  picked, made):
        _, _, ti, gt, tg = picked
        yi, ye, ts = made
        for h2 in range(4):
            bi, ps, free = PS.take()
            PE.wait(free, ts, tg)
            for k in range(2):
                kk = 2 * h2 + k
                t = mm1(ps[:, k * SEQ:(k + 1) * SEQ], ye[:, kk * P:(kk + 1) * P], gt)
            av_ = acc[:, 2 * h2:2 * h2 + 2, :].rearrange("p a b -> p (a b)")
            t_acc[h2] = V(lambda e, ps=ps, av_=av_: e.tensor_tensor(av_, av_, ps, ALU.add), t, t_acc[h2])
            PS.give(bi, t_acc[h2])
        YE.give(yi, t)
        GPT.give(ti, t)

    def all_experts(base):
        two = pick(0, base)
        prev = None
        for q in range(8):
            cur_ = two[q % 2]
            up = expert_up(q, cur_)
            if prev is not None:
                spread(q - 1, *prev)
            if q % 2 and q < 7:
                two = pick(q + 1, base)
            made = expert_down(q, up)
            prev = (cur_, made)
        spread(7, *prev)

    all_experts(0)

    main_slots = (list(s_slot), list(n_slot))
    queues = (PE, V, S, G, SP)
    before = everyone()
    for q_, s_ in zip(queues, (sem("x_pe"), sem("x_dve"), sem("x_act"), sem("x_pool"), None)):
        q_.enter(s_)
        q_.wait(before)
    s_slot[:] = [sem(f"x_slot{i}") for i in range(NRAW)]
    n_slot[:] = [0] * NRAW
    pools = (PS, RAW, HI, GP, GPT, YE)
    for p_ in pools:
        p_.free, p_.out = [[] for _ in p_.bufs], set()
    t_acc_main = list(t_acc)
    new_segment()
    all_experts(P)
    done = everyone()
    for q_ in queues:
        q_.wait(done)
    for q_ in queues:
        q_.leave(flag[0:1, 0:1], t_flag, before)
    s_slot[:], n_slot[:] = main_slots
    for p_ in pools:
        p_.free, p_.out = [[] for _ in p_.bufs], set()
    t_acc = [t_acc_main[j // 2] for j in range(8)]
    top[0] = m_b2
    g_n = everyone()
    tl, mu = sums(g_n)
    for j in range(8):
        tl.add(xm[:, j, :], t_acc[j])
    t_xc = layer_norm(xm, "ln2_g_2", "ln2_b_2", 1, xcur, tl, mu, g_n, None)

    g_o = everyone()
    fin = carve(2, 1024)
    for c in range(2):
        tf = []
        for hf in range(2):
            bi, ps, free = PS.take()
            PE.wait(free, t_xc)
            for k in range(4):
                t = PE(lambda e, ps=ps, k=k, hf=hf, c=c: e.transpose(ps[:, k * P:(k + 1) * P], xcur[:, 4 * hf + k, c * P:(c + 1) * P], ident))
            if hf:
                t = V(lambda e, ps=ps, c=c: e.tensor_copy(fin[:, c, 512:1024], ps), t, g_o)
            else:
                t = S(lambda e, ps=ps, c=c: e.copy(fin[:, c, 0:512], ps), t, g_o)
            PS.give(bi, t)
            tf.append(t)
        SP.quiet(lambda e, c=c: e.dma_start(out[0, c * P:(c + 1) * P, :], fin[:, c, :]).then_inc(s_out, 16), tf)
    SP.quiet(lambda e: e.wait_ge(s_out, 32))

    return (PE, V, S, G, SP), W["rec"]


INS = ["x", "meta_tokens", "pre_mix_norm", "w_in", "conv_w", "a_log", "dt_bias", "gdn_norm", "w_branch_gdn",
       "w_branch_dsa", "w_out", "post_mix_norm", "pre_mlp_norm", "w_up", "w_down", "post_mlp_norm", "mem_2",
       "positions_2", "w_in_a_2", "conv_a_2", "w_q_b_2", "w_kv_shared_2", "w_mem_kv_2", "w_o_2", "ln1_g_2",
       "ln1_b_2", "ln2_g_2", "ln2_b_2", "w_gu_dense_2", "w_down_dense_2", "w_router_2", "w_gu_moe_2",
       "w_down_moe_2"]


def kernel(**inputs):
    from concourse import bacc
    from concourse.bass_utils import run_bass_kernel_spmd

    nc = bacc.Bacc("TRN2", target_bir_lowering=False, num_devices=1)
    arrays, aps = {}, {}
    for name in INS:
        a = np.ascontiguousarray(inputs[name])
        arrays[f"in_{name}"] = a
        aps[name] = nc.dram_tensor(f"in_{name}", a.shape, mybir.dt.from_np(a.dtype), kind="ExternalInput").ap()
    table = np.ascontiguousarray(np.concatenate(list(shape_constants().values()), axis=1))
    arrays["in_table"] = table
    cst = nc.dram_tensor("in_table", table.shape, F32, kind="ExternalInput").ap()
    out = nc.dram_tensor("out_0", (1, SEQ, 1024), F32, kind="ExternalOutput").ap()
    program(nc, aps, cst, out)
    r = run_bass_kernel_spmd(nc, [arrays], core_ids=[0])
    return r.results[0]["out_0"]
```
